# Optimizing a Trainium2 kernel written in Bass

```python
import math
import jax, jax.numpy as jnp
from jax import lax
import numpy as np

D_MODEL = 1024
BATCH = 1
SEQ = 512
DEPTH = 1
DEC_BATCH = 1
DEC_SEQ = 64
PAST_LEN = 128

CHUNK = 64
D_CONV = 1024
CONV_A_WIDTH = 3
N_HEADS = 8
HEAD_K = 128
HEAD_V = 128
QK_DIM = N_HEADS * HEAD_K
V_DIM = N_HEADS * HEAD_V
QKV_DIM = 2 * QK_DIM + V_DIM
CONV_QKV_WIDTH = 4
IN_DIM = 3 * D_CONV + QKV_DIM + V_DIM + 2 * N_HEADS + 2 * D_MODEL
N_GROUPS = 4
EXPERTS_PER_GROUP = 8
N_EXPERTS = N_GROUPS * EXPERTS_PER_GROUP
TOP_K = 2
D_EXPERT = 256
EPS = 1e-6

kernel_name = "hybrid_conv_gdn_hmoe_stream_step"

def rmsnorm(x, g):
    xf = x.astype(jnp.float32)
    r = lax.rsqrt(jnp.mean(xf * xf, axis=-1, keepdims=True) + EPS)
    return (xf * r * g.astype(jnp.float32)).astype(x.dtype)

def causal_conv(x, prev, w):
    width = w.shape[0]
    L = x.shape[1]
    xp = jnp.concatenate([prev.astype(x.dtype), x], axis=1)
    y = sum(xp[:, j:j + L] * w[j] for j in range(width))
    return y, xp[:, -(width - 1):]

def l2norm(x):
    return x * lax.rsqrt(jnp.sum(x * x, axis=-1, keepdims=True) + EPS)

def gated_delta_chunked(q, k, v, g, beta, S0, chunk):
    B, L, H, DK = q.shape
    DV = v.shape[-1]
    n = L // chunk

    def split(t):
        t = t.reshape((B, n, chunk) + t.shape[2:])
        return jnp.moveaxis(t, 3, 1)

    q, k, v, g, beta = (split(t) for t in (q, k, v, g, beta))
    G = jnp.cumsum(g, axis=-1)
    idx = jnp.arange(chunk)
    incl = idx[:, None] >= idx[None, :]
    strict = idx[:, None] > idx[None, :]
    decay = jnp.exp(jnp.where(incl, G[..., :, None] - G[..., None, :], -jnp.inf))
    kk = jnp.einsum('bhnid,bhnjd->bhnij', k, k)
    A = jnp.where(strict, beta[..., :, None] * kk * decay, 0.0)
    eye = jnp.eye(chunk, dtype=q.dtype)
    T = lax.linalg.triangular_solve(eye + A, jnp.broadcast_to(eye, A.shape),
                                    left_side=True, lower=True, unit_diagonal=True)
    u = jnp.einsum('bhnij,bhnjd->bhnid', T, beta[..., None] * v)
    w = jnp.einsum('bhnij,bhnjd->bhnid', T, (beta * jnp.exp(G))[..., None] * k)
    attn = jnp.einsum('bhnid,bhnjd->bhnij', q, k) * decay
    qg = q * jnp.exp(G)[..., None]
    G_last = G[..., -1]
    kd = k * jnp.exp(G_last[..., None] - G)[..., None]

    def step(S, xs):
        qg_c, w_c, u_c, attn_c, kd_c, gl_c = xs
        v_new = u_c - jnp.einsum('bhcd,bhde->bhce', w_c, S)
        o = jnp.einsum('bhcd,bhde->bhce', qg_c, S) + jnp.einsum('bhij,bhje->bhie', attn_c, v_new)
        S = S * jnp.exp(gl_c)[..., None, None] + jnp.einsum('bhcd,bhce->bhde', kd_c, v_new)
        return S, o

    xs = tuple(jnp.moveaxis(t, 2, 0) for t in (qg, w, u, attn, kd, G_last))
    S_fin, o = lax.scan(step, S0, xs)
    o = jnp.transpose(o, (1, 0, 3, 2, 4)).reshape(B, L, H, DV)
    return o, S_fin

def token_mixers(xn, prev_a, prev_qkv, S0, w_in, conv_a_w, w_out_a, conv_qkv_w,
                 a_log, dt_bias, onorm_g, w_out_b, w_o, chunk):
    Bsz, L, _ = xn.shape
    proj = xn @ w_in
    sizes = [D_CONV, D_CONV, D_CONV, QKV_DIM, V_DIM, N_HEADS, N_HEADS, D_MODEL, D_MODEL]
    offs = []
    acc = 0
    for s in sizes[:-1]:
        acc += s
        offs.append(acc)
    h, b_gate, c_gate, qkv, z, beta_raw, a_raw, gate_a, gate_b = jnp.split(proj, offs, axis=-1)

    conv_u, new_a = causal_conv(c_gate * h, prev_a, conv_a_w)
    y_a = (b_gate * conv_u) @ w_out_a

    qkv_c, new_qkv = causal_conv(qkv, prev_qkv, conv_qkv_w)
    qkv_c = jax.nn.silu(qkv_c).astype(jnp.float32)
    q, k, v = jnp.split(qkv_c, [QK_DIM, 2 * QK_DIM], axis=-1)
    q = l2norm(q.reshape(Bsz, L, N_HEADS, HEAD_K)) * (HEAD_K ** -0.5)
    k = l2norm(k.reshape(Bsz, L, N_HEADS, HEAD_K))
    v = v.reshape(Bsz, L, N_HEADS, HEAD_V)
    beta = jax.nn.sigmoid(beta_raw.astype(jnp.float32))
    g = -jnp.exp(a_log.astype(jnp.float32)) * jax.nn.softplus(
        a_raw.astype(jnp.float32) + dt_bias.astype(jnp.float32))
    o, S_fin = gated_delta_chunked(q, k, v, g, beta, S0.astype(jnp.float32), chunk)
    zf = z.astype(jnp.float32).reshape(Bsz, L, N_HEADS, HEAD_V)
    o = rmsnorm(o, onorm_g) * jax.nn.silu(zf)
    y_b = o.reshape(Bsz, L, V_DIM).astype(xn.dtype) @ w_out_b

    m = jax.nn.sigmoid(gate_a) * y_a + jax.nn.sigmoid(gate_b) * y_b
    return m @ w_o, new_a, new_qkv, S_fin.astype(xn.dtype)

def hier_moe(xn, w_rg, b_rg, w_re, b_re, w_gate, w_up, w_down):
    shp = xn.shape
    t = xn.reshape(-1, D_MODEL)
    lg = (t @ w_rg + b_rg).astype(jnp.float32)
    pg = jax.nn.softmax(lg, axis=-1)
    gsel = jnp.argmax(lg, axis=-1)
    pg_sel = jnp.take_along_axis(pg, gsel[:, None], axis=-1)[:, 0]
    le = (t @ w_re + b_re).astype(jnp.float32).reshape(-1, N_GROUPS, EXPERTS_PER_GROUP)
    le_sel = jnp.take_along_axis(le, gsel[:, None, None], axis=1)[:, 0]
    pe = jax.nn.softmax(le_sel, axis=-1)
    top_p, top_i = lax.top_k(pe, TOP_K)
    top_p = top_p / jnp.sum(top_p, axis=-1, keepdims=True)
    expert_id = gsel[:, None] * EXPERTS_PER_GROUP + top_i
    combine = jnp.sum(jax.nn.one_hot(expert_id, N_EXPERTS, dtype=jnp.float32)
                      * (pg_sel[:, None] * top_p)[..., None], axis=1)

    def step(acc, xs):
        wg, wu, wd, c = xs
        hdn = jax.nn.silu(t @ wg) * (t @ wu)
        return acc + c[:, None] * (hdn @ wd).astype(jnp.float32), None

    acc0 = jnp.zeros((t.shape[0], D_MODEL), jnp.float32)
    acc, _ = lax.scan(step, acc0, (w_gate, w_up, w_down, combine.T.astype(t.dtype)))
    return acc.astype(xn.dtype).reshape(shp)

def setup_inputs(seed: int = 0) -> dict:
    key = jax.random.key(seed)
    ks = jax.random.split(key, 24)
    nrm = lambda k, shape, scale: jax.random.normal(k, shape, jnp.float32) * scale
    x_prompt = nrm(ks[0], (BATCH, SEQ, D_MODEL), 1.0)
    x_sample = nrm(ks[1], (DEC_BATCH, DEC_SEQ, D_MODEL), 1.0)
    cache_conv_a = nrm(ks[2], (DEPTH, DEC_BATCH, CONV_A_WIDTH - 1, D_CONV), 1.0)
    cache_conv_qkv = nrm(ks[3], (DEPTH, DEC_BATCH, CONV_QKV_WIDTH - 1, QKV_DIM), 1.0)
    state_gdn = nrm(ks[4], (DEPTH, DEC_BATCH, N_HEADS, HEAD_K, HEAD_V), 0.3)
    norm1_g = 1.0 + nrm(ks[5], (DEPTH, D_MODEL), 0.02)
    w_in = nrm(ks[6], (DEPTH, D_MODEL, IN_DIM), D_MODEL ** -0.5)
    conv_a_w = nrm(ks[7], (DEPTH, CONV_A_WIDTH, D_CONV), CONV_A_WIDTH ** -0.5)
    w_out_a = nrm(ks[8], (DEPTH, D_CONV, D_MODEL), D_CONV ** -0.5)
    conv_qkv_w = nrm(ks[9], (DEPTH, CONV_QKV_WIDTH, QKV_DIM), CONV_QKV_WIDTH ** -0.5)
    a_log = jnp.log(jax.random.uniform(ks[10], (DEPTH, N_HEADS), jnp.float32, 1.0, 16.0))
    dt = jnp.exp(jax.random.uniform(ks[11], (DEPTH, N_HEADS), jnp.float32,
                                    math.log(1e-3), math.log(1e-1)))
    dt_bias = dt + jnp.log(-jnp.expm1(-dt))
    onorm_g = 1.0 + nrm(ks[12], (DEPTH, HEAD_V), 0.02)
    w_out_b = nrm(ks[13], (DEPTH, V_DIM, D_MODEL), V_DIM ** -0.5)
    w_o = nrm(ks[14], (DEPTH, D_MODEL, D_MODEL), D_MODEL ** -0.5)
    norm2_g = 1.0 + nrm(ks[15], (DEPTH, D_MODEL), 0.02)
    w_router_group = nrm(ks[16], (DEPTH, D_MODEL, N_GROUPS), D_MODEL ** -0.5)
    b_router_group = nrm(ks[17], (DEPTH, N_GROUPS), 0.01)
    w_router_expert = nrm(ks[18], (DEPTH, D_MODEL, N_EXPERTS), D_MODEL ** -0.5)
    b_router_expert = nrm(ks[19], (DEPTH, N_EXPERTS), 0.01)
    w_gate = nrm(ks[20], (DEPTH, N_EXPERTS, D_MODEL, D_EXPERT), D_MODEL ** -0.5)
    w_up = nrm(ks[21], (DEPTH, N_EXPERTS, D_MODEL, D_EXPERT), D_MODEL ** -0.5)
    w_down = nrm(ks[22], (DEPTH, N_EXPERTS, D_EXPERT, D_MODEL), D_EXPERT ** -0.5)
    final_g = 1.0 + nrm(ks[23], (D_MODEL,), 0.02)
    return {"x_prompt": x_prompt, "x_sample": x_sample,
            "cache_conv_a": cache_conv_a, "cache_conv_qkv": cache_conv_qkv, "state_gdn": state_gdn,
            "norm1_g": norm1_g, "w_in": w_in, "conv_a_w": conv_a_w, "w_out_a": w_out_a,
            "conv_qkv_w": conv_qkv_w, "a_log": a_log, "dt_bias": dt_bias, "onorm_g": onorm_g,
            "w_out_b": w_out_b, "w_o": w_o, "norm2_g": norm2_g,
            "w_router_group": w_router_group, "b_router_group": b_router_group,
            "w_router_expert": w_router_expert, "b_router_expert": b_router_expert,
            "w_gate": w_gate, "w_up": w_up, "w_down": w_down, "final_g": final_g}

def reference(x_prompt, x_sample, cache_conv_a, cache_conv_qkv, state_gdn,
              norm1_g, w_in, conv_a_w, w_out_a, conv_qkv_w, a_log, dt_bias, onorm_g,
              w_out_b, w_o, norm2_g, w_router_group, b_router_group,
              w_router_expert, b_router_expert, w_gate, w_up, w_down, final_g):
    def run(x, prev_a, prev_qkv, S0):
        chunk = min(CHUNK, x.shape[1])
        new_a, new_qkv, new_S = [], [], []
        for l in range(DEPTH):
            mix, na, nq, ns = token_mixers(rmsnorm(x, norm1_g[l]), prev_a[l], prev_qkv[l], S0[l],
                                           w_in[l], conv_a_w[l], w_out_a[l], conv_qkv_w[l],
                                           a_log[l], dt_bias[l], onorm_g[l], w_out_b[l], w_o[l], chunk)
            x = x + mix
            x = x + hier_moe(rmsnorm(x, norm2_g[l]), w_router_group[l], b_router_group[l],
                             w_router_expert[l], b_router_expert[l], w_gate[l], w_up[l], w_down[l])
            new_a.append(na)
            new_qkv.append(nq)
            new_S.append(ns)
        return rmsnorm(x, final_g), jnp.stack(new_a), jnp.stack(new_qkv), jnp.stack(new_S)

    bp = x_prompt.shape[0]
    dt_ = x_prompt.dtype
    zero_a = jnp.zeros((DEPTH, bp, CONV_A_WIDTH - 1, D_CONV), dt_)
    zero_qkv = jnp.zeros((DEPTH, bp, CONV_QKV_WIDTH - 1, QKV_DIM), dt_)
    zero_S = jnp.zeros((DEPTH, bp, N_HEADS, HEAD_K, HEAD_V), dt_)
    y_prompt, conv_a_prompt, conv_qkv_prompt, gdn_prompt = run(x_prompt, zero_a, zero_qkv, zero_S)
    y_sample, conv_a_sample, conv_qkv_sample, gdn_sample = run(x_sample, cache_conv_a,
                                                               cache_conv_qkv, state_gdn)
    return (y_prompt, y_sample, conv_a_prompt, conv_qkv_prompt, gdn_prompt,
            conv_a_sample, conv_qkv_sample, gdn_sample)


_drawn_inputs = setup_inputs


def setup_inputs(seed=0):
    import zlib

    import numpy as np

    out = dict(_drawn_inputs(seed))
    spreads = {}
    factors = {'onorm_g': 28.78,
     'b_router_group': 43.027,
     'b_router_expert': 12.28,
     'final_g': 24.587,
     'norm2_g': 6.192}
    for name, (base, spread) in spreads.items():
        noise = np.random.default_rng([zlib.crc32(name.encode()), seed]).standard_normal(out[name].shape)
        drawn = base * np.exp(spread * noise) if base else spread * noise
        out[name] = __import__('jax').numpy.asarray(drawn.astype(out[name].dtype))
    for name, factor in factors.items():
        out[name] = (out[name] * factor).astype(out[name].dtype)
    return out
```

```python
from contextlib import ExitStack

import numpy as np

import concourse.bass as bass
from concourse import mybir

F32 = mybir.dt.float32
F32R = mybir.dt.float32r
I32 = mybir.dt.int32
ALU = mybir.AluOpType
ACT = mybir.ActivationFunctionType
X = mybir.AxisListType.X

P = 128
D = 1024
KC = D // P
PROMPT, STREAM = 512, 64
TOK = PROMPT + STREAM
HALF = TOK // 2
UNITS = 5
UW = UNITS * P
HEADS = 8
EPS = 1e-6
LEVELS = 6
GROUPS, PER_GROUP = 4, 8
EXPERTS = GROUPS * PER_GROUP
DE = 256
SLOTS = 2 * TOK
BLOCKS = EXPERTS + (SLOTS - EXPERTS) // P
ROWS = SLOTS + P

TQ, TK, TV, TZ, TGA, TGB, TH, TC, TB = range(9)
TILES = 9
PER = 3
POS = 2 * TILES * PER
ACT_HALVES = 2 * TC
DVE_HALVES = 2 * TILES - ACT_HALVES

PAR_QKV, PAR_A, PAR_CQKV, PAR_CA, PARS = 0, 12, 15, 24, 26
KBETA, KSUM, KEXP, KBEXP, KREST, KLAST, KINDS = range(7)
DEC_STEPS, DEC_ACTS = 11, 7
ROUTE_STEPS, R_GAP, R_PAIRS = 69, 24, 29
C_ID, C_UPPER, C_LOWER, C_ONES, C_BEFORE, C_LEVEL = (P * k for k in range(6))
C_MISC = C_LEVEL + P * (LEVELS + 1)
M_VALID, M_ALOG, M_DT, M_RBIAS, M_IOTA, M_END = 0, 5, 13, 21, 57, 57 + 40
CONSTS = C_MISC + M_END


def wait(engine, sem, value):
    if not isinstance(value, int) or value > 0:
        engine.wait_ge(sem, value)


def at(index, length=1):
    return bass.ds(index, length)


PIECES = [[(0, HALF, 0, False)], [(0, PROMPT - HALF, HALF, False), (PROMPT - HALF, STREAM, 0, True)]]


def padded(first, stream, pad):
    return first + (PROMPT + 2 * pad if stream else pad)


def encoder_layer(nc, A, O):
    scr_gate = nc.dram_tensor("scr_gate", (HEADS, 2, P, TOK), F32, kind="Internal").ap()
    scr_x2 = nc.dram_tensor("scr_x2", (UNITS * P, D), F32, kind="Internal").ap()
    scr_rows = nc.dram_tensor("scr_rows", (ROWS, D), F32, kind="Internal").ap()
    scr_y = nc.dram_tensor("scr_y", (BLOCKS * P, D), F32, kind="Internal").ap()

    top = ExitStack()
    with top:
        def sem(name):
            return top.enter_context(nc.semaphore(name))

        def sb(ctx, name, shape, dt=F32):
            return ctx.enter_context(nc.sbuf_tensor(name, shape, dt))

        proj = [top.enter_context(nc.psum_tensor(f"proj{k}", [P, 512], F32)) for k in range(3)]
        wideA = top.enter_context(nc.psum_tensor("wideA", [P, 1024], F32))
        wideB = top.enter_context(nc.psum_tensor("wideB", [P, 1024], F32))
        small = top.enter_context(nc.psum_tensor("small", [P, 512], F32))

        const = sb(top, "const", [P, CONSTS])
        ident = const[:, C_ID:C_ID + P]
        upper = const[:, C_UPPER:C_UPPER + P]
        ones = const[:, C_ONES:C_ONES + P]
        before = const[:, C_BEFORE:C_BEFORE + P]

        def level_mask(k):
            c = C_LEVEL + P * k
            return const[:, c:c + P].unsqueeze(1).to_broadcast([P, UNITS, P])

        lower_mask = const[:, C_LOWER:C_LOWER + P].unsqueeze(1).to_broadcast([P, UNITS, P])
        misc = const[:, C_MISC:CONSTS]
        small_sb = sb(top, "stats", [P, 64])
        epsq = small_sb[:, 60:62]
        coef = sb(top, "coef", [P, 2, UNITS])
        slot_row = sb(top, "slot_row", [P, 2 * UNITS], I32)
        slot_y = sb(top, "slot_y", [P, 2 * UNITS], I32)
        table = sb(top, "block_table", [1, 2 * BLOCKS], I32)

        ph1 = ExitStack()
        xnh = sb(ph1, "xnh", [P, KC, UW], F32R)
        xnl = sb(ph1, "xnl", [P, KC, UW], F32R)
        wraw = [sb(ph1, f"wraw{k}", [P, KC, P]) for k in range(3)]
        whi = [sb(ph1, f"whi{k}", [P, KC, P], F32R) for k in range(3)]
        wlo = [sb(ph1, f"wlo{k}", [P, KC, P], F32R) for k in range(3)]
        yab = ExitStack()
        ya = sb(yab, "ya", [P, HEADS, TOK])
        yb = sb(yab, "yb", [P, HEADS, TOK])
        gd = ExitStack()
        raw = sb(gd, "raw", [P, 3, TOK + 6])
        ubuf = sb(gd, "ubuf", [P, TOK + 4])
        aout = sb(gd, "aout", [P, TOK + 2])
        cout = [sb(gd, f"cout{k}", [P, TOK + 3]) for k in range(2)]
        sil = sb(gd, "sil", [P, 3, UW])
        gate = [sb(gd, f"gate{k}", [P, TOK]) for k in range(2)]
        par = sb(gd, "par", [P, HEADS, PARS])
        pcur = sb(gd, "pcur", [P, PAR_CQKV])
        dec = sb(gd, "dec", [P, HEADS, KINDS, UNITS])
        gcur = sb(gd, "gcur", [P, KINDS, UNITS])
        norms = sb(gd, "norms", [P, KC + 1])
        tails = sb(gd, "tails", [P, HEADS, 22])
        buf1 = sb(gd, "buf1", [P, 2 * UW])
        buf2 = sb(gd, "buf2", [P, 2 * UW])
        buf3 = sb(gd, "buf3", [P, 2 * UW])
        vbeta = sb(gd, "vbeta", [P, UW])
        kbexp = sb(gd, "kbexp", [P, UW])
        krest = sb(gd, "krest", [P, UW])
        kT = sb(gd, "kT", [P, UW])
        qT = sb(gd, "qT", [P, UW])
        T = sb(gd, "T", [P, UW])
        TT = sb(gd, "TT", [P, UW])
        vn = sb(gd, "vn", [P, UW])
        Sp = sb(gd, "Sp", [P, P])
        Ss = sb(gd, "Ss", [P, P])
        st = sb(gd, "st", [P, 40])
        dtmp = sb(gd, "dtmp", [P, 8, UNITS * HEADS])
        basb = sb(gd, "basb", [P, UNITS, 16])
        gd.close()

        g0 = ExitStack()
        xin = [sb(g0, f"xin{k}", [P, D]) for k in range(2)]
        sqx = sb(g0, "sqx", [P, D])
        w16 = sb(g0, "w16", [P, KC, 16])
        w16h = sb(g0, "w16h", [P, KC, 16], F32R)
        w16l = sb(g0, "w16l", [P, KC, 16], F32R)
        g0.close()

        g2 = ExitStack()
        ybh = sb(g2, "ybh", [P, KC, TOK], F32R)
        ybl = sb(g2, "ybl", [P, KC, TOK], F32R)
        tg = [sb(g2, f"tg{k}", [P, TOK]) for k in range(2)]
        mix = [sb(g2, f"mix{k}", [P, TOK]) for k in range(2)]
        g2.close()
        yab.close()
        m_ctx = ExitStack()
        mh = sb(m_ctx, "mh", [P, KC, TOK], F32R)
        ml = sb(m_ctx, "ml", [P, KC, TOK], F32R)
        x2 = sb(m_ctx, "x2", [P, UNITS, D])
        oT = [sb(m_ctx, f"oT{k}", [P, UW]) for k in range(2)]
        m_ctx.close()
        ph1.close()
        p3 = ExitStack()
        tn = sb(p3, "tn", [P, UNITS, D])
        g2row = sb(p3, "g2row", [P, D])
        wr = sb(p3, "wr", [P, KC, GROUPS + EXPERTS])
        tT = [sb(p3, f"tT{k}", [P, D]) for k in range(2)]
        zero = sb(p3, "zero", [P, D])
        sqs = sb(p3, "sqs", [P, D])
        lg = sb(p3, "lg", [P, UNITS, GROUPS + EXPERTS])
        r4 = [sb(p3, f"r4_{k}", [P, UNITS, GROUPS]) for k in range(4)]
        r8 = [sb(p3, f"r8_{k}", [P, UNITS, PER_GROUP]) for k in range(5)]
        r5 = sb(p3, "r5", [P, 12, UNITS])
        r32 = [sb(p3, f"r32_{k}", [P, UNITS, EXPERTS]) for k in range(5)]
        ex = sb(p3, "ex", [P, 6, EXPERTS])
        bt = sb(p3, "bt", [P, 3, BLOCKS, EXPERTS])
        brow = sb(p3, "brow", [P, 4, BLOCKS])
        p3.close()
        p4 = ExitStack()
        eraw = [sb(p4, f"eraw{k}", [P, 24 * DE]) for k in range(2)]
        ehi = [sb(p4, f"ehi{k}", [P, 24 * DE], F32R) for k in range(2)]
        elo = [sb(p4, f"elo{k}", [P, 24 * DE], F32R) for k in range(2)]
        xb = [sb(p4, f"xb{k}", [P, D]) for k in range(2)]
        xbh = [sb(p4, f"xbh{k}", [P, D], F32R) for k in range(2)]
        xbl = [sb(p4, f"xbl{k}", [P, D], F32R) for k in range(2)]
        yout = [sb(p4, f"yout{k}", [P, D]) for k in range(2)]
        hgate = [sb(p4, f"hgate{k}", [P, DE]) for k in range(2)]
        hid = [sb(p4, f"hid{k}", [P, DE]) for k in range(2)]
        hth = [sb(p4, f"hth{k}", [P, DE], F32R) for k in range(2)]
        htl = [sb(p4, f"htl{k}", [P, DE], F32R) for k in range(2)]
        p4.close()
        p5 = ExitStack()
        fx = [sb(p5, f"fx{k}", [P, D]) for k in range(2)]
        fy = [[sb(p5, f"fy{j}_{k}", [P, D]) for k in range(2)] for j in range(2)]
        fsq = sb(p5, "fsq", [P, D])
        fgrow = sb(p5, "fgrow", [P, D])
        p5.close()

        const_in = sem("const_in")
        x_in = [sem(f"x_in{k}") for k in range(2)]
        zeroed = sem("zeroed")
        x_square, x_root, x_recip, x_scaled = (sem(f"x_{s}") for s in ("square", "root", "recip", "scaled"))
        x_turned, x_high, x_low = (sem(f"x_{s}") for s in ("turned", "high", "low"))
        ba_w, ba_done, ba_out = sem("ba_w"), sem("ba_done"), sem("ba_out")
        dec_act, dec_dve, dec_pe = sem("dec_act"), sem("dec_dve"), sem("dec_pe")
        w_in = [sem(f"w_in{k}") for k in range(3)]
        w_high, w_low = sem("w_high"), sem("w_low")
        proj_done = sem("proj_done")
        act_half, dve_half = sem("act_half"), sem("dve_half")
        conv_step, conv_silu = sem("conv_step"), sem("conv_silu")
        gate_out = sem("gate_out")
        a_step = sem("a_step")
        pars_set, tail_kept, gdec_set = sem("pars_set"), sem("tail_kept"), sem("gdec_set")
        names = """qk_turned v_turned sums_spread hats_turned grams a_turned t_turned0 at_done tat_done
            t_turned uw_done ws_done kv_done o_turned
            qk_raw qk_square qk_root decay hats_T a_T tt0 tt_set w_set o_inter o_square o_root
            qk_sum qk_recip hats v_scaled dgap dclip decay_cut attn_set a_cut a_scaled t_cut t_set0 x_set t_set u_set
            vn_set s_set o_set o_sum o_recip o_scaled yb_set
            kbexp_set krest_set s_zero s_in s_out""".split()
        s = {n: sem(n) for n in names}
        tails_out = sem("tails_out")

        U = [slice(u * P, (u + 1) * P) for u in range(UNITS)]
        scan0 = 20 + 3 * LEVELS

        def spread(kind):
            return gcur[:, kind, :].unsqueeze(2).to_broadcast([P, UNITS, P])

        def units(ap):
            return ap.rearrange("p (u m) -> p u m", m=P)

        def gdn_tensor(pe, p, g):
            n = g + 1
            if p == 0:
                pe.wait_ge(conv_silu, 3 * g + 2)
                wait(pe, s["yb_set"], g)
                wait(pe, s["o_set"], g)
                for u in range(UNITS):
                    pe.transpose(wideA[:, U[u]], sil[:, 0, U[u]], ident)
                for u in range(UNITS):
                    mm = pe.transpose(wideB[:, U[u]], sil[:, 1, U[u]], ident)
                mm.then_inc(s["qk_turned"], 1)
            if p == 2:
                pe.wait_ge(conv_silu, 3 * g + 3)
                pe.wait_ge(s["qk_raw"], n)
                for u in range(UNITS):
                    mm = pe.transpose(wideA[:, U[u]], sil[:, 2, U[u]], ident)
                mm.then_inc(s["v_turned"], 1)
            if p == 4:
                pe.wait_ge(s["v_scaled"], n)
                pe.wait_ge(gdec_set, n)
                for u in range(UNITS):
                    mm = pe.transpose(wideA[:, U[u]], gcur[:, KSUM, u:u + 1].to_broadcast([P, P]), ident)
                mm.then_inc(s["sums_spread"], 1)
            if p == 8:
                pe.wait_ge(s["hats"], n)
                pe.wait_ge(s["dgap"], n)
                for u in range(UNITS):
                    pe.transpose(wideA[:, U[u]], buf3[:, u * P:(u + 1) * P], ident)
                for u in range(UNITS):
                    mm = pe.transpose(wideB[:, U[u]], buf3[:, UW + u * P:UW + (u + 1) * P], ident)
                mm.then_inc(s["hats_turned"], 1)
            if p == 11:
                pe.wait_ge(s["hats_T"], n)
                for u in range(UNITS):
                    pe.matmul(wideA[:, U[u]], qT[:, U[u]], kT[:, U[u]], start=True, stop=True)
                for u in range(UNITS):
                    mm = pe.matmul(wideB[:, U[u]], kT[:, U[u]], kT[:, U[u]], start=True, stop=True)
                mm.then_inc(s["grams"], 1)
            if p == 15:
                pe.wait_ge(s["a_scaled"], n)
                for u in range(UNITS):
                    pe.transpose(wideA[:, U[u]], buf1[:, u * P:(u + 1) * P], ident)
                for u in range(UNITS):
                    mm = pe.transpose(wideB[:, U[u]], buf1[:, UW + u * P:UW + (u + 1) * P], ident)
                mm.then_inc(s["a_turned"], 1)
            if p == 17:
                pe.wait_ge(s["t_set0"], n)
                pe.wait_ge(s["a_T"], n)
                for u in range(UNITS):
                    mm = pe.transpose(wideA[:, U[u]], T[:, U[u]], ident)
                mm.then_inc(s["t_turned0"], 1)
            if 19 <= p < 19 + 3 * LEVELS:
                k, step = divmod(p - 19, 3)
                done = g * LEVELS + k
                if step == 0:
                    if k > 0:
                        pe.wait_ge(s["tt_set"], done)
                    for u in range(UNITS):
                        mm = pe.matmul(wideB[:, U[u]], buf3[:, UW + u * P:UW + (u + 1) * P], T[:, U[u]],
                                       start=True, stop=True)
                    mm.then_inc(s["at_done"], 1)
                elif step == 1:
                    pe.wait_ge(s["x_set"], done + 1)
                    if k == 0:
                        pe.wait_ge(s["tt0"], n)
                    for u in range(UNITS):
                        mm = pe.matmul(wideA[:, U[u]], TT[:, U[u]], buf2[:, UW + u * P:UW + (u + 1) * P],
                                       start=True, stop=True)
                    mm.then_inc(s["tat_done"], 1)
                else:
                    pe.wait_ge(s["t_set"], done + 1)
                    for u in range(UNITS):
                        mm = pe.transpose(wideB[:, U[u]], T[:, U[u]], ident)
                    mm.then_inc(s["t_turned"], 1)
            if p == scan0 - 1:
                pe.wait_ge(s["tt_set"], LEVELS * n)
                pe.wait_ge(s["kbexp_set"], n)
                for u in range(UNITS):
                    pe.matmul(wideA[:, U[u]], TT[:, U[u]], vbeta[:, U[u]], start=True, stop=True)
                for u in range(UNITS):
                    mm = pe.matmul(wideB[:, U[u]], kbexp[:, U[u]], TT[:, U[u]], start=True, stop=True)
                mm.then_inc(s["uw_done"], 1)
            if scan0 + 1 <= p < scan0 + 9:
                c, step = divmod(p - scan0 - 1, 2)
                if step == 0:
                    if c == 0:
                        pe.wait_ge(s["w_set"], n)
                        pe.wait_ge(s["s_zero"], n)
                        pe.wait_ge(s["s_in"], 16 * n)
                        wait(pe, s["o_inter"], 4 * g)
                    else:
                        pe.wait_ge(s["s_set"], 4 * g + c)
                        pe.wait_ge(s["o_inter"], 4 * g + c)
                    mm = None
                    for u, state, o in [(c, Sp, 0)] + ([(4, Ss, 2 * P)] if c == 0 else []):
                        pe.matmul(small[:, o:o + P], buf1[:, UW + u * P:UW + (u + 1) * P], state[:, :],
                                  start=True, stop=True)
                        mm = pe.matmul(small[:, o + P:o + 2 * P], qT[:, U[u]], state[:, :], start=True, stop=True)
                    mm.then_inc(s["ws_done"], 1)
                else:
                    pe.wait_ge(s["vn_set"], 4 * g + c + 1)
                    pe.wait_ge(s["krest_set"], n)
                    for u, o in [(c, 0)] + ([(4, P)] if c == 0 else []):
                        pe.matmul(wideB[:, U[u]], buf3[:, u * P:(u + 1) * P], vn[:, U[u]], start=True, stop=True)
                        mm = pe.matmul(wideA[:, o:o + P], krest[:, U[u]], vn[:, U[u]], start=True, stop=True)
                    mm.then_inc(s["kv_done"], 1)
            if p == 52:
                pe.wait_ge(s["o_scaled"], n)
                for u in range(UNITS):
                    mm = pe.transpose(wideA[:, U[u]], vn[:, U[u]], ident)
                mm.then_inc(s["o_turned"], 1)

        def gdn_scalar(act, p, g):
            n = g + 1
            if p == 0:
                act.wait_ge(s["qk_turned"], n)
                wait(act, s["uw_done"], g)
                wait(act, s["kv_done"], 4 * g)
                act.activation(buf1[:, 0:UW], wideA[:, 0:UW], ACT.Copy)
                act.activation(buf1[:, UW:2 * UW], wideB[:, 0:UW], ACT.Copy).then_inc(s["qk_raw"], 1)
                wait(act, s["o_sum"], g)
                act.wait_ge(s["qk_raw"], n)
                act.activation(buf2[:, :], buf1[:, :], ACT.Square).then_inc(s["qk_square"], 1)
            if p == 3:
                act.wait_ge(s["qk_sum"], n)
                act.activation(st[:, 10:15], st[:, 0:5], ACT.Sqrt, scale=float(P), bias=epsq[:, 0:1])
                act.activation(st[:, 15:20], st[:, 5:10], ACT.Sqrt, bias=epsq[:, 1:2]).then_inc(s["qk_root"], 1)
            if p == 6:
                act.wait_ge(s["dclip"], n)
                act.activation(buf2[:, 0:UW], buf2[:, 0:UW], ACT.Exp, scale=-1.0).then_inc(s["decay"], 1)
            if p == 8:
                act.wait_ge(s["hats_turned"], n)
                act.activation(qT[:, :], wideA[:, 0:UW], ACT.Copy)
                act.activation(kT[:, :], wideB[:, 0:UW], ACT.Copy).then_inc(s["hats_T"], 1)
            if p == 15:
                act.wait_ge(s["a_turned"], n)
                act.wait_ge(s["krest_set"], n)
                act.activation(buf3[:, 0:UW], wideA[:, 0:UW], ACT.Copy)
                act.activation(buf3[:, UW:2 * UW], wideB[:, 0:UW], ACT.Copy).then_inc(s["a_T"], 1)
            if p == 17:
                act.wait_ge(s["t_turned0"], n)
                act.activation(TT[:, :], wideA[:, 0:UW], ACT.Copy).then_inc(s["tt0"], 1)
            if 19 <= p < 19 + 3 * LEVELS and (p - 19) % 3 == 2:
                k = (p - 19) // 3
                act.wait_ge(s["t_turned"], g * LEVELS + k + 1)
                act.activation(TT[:, :], wideB[:, 0:UW], ACT.Copy).then_inc(s["tt_set"], 1)
            if p == scan0 - 1:
                act.wait_ge(s["uw_done"], n)
                act.activation(buf1[:, UW:2 * UW], wideB[:, 0:UW], ACT.Copy).then_inc(s["w_set"], 1)
            if scan0 + 1 <= p < scan0 + 9 and (p - scan0 - 1) % 2 == 0:
                c = (p - scan0 - 1) // 2
                act.wait_ge(s["ws_done"], 4 * g + c + 1)
                act.wait_ge(s["vn_set"], 4 * g + c + 1)
                if c == 0:
                    act.activation(kT[:, U[4]], small[:, 3 * P:4 * P], ACT.Copy, scale=gcur[:, KEXP, 4:5])
                act.activation(kT[:, U[c]], small[:, P:2 * P], ACT.Copy, scale=gcur[:, KEXP, c:c + 1])\
                   .then_inc(s["o_inter"], 1)
            if p == 47:
                act.wait_ge(s["o_set"], n)
                act.activation(buf2[:, 0:UW], vn[:, :], ACT.Square).then_inc(s["o_square"], 1)
            if p == 48:
                act.wait_ge(s["s_set"], 4 * n)
                for name, state in (("gdn_prompt", Sp), ("gdn_sample", Ss)):
                    act.dma_start(O[name][at(g), :, :].rearrange("a k v -> (a k) v"), state[:, :])\
                       .then_inc(s["s_out"], 16)
            if p == 49:
                act.wait_ge(s["o_sum"], n)
                act.activation(st[:, 35:40], st[:, 30:35], ACT.Sqrt, scale=1.0 / P, bias=epsq[:, 1:2])\
                   .then_inc(s["o_root"], 1)

        def gdn_vector(dve, p, g):
            n = g + 1
            if p == 2:
                dve.wait_ge(s["qk_square"], n)
                dve.tensor_reduce(st[:, 0:10], buf2[:, :].rearrange("p (u m) -> p u m", m=P), X, ALU.add)\
                   .then_inc(s["qk_sum"], 1)
                dve.wait_ge(s["v_turned"], n)
                dve.wait_ge(gdec_set, n)
                dve.tensor_tensor(units(vbeta[:, :]), units(wideA[:, 0:UW]), spread(KBETA), ALU.mult)\
                   .then_inc(s["v_scaled"], 1)
            if p == 4:
                dve.wait_ge(s["qk_root"], n)
                dve.reciprocal(st[:, 20:30], st[:, 10:20]).then_inc(s["qk_recip"], 1)
                dve.wait_ge(s["qk_recip"], n)
                dve.tensor_tensor(units(buf3[:, :]), units(buf1[:, :]),
                                  st[:, 20:30].unsqueeze(2).to_broadcast([P, 2 * UNITS, P]), ALU.mult)\
                   .then_inc(s["hats"], 1)
            if p == 5:
                dve.wait_ge(s["sums_spread"], n)
                dve.tensor_tensor(units(buf2[:, 0:UW]), units(wideA[:, 0:UW]), spread(KSUM), ALU.subtract)\
                   .then_inc(s["dgap"], 1)
                dve.wait_ge(s["dgap"], n)
                dve.tensor_scalar(buf2[:, 0:UW], buf2[:, 0:UW], 0.0, None, ALU.max).then_inc(s["dclip"], 1)
            if p == 7:
                dve.wait_ge(s["decay"], n)
                dve.tensor_tensor(units(buf2[:, 0:UW]), units(buf2[:, 0:UW]), lower_mask, ALU.mult)\
                   .then_inc(s["decay_cut"], 1)
            if p == 11:
                dve.wait_ge(s["grams"], n)
                dve.wait_ge(s["decay_cut"], n)
                dve.tensor_tensor(buf1[:, UW:2 * UW], wideB[:, 0:UW], buf2[:, 0:UW], ALU.mult)\
                   .then_inc(s["a_cut"], 1)
                dve.tensor_tensor(buf1[:, 0:UW], wideA[:, 0:UW], buf2[:, 0:UW], ALU.mult)\
                   .then_inc(s["attn_set"], 1)
                dve.wait_ge(s["a_cut"], n)
                dve.tensor_tensor(units(buf1[:, UW:2 * UW]), units(buf1[:, UW:2 * UW]), spread(KBETA), ALU.mult)\
                   .then_inc(s["a_scaled"], 1)
            if p == 13:
                dve.wait_ge(s["a_scaled"], n)
                dve.tensor_tensor(units(T[:, :]), units(buf1[:, UW:2 * UW]), level_mask(0), ALU.mult)\
                   .then_inc(s["t_cut"], 1)
                dve.wait_ge(s["t_cut"], n)
                dve.tensor_tensor(units(T[:, :]), units(T[:, :]),
                                  ident.unsqueeze(1).to_broadcast([P, UNITS, P]), ALU.add).then_inc(s["t_set0"], 1)
            if 19 <= p < 19 + 3 * LEVELS:
                k, step = divmod(p - 19, 3)
                done = g * LEVELS + k
                if step == 0:
                    dve.wait_ge(s["at_done"], done + 1)
                    dve.tensor_tensor(units(buf2[:, UW:2 * UW]), units(wideB[:, 0:UW]), level_mask(k + 1),
                                      ALU.mult).then_inc(s["x_set"], 1)
                elif step == 1:
                    dve.wait_ge(s["tat_done"], done + 1)
                    dve.tensor_tensor(T[:, :], T[:, :], wideA[:, 0:UW], ALU.add).then_inc(s["t_set"], 1)
            if p == scan0 - 1:
                dve.wait_ge(s["uw_done"], n)
                dve.tensor_copy(buf1[:, 0:UW], wideA[:, 0:UW]).then_inc(s["u_set"], 1)
            if scan0 + 1 <= p < scan0 + 9:
                c, step = divmod(p - scan0 - 1, 2)
                if step == 0:
                    dve.wait_ge(s["ws_done"], 4 * g + c + 1)
                    if c == 0:
                        dve.wait_ge(s["u_set"], n)
                        dve.tensor_tensor(vn[:, U[4]], buf1[:, 4 * P:5 * P], small[:, 2 * P:3 * P], ALU.subtract)
                    dve.tensor_tensor(vn[:, U[c]], buf1[:, c * P:(c + 1) * P], small[:, 0:P], ALU.subtract)\
                       .then_inc(s["vn_set"], 1)
                else:
                    dve.wait_ge(s["kv_done"], 4 * g + c + 1)
                    if c == 0:
                        dve.scalar_tensor_tensor(Ss[:, :], Ss[:, :], gcur[:, KLAST, 4:5], wideA[:, P:2 * P],
                                                 ALU.mult, ALU.add)
                    dve.scalar_tensor_tensor(Sp[:, :], Sp[:, :], gcur[:, KLAST, c:c + 1], wideA[:, 0:P],
                                             ALU.mult, ALU.add).then_inc(s["s_set"], 1)
                    if c == 3:
                        dve.wait_ge(s["o_inter"], 4 * n)
                        dve.tensor_tensor(vn[:, :], kT[:, :], wideB[:, 0:UW], ALU.add).then_inc(s["o_set"], 1)
            if p == 48:
                dve.wait_ge(s["o_square"], n)
                dve.tensor_reduce(st[:, 30:35], units(buf2[:, 0:UW]), X, ALU.add).then_inc(s["o_sum"], 1)
            if p == 50:
                dve.wait_ge(s["o_root"], n)
                dve.reciprocal(st[:, 20:25], st[:, 35:40]).then_inc(s["o_recip"], 1)
                dve.wait_ge(s["o_recip"], n)
                dve.tensor_tensor(units(vn[:, :]), units(vn[:, :]),
                                  st[:, 20:25].unsqueeze(2).to_broadcast([P, UNITS, P]), ALU.mult)\
                   .then_inc(s["o_scaled"], 1)
            if p == 53:
                dve.wait_ge(s["o_turned"], n)
                dve.wait_ge(act_half, ACT_HALVES * g + 2 * TZ + 2)
                head = yb[:, at(g), :].rearrange("p a m -> p (a m)")
                dve.scalar_tensor_tensor(head, wideA[:, 0:TOK], norms[:, KC:KC + 1], head, ALU.mult, ALU.mult)\
                   .then_inc(s["yb_set"], 1)

        def gdn_pool(pool, g):
            n = g + 1
            wait(pool, s["yb_set"], g)
            pool.tensor_copy(gcur[:, :, :], dec[:, at(g), :, :].rearrange("p a k u -> p (a k) u"))\
                .then_inc(gdec_set, 1)
            pool.wait_ge(gdec_set, n)
            pool.wait_ge(s["hats"], n)
            pool.tensor_tensor(units(kbexp[:, :]), units(buf3[:, UW:2 * UW]), spread(KBEXP), ALU.mult)\
                .then_inc(s["kbexp_set"], 1)
            wait(pool, s["s_out"], 32 * g)
            pool.tensor_tensor(units(krest[:, :]), units(buf3[:, UW:2 * UW]), spread(KREST), ALU.mult)\
                .then_inc(s["krest_set"], 1)
            pool.memset(Sp[:, :], 0.0).then_inc(s["s_zero"], 1)
            pool.dma_start(Ss[:, :], A["state"][at(g), :, :].rearrange("a k v -> (a k) v")).then_inc(s["s_in"], 16)

        def half_read(h, i):
            if not isinstance(h, int):
                raise TypeError
            if h < 0:
                h, i = h + 2 * TILES, i - 1
            if isinstance(i, int) and i < 0:
                return act_half, 0
            if h < ACT_HALVES:
                return act_half, ACT_HALVES * i + h + 1
            return dve_half, DVE_HALVES * i + h - ACT_HALVES + 1

        def proj_tensor(pe, p, i):
            h, part = divmod(p, PER)
            t, hh = divmod(h, 2)
            if part == 0:
                if hh == 0:
                    pe.wait_ge(w_low, TILES * i + t + 1)
                wait(pe, *half_read(h - 3, i))
            out = proj[h % 3][:, 0:HALF]
            for j in range(8 * part, 8 * part + 8):
                kc, term = divmod(j, 3)
                w = (whi, whi, wlo)[term][t % 3]
                x = (xnh, xnl, xnh)[term]
                mm = pe.matmul(out, w[:, kc, :], x[:, kc, hh * HALF:(hh + 1) * HALF], start=(j == 0), stop=(j == 23))
            if part == PER - 1:
                mm.then_inc(proj_done, 1)

        def split_high(act, i, t):
            act.wait_ge(w_in[t % 3], 16 * (3 * i + t // 3 + 1))
            wait(act, proj_done, 2 * TILES * i + 2 * (t - 2))
            act.activation(whi[t % 3][:, :, :], wraw[t % 3][:, :, :], ACT.Copy).then_inc(w_high, 1)

        def split_low(dve, i, t):
            dve.wait_ge(w_high, TILES * i + t + 1)
            dve.tensor_tensor(wlo[t % 3][:, :, :], wraw[t % 3][:, :, :], whi[t % 3][:, :, :].bitcast(F32),
                              ALU.subtract).then_inc(w_low, 1)

        CONV_AT = {7 + k: (0, k) for k in range(4)} | {13 + k: (1, k) for k in range(4)} | {19 + k: (2, k) for k in range(4)}
        A_AT = {48: 0, 49: 1, 50: 2}

        def proj_scalar(act, p, i, last=False):
            h, part = divmod(p, PER)
            t, hh = divmod(h, 2)
            if part == 0 and hh == 0 and not (last and t + 2 >= TILES):
                split_high(act, i, t + 2)
            if part == PER - 1 and t < TC:
                act.wait_ge(proj_done, 2 * TILES * i + h + 1)
                src = proj[h % 3]
                if t in (TQ, TK, TV):
                    wait(act, conv_step, 12 * (i - 1) + 4 * (t - TQ) + 4)
                    wait(act, tail_kept, 2 * (i - 1) + 1)
                    for lo, count, first, stream in PIECES[hh]:
                        c = padded(first, stream, 3)
                        ins = act.activation(raw[:, t - TQ, c:c + count], src[:, lo:lo + count], ACT.Copy)
                elif t == TZ:
                    ins = act.activation(yb[:, at(i), hh * HALF:(hh + 1) * HALF].rearrange("p a m -> p (a m)"),
                                         src[:, 0:HALF], ACT.Silu)
                elif t in (TGA, TGB):
                    wait(act, gate_out, 32 * i)
                    ins = act.activation(gate[t - TGA][:, hh * HALF:(hh + 1) * HALF], src[:, 0:HALF], ACT.Tanh,
                                         scale=0.5)
                else:
                    wait(act, tail_kept, 2 * i)
                    wait(act, a_step, 3 * i)
                    for lo, count, first, stream in PIECES[hh]:
                        c = padded(first, stream, 2)
                        ins = act.activation(ubuf[:, c:c + count], src[:, lo:lo + count], ACT.Copy)
                ins.then_inc(act_half, 1)
                if t in (TGA, TGB) and hh == 1:
                    act.wait_ge(act_half, ACT_HALVES * i + 2 * t + 2)
                    act.dma_start(scr_gate[at(i), t - TGA, :, :].rearrange("a p m -> (a p) m"),
                                  gate[t - TGA][:, :]).then_inc(gate_out, 16)
            if p in (11, 17, 23):
                k = (p - 11) // 6
                act.wait_ge(conv_step, 12 * i + 4 * k + 4)
                if k < 2:
                    wait(act, s["qk_turned"], i)
                else:
                    wait(act, s["v_turned"], i)
                act.activation(sil[:, k, 0:PROMPT], cout[k % 2][:, 0:PROMPT], ACT.Silu)
                act.activation(sil[:, k, PROMPT:TOK], cout[k % 2][:, PROMPT + 3:TOK + 3], ACT.Silu)\
                   .then_inc(conv_silu, 1)

        def proj_vector(dve, p, i, last=False):
            h, part = divmod(p, PER)
            t, hh = divmod(h, 2)
            if part == 0 and hh == 0 and not (last and t + 2 >= TILES):
                split_low(dve, i, t + 2)
            if p in CONV_AT:
                k, j = CONV_AT[p]
                n = 12 * i + 4 * k + j
                y = cout[k % 2][:, :]
                if j == 0:
                    dve.wait_ge(act_half, ACT_HALVES * i + 2 * k + 2)
                    dve.wait_ge(pars_set, i + 1)
                    wait(dve, conv_silu, 3 * i + k - 1 if k == 2 else 3 * (i - 1) + (3 if k == 0 else 2))
                    dve.tensor_scalar(y, raw[:, k, 0:TOK + 3], pcur[:, 4 * k:4 * k + 1], None, ALU.mult)\
                       .then_inc(conv_step, 1)
                else:
                    dve.wait_ge(conv_step, n)
                    dve.scalar_tensor_tensor(y, raw[:, k, j:j + TOK + 3], pcur[:, 4 * k + j:4 * k + j + 1], y,
                                             ALU.mult, ALU.add).then_inc(conv_step, 1)
            if p in A_AT:
                j = A_AT[p]
                if j == 0:
                    dve.wait_ge(dve_half, DVE_HALVES * i + 2)
                    dve.tensor_scalar(aout[:, :], ubuf[:, 0:TOK + 2], pcur[:, PAR_A:PAR_A + 1], None, ALU.mult)\
                       .then_inc(a_step, 1)
                else:
                    dve.wait_ge(a_step, 3 * i + j)
                    dve.scalar_tensor_tensor(aout[:, :], ubuf[:, j:j + TOK + 2], pcur[:, PAR_A + j:PAR_A + j + 1],
                                             aout[:, :], ALU.mult, ALU.add).then_inc(a_step, 1)
            if part == PER - 1 and t >= TC:
                dve.wait_ge(proj_done, 2 * TILES * i + h + 1)
                src = proj[h % 3]
                if t == TC:
                    dve.wait_ge(act_half, ACT_HALVES * i + 2 * TH + hh + 1)
                else:
                    dve.wait_ge(a_step, 3 * i + 3)
                for lo, count, first, stream in PIECES[hh]:
                    if t == TC:
                        c = padded(first, stream, 2)
                        ins = dve.tensor_tensor(ubuf[:, c:c + count], src[:, lo:lo + count], ubuf[:, c:c + count],
                                                ALU.mult)
                    else:
                        c = first + (PROMPT + 2 if stream else 0)
                        o = hh * HALF + lo
                        ins = dve.tensor_tensor(ya[:, at(i), o:o + count].rearrange("p a m -> p (a m)"),
                                                src[:, lo:lo + count], aout[:, c:c + count], ALU.mult)
                ins.then_inc(dve_half, 1)

        def proj_pool(pool, i):
            wait(pool, a_step, 3 * i)
            pool.tensor_copy(pcur[:, :], par[:, at(i), 0:PAR_CQKV].rearrange("p a k -> p (a k)"))
            pool.tensor_copy(raw[:, :, PROMPT + 3:PROMPT + 6],
                             par[:, at(i), PAR_CQKV:PAR_CA].rearrange("p a (k j) -> p (a k) j", j=3))
            pool.tensor_copy(ubuf[:, PROMPT + 2:PROMPT + 4],
                             par[:, at(i), PAR_CA:PARS].rearrange("p a k -> p (a k)")).then_inc(pars_set, 1)

        def tails_pool(pool, i, which):
            if which == 0:
                pool.wait_ge(act_half, ACT_HALVES * i + 2 * TV + 2)
                for k in range(2):
                    ins = pool.tensor_copy(
                        tails[:, at(i), 9 * k:9 * k + 9].rearrange("p a (c j) -> p (a c) j", j=3),
                        raw[:, :, PROMPT + k * (STREAM + 3):PROMPT + 3 + k * (STREAM + 3)])
                ins.then_inc(tail_kept, 1)
            else:
                pool.wait_ge(dve_half, DVE_HALVES * i + 2)
                for k in range(2):
                    c = PROMPT + k * (STREAM + 2)
                    ins = pool.tensor_copy(tails[:, at(i), 18 + 2 * k:20 + 2 * k].rearrange("p a j -> p (a j)"),
                                           ubuf[:, c:c + 2])
                ins.then_inc(tail_kept, 1)

        ya_high, yb_high, ya_low, yb_low = (sem(k) for k in ("ya_high", "yb_high", "ya_low", "yb_low"))
        p2_w, g_in = [sem("p2_w0"), sem("p2_w1")], [sem("gate_in0"), sem("gate_in1")]
        p2_high, p2_low, y_done, mixed, m_half, m_sum, m_high, m_low = (
            sem("p2_" + k) for k in ("high", "low", "done", "mixed", "mhalf", "msum", "mhigh", "mlow"))
        o_copied, o_back, x2_set, x2_in, oT_zero = (sem("o_" + k) for k in ("copied", "back", "x2", "x2in", "zero"))
        n_names = "square root recip scaled turned copied logits out rows".split()
        nx = {k: sem("n_" + k) for k in n_names}
        p3_in, route, route_act, route_pe, zero_set, zero_out = (sem(k) for k in
                                                                 ("p3_in", "route", "route_act", "route_pe", "zero_set", "zero_out"))
        spread_rows = sem("spread_rows")
        e_w = [sem("e_w0"), sem("e_w1")]
        e_x = [sem("e_x0"), sem("e_x1")]
        e_high, e_low, e_xt, e_xh, e_xl, e_gu, e_silu, e_hid, e_ht, e_hh, e_hl, e_dn, e_y = (
            sem("e_" + k) for k in "high low xt xh xl gu silu hid ht hh hl dn y".split())
        e_out = [sem("e_out0"), sem("e_out1")]
        f_x = [sem("f_x0"), sem("f_x1")]
        f_y = [sem("f_y0"), sem("f_y1")]
        f_sum, f_sq, f_root, f_rec, f_set = (sem("f_" + k) for k in "sum sq root rec set".split())
        f_out = [sem("f_out0"), sem("f_out1")]

        def wide(c):
            return wideB if c % 2 else wideA

        def table_view(kind):
            return dec[:, :, kind, :]

        def by_head(row):
            return dtmp[:, row, :].rearrange("p (u h) -> p h u", h=HEADS)

        def phase0_tensor(pe):
            pe.wait_ge(const_in, 16 * 4)
            for c in range(UNITS):
                pe.wait_ge(x_scaled, c + 1)
                wait(pe, x_low, c - 1)
                for k in range(KC):
                    mm = pe.transpose(wide(c)[:, k * P:(k + 1) * P], xin[c % 2][:, k * P:(k + 1) * P], ident)
                mm.then_inc(x_turned, 1)
            pe.wait_ge(x_low, UNITS)
            pe.wait_ge(ba_w, 2)
            for c in range(UNITS):
                for j in range(3 * KC):
                    k, term = divmod(j, 3)
                    x = (xnh, xnl, xnh)[term][:, k, c * P:(c + 1) * P]
                    w = (w16h, w16h, w16l)[term][:, k, :]
                    mm = pe.matmul(small[:, 16 * c:16 * c + 16], x, w, start=(j == 0), stop=(j == 3 * KC - 1))
            mm.then_inc(ba_done, 1)
            pe.wait_ge(dec_dve, 6)
            pe.matmul(small[:, 0:UNITS * HEADS], upper, dtmp[:, 7, :], start=True, stop=True)
            pe.matmul(small[:, 64:64 + UNITS * HEADS], ones, dtmp[:, 7, :], start=True, stop=True).then_inc(dec_pe, 1)

        def decays_scalar(act):
            row = dtmp[:, :, :]
            act.wait_ge(dec_dve, 1)
            act.activation(row[:, 0, :], basb[:, :, 0:HEADS], ACT.Tanh, scale=0.5).then_inc(dec_act, 1)
            act.wait_ge(dec_dve, 3)
            act.activation(row[:, 3, :], row[:, 2, :], ACT.Exp, scale=-1.0).then_inc(dec_act, 1)
            act.wait_ge(dec_act, 2)
            act.activation(row[:, 4, :], row[:, 3, :], ACT.Ln, bias=1.0).then_inc(dec_act, 1)
            act.activation(row[:, 6, 0:HEADS], misc[:, M_ALOG:M_ALOG + HEADS], ACT.Exp).then_inc(dec_act, 1)
            act.wait_ge(dec_dve, 10)
            act.activation(table_view(KEXP), table_view(KSUM), ACT.Exp).then_inc(dec_act, 1)
            act.activation(table_view(KREST), table_view(KREST), ACT.Exp).then_inc(dec_act, 1)
            act.activation(table_view(KLAST), by_head(1), ACT.Exp).then_inc(dec_act, 1)

        def decays_vector(dve):
            row = dtmp[:, :, :]

            def framed(r):
                return dtmp[:, r, :].rearrange("p (u h) -> p u h", h=HEADS)

            dve.wait_ge(ba_done, 1)
            dve.tensor_copy(basb[:, :, :], small[:, 0:UNITS * 16].rearrange("p (u h) -> p u h", h=16))\
               .then_inc(dec_dve, 1)
            dve.wait_ge(dec_dve, 1)
            dve.tensor_tensor(framed(1), basb[:, :, HEADS:16],
                              misc[:, M_DT:M_DT + HEADS].unsqueeze(1).to_broadcast([P, UNITS, HEADS]), ALU.add)\
               .then_inc(dec_dve, 1)
            dve.wait_ge(dec_dve, 2)
            dve.scalar_tensor_tensor(row[:, 2, :], row[:, 1, :], -1.0, row[:, 1, :], ALU.mult, ALU.max)\
               .then_inc(dec_dve, 1)
            dve.wait_ge(dec_act, 3)
            dve.scalar_tensor_tensor(row[:, 5, :], row[:, 1, :], 0.0, row[:, 4, :], ALU.max, ALU.add)\
               .then_inc(dec_dve, 1)
            dve.wait_ge(dec_act, 4)
            dve.wait_ge(dec_dve, 4)
            dve.scalar_tensor_tensor(framed(7), framed(5), -1.0,
                                     row[:, 6, 0:HEADS].unsqueeze(1).to_broadcast([P, UNITS, HEADS]),
                                     ALU.mult, ALU.mult).then_inc(dec_dve, 1)
            dve.wait_ge(dec_dve, 5)
            dve.tensor_tensor(framed(7), framed(7),
                              misc[:, M_VALID:M_VALID + UNITS].unsqueeze(2).to_broadcast([P, UNITS, HEADS]),
                              ALU.mult).then_inc(dec_dve, 1)
            dve.tensor_scalar(table_view(KBETA), by_head(0), 0.5, 0.5, ALU.mult, ALU.add).then_inc(dec_dve, 1)
            dve.wait_ge(dec_pe, 1)
            dve.tensor_copy(table_view(KSUM), small[:, 0:UNITS * HEADS].rearrange("p (u h) -> p h u", h=HEADS))\
               .then_inc(dec_dve, 1)
            dve.tensor_copy(row[:, 1, :], small[:, 64:64 + UNITS * HEADS]).then_inc(dec_dve, 1)
            dve.wait_ge(dec_dve, 9)
            dve.tensor_tensor(table_view(KREST), by_head(1), table_view(KSUM), ALU.subtract).then_inc(dec_dve, 1)
            dve.wait_ge(dec_act, 5)
            dve.tensor_tensor(table_view(KBEXP), table_view(KBETA), table_view(KEXP), ALU.mult).then_inc(dec_dve, 1)

        banks = [[proj[0], proj[1]], [proj[2], small]]

        def out_tensor(pe, q, k, xh, xl):
            pe.wait_ge(p2_low, q + 1)
            for hh in range(2):
                if isinstance(q, int) and q < 2:
                    pass
                elif xh is mh and not (isinstance(q, int) and q < 2 * KC + 2):
                    pe.wait_ge(o_copied, q - 2 * KC - 1)
                else:
                    pe.wait_ge(mixed, q - 1)
                for j in range(3 * KC):
                    kc, term = divmod(j, 3)
                    w = (whi, whi, wlo)[term][k]
                    x = (xh, xl, xh)[term]
                    mm = pe.matmul(banks[k][hh][:, 0:HALF], w[:, kc, :], x[:, kc, hh * HALF:(hh + 1) * HALF],
                                   start=(j == 0), stop=(j == 3 * KC - 1))
                mm.then_inc(y_done, 1)

        def back_tensor(pe, q, k):
            pe.wait_ge(o_copied, q - 2 * KC + 1)
            if not (isinstance(q, int) and q < 2 * KC + 2):
                pe.wait_ge(x2_set, q - 2 * KC - 1)
            for u in range(UNITS):
                mm = pe.transpose(wide(k)[:, U[u]], oT[k][:, U[u]], ident)
            mm.then_inc(o_back, 1)

        def phase2_tensor(pe):
            pe.wait_ge(ya_low, 1)
            for k in range(2):
                out_tensor(pe, k, k, xnh, xnl)
            with pe.Fori(1, KC // 2) as j:
                for k in range(2):
                    out_tensor(pe, 2 * j + k, k, xnh, xnl)
            pe.wait_ge(yb_low, 1)
            with pe.Fori(KC // 2, KC) as j:
                for k in range(2):
                    out_tensor(pe, 2 * j + k, k, ybh, ybl)
            pe.wait_ge(m_low, KC)
            first = 2 * KC
            out_tensor(pe, first, 0, mh, ml)
            out_tensor(pe, first + 1, 1, mh, ml)
            back_tensor(pe, first, 0)
            with pe.Fori(KC + 1, KC + KC // 2) as j:
                out_tensor(pe, 2 * j, 0, mh, ml)
                back_tensor(pe, 2 * j - 1, 1)
                out_tensor(pe, 2 * j + 1, 1, mh, ml)
                back_tensor(pe, 2 * j, 0)
            back_tensor(pe, 3 * KC - 1, 1)

        def out_split_high(act, q, k):
            if isinstance(q, int):
                act.wait_ge(p2_w[k], 16 * (q // 2 + 1))
            else:
                act.wait_ge(p2_w[k], 8 * (q - k) + 16)
            wait(act, y_done, 2 * (q - 1))
            act.activation(whi[k][:, :, :], wraw[k][:, :, :], ACT.Copy).then_inc(p2_high, 1)

        def out_split_low(dve, q, k):
            dve.wait_ge(p2_high, q + 1)
            dve.tensor_tensor(wlo[k][:, :, :], wraw[k][:, :, :], whi[k][:, :, :].bitcast(F32), ALU.subtract)\
               .then_inc(p2_low, 1)

        def mix_high(act, q, k):
            m = q - KC
            act.wait_ge(m_sum, m + 1)
            act.activation(mh[:, at(m), :].rearrange("p a m -> p (a m)"), mix[k][:, :], ACT.Copy, scale=0.5)\
               .then_inc(m_high, 1)

        def o_copy(act, q, k):
            n = q - 2 * KC
            act.wait_ge(y_done, 2 * q + 2)
            if not (isinstance(q, int) and n < 2):
                act.wait_ge(o_back, n - 1)
            for hh in range(2):
                ins = act.activation(oT[k][:, hh * HALF:(hh + 1) * HALF], banks[k][hh][:, 0:HALF], ACT.Copy)
            ins.then_inc(o_copied, 1)

        def phase2_scalar(act):
            act.wait_ge(proj_done, 2 * TILES * HEADS)
            act.wait_ge(dve_half, DVE_HALVES * HEADS)
            act.activation(xnh[:, :, 0:TOK], ya[:, :, :], ACT.Copy).then_inc(ya_high, 1)
            for k in range(2):
                out_split_high(act, k, k)
            act.wait_ge(s["yb_set"], HEADS)
            act.wait_ge(s["s_out"], 32 * HEADS)
            act.wait_ge(tails_out, 16)
            act.activation(ybh[:, :, :], yb[:, :, :], ACT.Copy).then_inc(yb_high, 1)
            with act.Fori(1, KC // 2) as j:
                for k in range(2):
                    out_split_high(act, 2 * j + k, k)
            for k in range(2):
                out_split_high(act, KC + k, k)
                if k == 1:
                    act.wait_ge(yb_low, 1)
                    act.wait_ge(ya_low, 1)
                    mix_high(act, KC, 0)
            with act.Fori(KC // 2 + 1, KC) as j:
                out_split_high(act, 2 * j, 0)
                mix_high(act, 2 * j - 1, 1)
                out_split_high(act, 2 * j + 1, 1)
                mix_high(act, 2 * j, 0)
            out_split_high(act, 2 * KC, 0)
            mix_high(act, 2 * KC - 1, 1)
            out_split_high(act, 2 * KC + 1, 1)
            act.wait_ge(oT_zero, 2)
            o_copy(act, 2 * KC, 0)
            with act.Fori(KC + 1, KC + KC // 2) as j:
                out_split_high(act, 2 * j, 0)
                o_copy(act, 2 * j - 1, 1)
                out_split_high(act, 2 * j + 1, 1)
                o_copy(act, 2 * j, 0)
            o_copy(act, 3 * KC - 1, 1)

        def mix_a(dve, q, k):
            if isinstance(q, int):
                dve.wait_ge(g_in[k], 16 * (q // 2 + 1))
            else:
                dve.wait_ge(g_in[k], 8 * (q - k) + 16)
            dve.wait_ge(y_done, 2 * q + 2)
            for hh in range(2):
                h = slice(hh * HALF, (hh + 1) * HALF)
                ins = dve.scalar_tensor_tensor(ya[:, at(q), h].rearrange("p a m -> p (a m)"), tg[k][:, h], 1.0,
                                               banks[k][hh][:, 0:HALF], ALU.add, ALU.mult)
            ins.then_inc(mixed, 1)

        def mix_b(dve, q, k):
            m = q - KC
            if isinstance(q, int):
                dve.wait_ge(g_in[k], 16 * (q // 2 + 1))
                wait(dve, m_high, m - 1)
            else:
                dve.wait_ge(g_in[k], 8 * (q - k) + 16)
                dve.wait_ge(m_high, m - 1)
            dve.wait_ge(y_done, 2 * q + 2)
            for hh in range(2):
                h = slice(hh * HALF, (hh + 1) * HALF)
                ins = dve.scalar_tensor_tensor(mix[k][:, h], tg[k][:, h], 1.0, banks[k][hh][:, 0:HALF],
                                               ALU.add, ALU.mult)
            ins.then_inc(mixed, 1)
            dve.wait_ge(mixed, q + 1)
            dve.tensor_tensor(mix[k][:, :], mix[k][:, :], ya[:, at(m), :].rearrange("p a m -> p (a m)"), ALU.add)\
               .then_inc(m_sum, 1)
            dve.wait_ge(m_high, m + 1)
            dve.scalar_tensor_tensor(ml[:, at(m), :].rearrange("p a m -> p (a m)"), mix[k][:, :], 0.5,
                                     mh[:, at(m), :].bitcast(F32).rearrange("p a m -> p (a m)"),
                                     ALU.mult, ALU.subtract).then_inc(m_low, 1)

        def x2_add(dve, q, k):
            n = q - 2 * KC
            dve.wait_ge(o_back, n + 1)
            dst = x2[:, :, at(n * P, P)]
            dve.tensor_tensor(dst, dst, wide(k)[:, 0:UW].rearrange("p (u m) -> p u m", m=P), ALU.add)\
               .then_inc(x2_set, 1)

        def phase2_vector(dve):
            dve.wait_ge(ya_high, 1)
            dve.tensor_tensor(xnl[:, :, 0:TOK], ya[:, :, :], xnh[:, :, 0:TOK].bitcast(F32), ALU.subtract)\
               .then_inc(ya_low, 1)
            for k in range(2):
                out_split_low(dve, k, k)
            dve.wait_ge(yb_high, 1)
            dve.tensor_tensor(ybl[:, :, :], yb[:, :, :], ybh[:, :, :].bitcast(F32), ALU.subtract)\
               .then_inc(yb_low, 1)
            dve.wait_ge(ya_low, 1)
            mix_a(dve, 0, 0)
            with dve.Fori(1, KC // 2) as j:
                out_split_low(dve, 2 * j, 0)
                mix_a(dve, 2 * j - 1, 1)
                out_split_low(dve, 2 * j + 1, 1)
                mix_a(dve, 2 * j, 0)
            out_split_low(dve, KC, 0)
            mix_a(dve, KC - 1, 1)
            out_split_low(dve, KC + 1, 1)
            mix_b(dve, KC, 0)
            with dve.Fori(KC // 2 + 1, KC) as j:
                out_split_low(dve, 2 * j, 0)
                mix_b(dve, 2 * j - 1, 1)
                out_split_low(dve, 2 * j + 1, 1)
                mix_b(dve, 2 * j, 0)
            out_split_low(dve, 2 * KC, 0)
            mix_b(dve, 2 * KC - 1, 1)
            out_split_low(dve, 2 * KC + 1, 1)
            dve.wait_ge(x2_in, 32)
            dve.wait_ge(oT_zero, 2)
            with dve.Fori(KC + 1, KC + KC // 2) as j:
                out_split_low(dve, 2 * j, 0)
                x2_add(dve, 2 * j - 2, 0)
                out_split_low(dve, 2 * j + 1, 1)
                x2_add(dve, 2 * j - 1, 1)
            x2_add(dve, 3 * KC - 2, 0)
            x2_add(dve, 3 * KC - 1, 1)

        def phase3_scalar(act):
            act.wait_ge(x2_set, KC)
            for c in range(UNITS):
                wait(act, nx["square"], c)
                act.activation(sqs[:, :], x2[:, c, :], ACT.Square, accum_out=small_sb[:, 24 + c:25 + c])\
                   .then_inc(nx["square"], 1)
            act.wait_ge(nx["square"], UNITS)
            act.activation(small_sb[:, 32:32 + UNITS], small_sb[:, 24:24 + UNITS], ACT.Sqrt, scale=1.0 / D,
                           bias=epsq[:, 1:2]).then_inc(nx["root"], 1)
            for c in range(UNITS):
                act.wait_ge(nx["turned"], c + 1)
                wait(act, nx["logits"], c - 1)
                act.activation(tT[c % 2][:, :], wide(c)[:, :], ACT.Copy).then_inc(nx["copied"], 1)
            act.wait_ge(route, R_GAP)
            act.activation(r4[3][:, :, :], r4[2][:, :, :], ACT.Exp).then_inc(route_act, 1)
            act.activation(r5[:, 9, :], r5[:, 8, :], ACT.Exp).then_inc(route_act, 1)

        def phase3_tensor(pe):
            pe.wait_ge(p3_in, 32)
            for c in range(UNITS):
                pe.wait_ge(nx["scaled"], c + 1)
                wait(pe, nx["copied"], c - 1)
                for k in range(KC):
                    mm = pe.transpose(wide(c)[:, k * P:(k + 1) * P], tn[:, c, k * P:(k + 1) * P], ident)
                mm.then_inc(nx["turned"], 1)
                pe.wait_ge(nx["copied"], c + 1)
                n = GROUPS + EXPERTS
                for k in range(KC):
                    mm = pe.matmul(small[:, n * c:n * c + n], tT[c % 2][:, k * P:(k + 1) * P], wr[:, k, :],
                                   start=(k == 0), stop=(k == KC - 1))
                mm.then_inc(nx["logits"], 1)
            pe.wait_ge(route, R_PAIRS)
            E = EXPERTS
            for c in range(UNITS):
                for j in range(c + 1):
                    pe.matmul(proj[0][:, E * c:E * c + E], ones if j < c else before, r32[0][:, j, :],
                              start=(j == 0), stop=(j == c))
            for j in range(UNITS):
                mm = pe.matmul(proj[0][:, E * UNITS:E * UNITS + E], ones, r32[0][:, j, :], start=(j == 0),
                               stop=(j == UNITS - 1))
            mm.then_inc(route_pe, 1)

        def phase3_vector(dve):
            dve.wait_ge(nx["root"], 1)
            dve.reciprocal(small_sb[:, 40:40 + UNITS], small_sb[:, 32:32 + UNITS]).then_inc(nx["recip"], 1)
            dve.wait_ge(nx["recip"], 1)
            dve.wait_ge(p3_in, 32)
            for c in range(UNITS):
                dve.scalar_tensor_tensor(tn[:, c, :], x2[:, c, :], small_sb[:, 40 + c:41 + c], g2row[:, :],
                                         ALU.mult, ALU.mult).then_inc(nx["scaled"], 1)
            dve.wait_ge(nx["logits"], UNITS)
            chain = [0]

            def link(ins):
                chain[0] += 1
                ins.then_inc(route, 1)
                dve.wait_ge(route, chain[0])

            def over(ap, axis, shape):
                return ap.unsqueeze(axis).to_broadcast(shape)

            def first_largest(values, count, top_row, index_row, tmp, chosen):
                shape = [P, UNITS, count]
                iota = over(misc[:, M_IOTA:M_IOTA + count], 1, shape)
                link(dve.tensor_reduce(r5[:, top_row, :], values, X, ALU.max))
                link(dve.tensor_tensor(tmp, values, over(r5[:, top_row, :], 2, shape), ALU.is_equal))
                link(dve.scalar_tensor_tensor(tmp, tmp, -64.0, iota, ALU.mult, ALU.add))
                link(dve.tensor_reduce(r5[:, index_row, :], tmp, X, ALU.min))
                link(dve.tensor_scalar(r5[:, index_row, :], r5[:, index_row, :], 64.0, None, ALU.add))
                link(dve.tensor_tensor(chosen, iota, over(r5[:, index_row, :], 2, shape), ALU.is_equal))

            n = GROUPS + EXPERTS
            link(dve.tensor_tensor(lg[:, :, :], small[:, 0:UNITS * n].rearrange("p (u n) -> p u n", n=n),
                                   over(misc[:, M_RBIAS:M_RBIAS + n], 1, [P, UNITS, n]), ALU.add))
            first_largest(lg[:, :, 0:GROUPS], GROUPS, 0, 1, r4[1][:, :, :], r4[0][:, :, :])
            shape4 = [P, UNITS, GROUPS, PER_GROUP]

            def grouped(t):
                return t.rearrange("p u (g e) -> p u g e", g=GROUPS)

            link(dve.tensor_tensor(grouped(r32[0][:, :, :]), grouped(lg[:, :, GROUPS:n]), over(r4[0][:, :, :], 3, shape4),
                                   ALU.mult))
            link(dve.tensor_reduce(r8[0][:, :, :], r32[0][:, :, :].rearrange("p u (g e) -> p u e g", g=GROUPS), X,
                                   ALU.add))
            first_largest(r8[0][:, :, :], PER_GROUP, 4, 5, r8[4][:, :, :], r8[1][:, :, :])
            link(dve.scalar_tensor_tensor(r8[2][:, :, :], r8[1][:, :, :], -3.0e38, r8[0][:, :, :], ALU.mult, ALU.add))
            first_largest(r8[2][:, :, :], PER_GROUP, 6, 7, r8[4][:, :, :], r8[3][:, :, :])
            link(dve.tensor_tensor(r4[2][:, :, :], lg[:, :, 0:GROUPS], over(r5[:, 0, :], 2, [P, UNITS, GROUPS]),
                                   ALU.subtract))
            link(dve.tensor_tensor(r5[:, 8, :], r5[:, 6, :], r5[:, 4, :], ALU.subtract))
            assert chain[0] == R_GAP, chain
            valid = over(misc[:, M_VALID:M_VALID + UNITS], 2, [P, UNITS, EXPERTS])
            for k, chosen in ((1, r8[1]), (2, r8[3])):
                link(dve.tensor_tensor(grouped(r32[k][:, :, :]), over(r4[0][:, :, :], 3, shape4),
                                       over(chosen[:, :, :], 2, shape4), ALU.mult))
                link(dve.tensor_tensor(r32[k][:, :, :], r32[k][:, :, :], valid, ALU.mult))
            link(dve.tensor_tensor(r32[0][:, :, :], r32[1][:, :, :], r32[2][:, :, :], ALU.add))
            assert chain[0] == R_PAIRS, chain
            dve.wait_ge(route_act, 2)
            link(dve.tensor_reduce(r5[:, 2, :], r4[3][:, :, :], X, ALU.add))
            link(dve.scalar_tensor_tensor(r5[:, 3, :], r5[:, 9, :], 1.0, r5[:, 2, :], ALU.add, ALU.mult))
            link(dve.reciprocal(coef[:, 0, :], r5[:, 3, :]))
            link(dve.tensor_tensor(coef[:, 1, :], coef[:, 0, :], r5[:, 9, :], ALU.mult))
            dve.wait_ge(route_pe, 1)
            E = EXPERTS
            link(dve.tensor_copy(r32[3][:, :, :], proj[0][:, 0:UNITS * E].rearrange("p (u e) -> p u e", e=E)))
            link(dve.tensor_copy(ex[:, 0, :], proj[0][:, UNITS * E:UNITS * E + E]))
            link(dve.tensor_scalar(ex[:, 1, :], ex[:, 0, :], 0.0, None, ALU.is_gt))
            for k in range(1, (TOK - 1) // P + 1):
                link(dve.scalar_tensor_tensor(ex[:, 1, :], ex[:, 0, :], float(P * k), ex[:, 1, :], ALU.is_gt, ALU.add))
            for src, dst in ((0, 2), (1, 3)):
                link(dve.tensor_tensor_scan(ex[:, dst, :], ones[:, 0:E], ex[:, src, :], 0.0, ALU.mult, ALU.add))
                link(dve.tensor_tensor(ex[:, dst, :], ex[:, dst, :], ex[:, src, :], ALU.subtract))
            shape = [P, UNITS, E]
            link(dve.tensor_tensor(r32[4][:, :, :], r32[3][:, :, :], over(ex[:, 2, :], 1, shape), ALU.add))
            for k in (1, 2):
                link(dve.tensor_tensor(r32[0][:, :, :], r32[k][:, :, :], r32[4][:, :, :], ALU.mult))
                link(dve.tensor_reduce(r5[:, 10, :], r32[0][:, :, :], X, ALU.add))
                link(dve.tensor_copy(slot_row[:, (k - 1) * UNITS:k * UNITS], r5[:, 10, :]))
            link(dve.scalar_tensor_tensor(r32[4][:, :, :], over(ex[:, 3, :], 1, shape), float(P), r32[3][:, :, :],
                                          ALU.mult, ALU.add))
            for k in (1, 2):
                link(dve.tensor_tensor(r32[0][:, :, :], r32[k][:, :, :], r32[4][:, :, :], ALU.mult))
                link(dve.tensor_reduce(r5[:, 11, :], r32[0][:, :, :], X, ALU.add))
                link(dve.tensor_copy(slot_y[:, (k - 1) * UNITS:k * UNITS], r5[:, 11, :]))
            one = [1, BLOCKS, E]
            blocks = misc[0:1, M_IOTA:M_IOTA + BLOCKS]
            link(dve.tensor_tensor(bt[0:1, 0, :, :], over(ex[0:1, 3, :], 1, one), over(blocks, 2, one), ALU.is_le))
            link(dve.tensor_reduce(brow[0:1, 0, :], bt[0:1, 0, :, :], X, ALU.add))
            link(dve.tensor_scalar(brow[0:1, 0, :], brow[0:1, 0, :], -1.0, None, ALU.add))
            link(dve.tensor_copy(table[0:1, 0:BLOCKS], brow[0:1, 0, :]))
            link(dve.tensor_tensor(bt[0:1, 1, :, :], over(misc[0:1, M_IOTA:M_IOTA + E], 1, one),
                                   over(brow[0:1, 0, :], 2, one), ALU.is_equal))
            link(dve.scalar_tensor_tensor(ex[0:1, 4, :], ex[0:1, 3, :], -float(P), ex[0:1, 2, :], ALU.mult, ALU.add))
            link(dve.tensor_tensor(bt[0:1, 2, :, :], bt[0:1, 1, :, :], over(ex[0:1, 4, :], 1, one), ALU.mult))
            link(dve.tensor_reduce(brow[0:1, 1, :], bt[0:1, 2, :, :], X, ALU.add))
            link(dve.scalar_tensor_tensor(brow[0:1, 2, :], blocks, float(P), brow[0:1, 1, :], ALU.mult, ALU.add))
            link(dve.tensor_scalar(brow[0:1, 2, :], brow[0:1, 2, :], float(SLOTS), None, ALU.min))
            link(dve.tensor_copy(table[0:1, BLOCKS:2 * BLOCKS], brow[0:1, 2, :]))
            assert chain[0] == ROUTE_STEPS, chain

        GU = 16 * DE

        def rows_turned(pe, b, k):
            pe.wait_ge(e_x[k], 8 * (b - k) + 16)
            wait(pe, e_xl, b)
            v = xb[k][:, :].rearrange("s (p c) -> s c p", c=KC)
            for c in range(KC):
                mm = pe.transpose(wideA[:, c * P:(c + 1) * P], v[:, c, :], ident)
            mm.then_inc(e_xt, 1)

        def down(pe, b, k):
            pe.wait_ge(e_hl, b + 1)
            pe.wait_ge(e_low, 2 * b + 2)
            wait(pe, e_y, b)
            for n in range(2):
                for j in range(6):
                    c, term = divmod(j, 3)
                    x = (hth, htl, hth)[term][k][:, c * P:(c + 1) * P]
                    w = (ehi, ehi, elo)[term][k][:, GU + c * D + 512 * n:GU + c * D + 512 * (n + 1)]
                    mm = pe.matmul(wideB[:, 512 * n:512 * (n + 1)], x, w, start=(j == 0), stop=(j == 5))
            mm.then_inc(e_dn, 1)

        def expert_tensor(pe, b, k, first=False, last=False):
            pe.wait_ge(e_low, 2 * b + 1)
            pe.wait_ge(e_xl, b + 1)
            wait(pe, e_hid, b - 1)
            for j in range(3 * KC):
                c, term = divmod(j, 3)
                x = (xbh, xbl, xbh)[term][k][:, c * P:(c + 1) * P]
                w = (ehi, ehi, elo)[term][k][:, 0:GU].rearrange("p (w c n) -> p w c n", w=2, c=KC)[:, :, c, :]
                mm = pe.matmul(proj[k][:, :].rearrange("p (w n) -> p w n", w=2), x, w, start=(j == 0),
                               stop=(j == 3 * KC - 1))
            mm.then_inc(e_gu, 1)
            if not last:
                rows_turned(pe, b + 1, 1 - k)
            if not first:
                down(pe, b - 1, 1 - k)
            pe.wait_ge(e_hid, b + 1)
            wait(pe, e_hl, b)
            v = hid[k][:, :].rearrange("s (p c) -> s c p", c=2)
            for c in range(2):
                mm = pe.transpose(proj[2][:, c * P:(c + 1) * P], v[:, c, :], ident)
            mm.then_inc(e_ht, 1)

        def phase4_tensor(pe):
            pe.wait_ge(route, ROUTE_STEPS)
            rows_turned(pe, 0, 0)
            expert_tensor(pe, 0, 0, first=True)
            expert_tensor(pe, 1, 1)
            with pe.Fori(1, BLOCKS // 2 - 1) as i:
                for k in range(2):
                    expert_tensor(pe, 2 * i + k, k)
            expert_tensor(pe, BLOCKS - 2, 0)
            expert_tensor(pe, BLOCKS - 1, 1, last=True)
            down(pe, BLOCKS - 1, 1)

        def weights_high(act, b, k, part):
            if part == 0:
                act.wait_ge(e_w[k], 24 * (b - k) + 48)
                wait(act, e_gu, b - 1)
                wait(act, e_dn, b - 1)
                act.activation(ehi[k][:, 0:GU], eraw[k][:, 0:GU], ACT.Copy).then_inc(e_high, 1)
            else:
                act.activation(ehi[k][:, GU:], eraw[k][:, GU:], ACT.Copy).then_inc(e_high, 1)

        def weights_low(dve, b, k, part):
            dve.wait_ge(e_high, 2 * b + 1 + part)
            cols = slice(0, GU) if part == 0 else slice(GU, 24 * DE)
            dve.tensor_tensor(elo[k][:, cols], eraw[k][:, cols], ehi[k][:, cols].bitcast(F32), ALU.subtract)\
               .then_inc(e_low, 1)

        def rows_high(act, b, k):
            act.wait_ge(e_xt, b + 1)
            act.activation(xbh[k][:, :], wideA[:, :], ACT.Copy).then_inc(e_xh, 1)

        def rows_low(dve, b, k):
            dve.wait_ge(e_xh, b + 1)
            dve.tensor_tensor(xbl[k][:, :], wideA[:, :], xbh[k][:, :].bitcast(F32), ALU.subtract).then_inc(e_xl, 1)

        def y_copy(act, b, k):
            act.wait_ge(e_dn, b + 1)
            if not (isinstance(b, int) and b < 2):
                act.wait_ge(e_out[k], 8 * (b - k))
            act.activation(yout[k][:, :], wideB[:, :], ACT.Copy).then_inc(e_y, 1)

        def expert_scalar(act, b, k, first=False, last=False):
            if not last:
                weights_high(act, b + 1, 1 - k, 0)
            act.wait_ge(e_gu, b + 1)
            wait(act, e_hid, b - 1)
            act.activation(hgate[k][:, :], proj[k][:, 0:DE], ACT.Silu).then_inc(e_silu, 1)
            if not last:
                rows_high(act, b + 1, 1 - k)
            if not first:
                y_copy(act, b - 1, 1 - k)
            if not last:
                weights_high(act, b + 1, 1 - k, 1)
            act.wait_ge(e_ht, b + 1)
            act.activation(hth[k][:, :], proj[2][:, 0:DE], ACT.Copy).then_inc(e_hh, 1)

        def phase4_scalar(act):
            act.wait_ge(route, ROUTE_STEPS)
            for part in range(2):
                weights_high(act, 0, 0, part)
            rows_high(act, 0, 0)
            expert_scalar(act, 0, 0, first=True)
            expert_scalar(act, 1, 1)
            with act.Fori(1, BLOCKS // 2 - 1) as i:
                for k in range(2):
                    expert_scalar(act, 2 * i + k, k)
            expert_scalar(act, BLOCKS - 2, 0)
            expert_scalar(act, BLOCKS - 1, 1, last=True)
            y_copy(act, BLOCKS - 1, 1)

        def expert_vector(dve, b, k, last=False):
            if not last:
                weights_low(dve, b + 1, 1 - k, 0)
            dve.wait_ge(e_silu, b + 1)
            wait(dve, e_ht, b - 1)
            dve.tensor_tensor(hid[k][:, :], proj[k][:, DE:2 * DE], hgate[k][:, :], ALU.mult).then_inc(e_hid, 1)
            if not last:
                rows_low(dve, b + 1, 1 - k)
                weights_low(dve, b + 1, 1 - k, 1)
            dve.wait_ge(e_hh, b + 1)
            dve.tensor_tensor(htl[k][:, :], proj[2][:, 0:DE], hth[k][:, :].bitcast(F32), ALU.subtract)\
               .then_inc(e_hl, 1)

        def phase4_vector(dve):
            for part in range(2):
                weights_low(dve, 0, 0, part)
            rows_low(dve, 0, 0)
            expert_vector(dve, 0, 0)
            expert_vector(dve, 1, 1)
            with dve.Fori(1, BLOCKS // 2 - 1) as i:
                for k in range(2):
                    expert_vector(dve, 2 * i + k, k)
            expert_vector(dve, BLOCKS - 2, 0)
            expert_vector(dve, BLOCKS - 1, 1, last=True)

        def phase5_scalar(act):
            for c in range(UNITS):
                r = slice(0, P if c < 4 else STREAM)
                act.wait_ge(f_sum, 2 * c + 2)
                wait(act, f_sq, c)
                act.activation(fsq[r, :], fx[c % 2][r, :], ACT.Square, accum_out=small_sb[r, 48:49]).then_inc(f_sq, 1)
                act.wait_ge(f_sq, c + 1)
                act.activation(small_sb[r, 49:50], small_sb[r, 48:49], ACT.Sqrt, scale=1.0 / D,
                               bias=epsq[r, 1:2]).then_inc(f_root, 1)
                act.wait_ge(f_set, c + 1)
                act.dma_start(O["y"][c * P:c * P + r.stop, :], fx[c % 2][r, :]).then_inc(f_out[c % 2], 16)

        def phase5_vector(dve):
            dve.wait_ge(p3_in, 48)
            for c in range(UNITS):
                r = slice(0, P if c < 4 else STREAM)
                dve.wait_ge(f_x[c % 2], 16 * (c // 2 + 1))
                dve.wait_ge(f_y[c % 2], 32 * (c // 2 + 1))
                for k in range(2):
                    dve.scalar_tensor_tensor(fx[c % 2][r, :], fy[k][c % 2][r, :], coef[r, k, c:c + 1], fx[c % 2][r, :],
                                             ALU.mult, ALU.add).then_inc(f_sum, 1)
                    dve.wait_ge(f_sum, 2 * c + k + 1)
                dve.wait_ge(f_root, c + 1)
                dve.reciprocal(small_sb[r, 50:51], small_sb[r, 49:50]).then_inc(f_rec, 1)
                dve.wait_ge(f_rec, c + 1)
                dve.scalar_tensor_tensor(fx[c % 2][r, :], fx[c % 2][r, :], small_sb[r, 50:51], fgrow[r, :], ALU.mult,
                                         ALU.mult).then_inc(f_set, 1)

        block = top.enter_context(nc.Block())

        @block.sync
        def _(sp):
            sp.dma_start(const[:, :], A["consts"]).then_inc(const_in, 16)
            for c in range(UNITS):
                if c >= 2:
                    sp.wait_ge(x_turned, c - 1)
                rows = P if c < 4 else STREAM
                sp.dma_start(xin[c % 2][0:rows, :], A["x"][c * P:c * P + rows, :]).then_inc(x_in[c % 2], 16)
                if c == 0:
                    sp.dma_start(norms[:, :], A["norms"]).then_inc(const_in, 16)
                    sp.dma_start(w16[:, :, :], A["w16"]).then_inc(const_in, 16)
                    sp.dma_start(par[:, :, :], A["params"]).then_inc(const_in, 16)
                if c < 3:
                    sp.dma_start(wraw[c][:, :, :], A["w_in"][c]).then_inc(w_in[c], 16)

            def tile_load(i, t):
                sp.wait_ge(w_low, TILES * i + t - 2)
                k = i * TILES + t
                sp.dma_start(wraw[t % 3][:, :, :], A["w_in"][at(k)].rearrange("a p k m -> (a p) k m"))\
                  .then_inc(w_in[t % 3], 16)

            for t in range(3, TILES):
                tile_load(0, t)
            with sp.Fori(1, HEADS) as i:
                for t in range(TILES):
                    tile_load(i, t)
            def out_load(q, k):
                wait(sp, p2_low, q - 1)
                sp.dma_start(wraw[k][:, :, :], A["w_out"][at(q)].rearrange("a p k m -> (a p) k m"))\
                  .then_inc(p2_w[k], 16)

            def gate_load(q, which, k):
                wait(sp, mixed, q - 1)
                m = q - KC * which
                sp.dma_start(tg[k][:, :], scr_gate[at(m), which, :, :].rearrange("a p m -> (a p) m"))\
                  .then_inc(g_in[k], 16)

            for k in range(2):
                sp.wait_ge(w_low, TILES * HEADS - 2 + k)
                out_load(k, k)
            sp.wait_ge(gate_out, 32 * HEADS)
            sp.wait_ge(s["yb_set"], HEADS)
            for k in range(2):
                gate_load(k, 0, k)
            with sp.Fori(1, KC // 2) as j:
                for k in range(2):
                    out_load(2 * j + k, k)
                    gate_load(2 * j + k, 0, k)
            with sp.Fori(KC // 2, KC) as j:
                for k in range(2):
                    out_load(2 * j + k, k)
                    gate_load(2 * j + k, 1, k)
            for k in range(2):
                out_load(2 * KC + k, k)
            sp.wait_ge(y_done, 32)
            sp.wait_ge(mixed, 16)
            sp.dma_start(x2[:, 0:4, :], A["x"][0:PROMPT, :].rearrange("(c p) d -> p c d", p=P)).then_inc(x2_in, 16)
            sp.dma_start(x2[0:STREAM, 4, :], A["x"][PROMPT:TOK, :]).then_inc(x2_in, 16)
            with sp.Fori(KC + 1, KC + KC // 2) as j:
                for k in range(2):
                    out_load(2 * j + k, k)
            sp.wait_ge(y_done, 48)
            sp.dma_start(g2row[:, :], A["g2row"]).then_inc(p3_in, 16)
            sp.dma_start(wr[:, :, :], A["w_router"]).then_inc(p3_in, 16)
            sp.wait_ge(x2_set, 8)
            sp.dma_start(scr_x2.rearrange("(c p) d -> p c d", p=P), x2[:, :, :]).then_inc(nx["out"], 16)
            sp.wait_ge(zero_set, 1)
            sp.dma_start(scr_rows[SLOTS:ROWS, :], zero[:, :]).then_inc(zero_out, 16)

            def expert_load(b, k):
                e = sp.value_load(table[0:1, at(b)], min_val=0, max_val=EXPERTS - 1)
                r = sp.value_load(table[0:1, at(b + BLOCKS)], min_val=0, max_val=SLOTS)
                sp.dma_start(xb[k][:, :], scr_rows[at(r, P), :]).then_inc(e_x[k], 16)
                v = eraw[k][:, 0:16 * DE].rearrange("p (w n) -> p w n", w=2)
                for j, w in enumerate(("w_gate", "w_up")):
                    sp.dma_start(v[:, j, :], A[w][at(e), :, :].rearrange("a (p c) n -> (a p) (c n)", p=P))\
                      .then_inc(e_w[k], 16)
                sp.dma_start(eraw[k][:, 16 * DE:], A["w_down"][at(e), :, :].rearrange("a (p c) n -> (a p) (c n)", p=P))\
                  .then_inc(e_w[k], 16)

            sp.wait_ge(route, ROUTE_STEPS)
            sp.wait_ge(spread_rows, 16 * 2 * UNITS)
            sp.wait_ge(nx["out"], 16)
            sp.wait_ge(zero_out, 16)
            for k in range(2):
                expert_load(k, k)

            def y_store(b, k):
                sp.wait_ge(e_y, b + 1)
                sp.dma_start(scr_y[at(b * P, P), :], yout[k][:, :]).then_inc(e_out[k], 16)

            with sp.Fori(1, BLOCKS // 2) as i:
                for k in range(2):
                    sp.wait_ge(e_low, 2 * (2 * i + k - 1))
                    sp.wait_ge(e_xt, 2 * i + k - 1)
                    expert_load(2 * i + k, k)
                    if k == 1:
                        for b in range(2):
                            y_store(2 * i - 2 + b, b)
            for b in range(2):
                y_store(BLOCKS - 2 + b, b)
            sp.wait_ge(e_out[0], 16 * (BLOCKS // 2))
            sp.wait_ge(e_out[1], 16 * (BLOCKS // 2))
            sp.dma_start(fgrow[:, :], A["final_row"]).then_inc(p3_in, 16)
            for c in range(UNITS):
                if c >= 2:
                    sp.wait_ge(f_out[c % 2], 16 * (c // 2))
                rows = P if c < 4 else STREAM
                sp.dma_start(fx[c % 2][0:rows, :], scr_x2[c * P:c * P + rows, :]).then_inc(f_x[c % 2], 16)
            sp.wait_ge(f_out[0], 48)
            sp.wait_ge(f_out[1], 32)
            sp.wait_ge(s["s_out"], 32 * HEADS)
            sp.wait_ge(tails_out, 16)

        @block.gpsimd
        def _(pool):
            pool.memset(epsq[:, 0:1], EPS * P)
            pool.memset(epsq[:, 1:2], EPS).then_inc(zeroed, 1)
            pool.wait_ge(x_turned, 3)
            pool.memset(xin[0][STREAM:P, :], 0.0).then_inc(zeroed, 1)
            pool.wait_ge(x_turned, UNITS)
            pool.wait_ge(ba_w, 2)
            pool.wait_ge(ba_done, 1)
            pool.memset(raw[:, :, 0:3], 0.0)
            pool.memset(ubuf[:, 0:2], 0.0)
            pool.memset(sil[:, :, TOK:UW], 0.0).then_inc(zeroed, 1)
            pool.wait_ge(const_in, 16 * 4)
            proj_pool(pool, 0)
            tails_pool(pool, 0, 0)
            tails_pool(pool, 0, 1)
            pool.wait_ge(dec_dve, DEC_STEPS)
            pool.wait_ge(dec_act, DEC_ACTS)
            with pool.Fori(1, HEADS) as i:
                proj_pool(pool, i)
                gdn_pool(pool, i - 1)
                tails_pool(pool, i, 0)
                tails_pool(pool, i, 1)
            gdn_pool(pool, HEADS - 1)
            pool.wait_ge(tail_kept, 2 * HEADS)
            pool.dma_start(O["tails"], tails[:, :, :]).then_inc(tails_out, 16)
            pool.wait_ge(s["s_out"], 32 * HEADS)
            pool.wait_ge(tails_out, 16)
            pool.wait_ge(y_done, 32)
            pool.memset(oT[0][:, TOK:UW], 0.0)
            pool.memset(oT[1][:, TOK:UW], 0.0).then_inc(oT_zero, 1)
            pool.wait_ge(oT_zero, 1)
            pool.memset(x2[STREAM:P, 4, :], 0.0).then_inc(oT_zero, 1)
            pool.wait_ge(y_done, 48)
            pool.memset(zero[:, :], 0.0).then_inc(zero_set, 1)
            pool.wait_ge(route, ROUTE_STEPS)
            pool.wait_ge(nx["scaled"], UNITS)
            for c in range(UNITS):
                rows = P if c < 4 else STREAM
                for k in range(2):
                    pool.indirect_dma_start(
                        scr_rows[0:SLOTS, :],
                        bass.IndirectOffsetOnAxis(slot_row[0:rows, k * UNITS + c:k * UNITS + c + 1], axis=0),
                        tn[0:rows, c, :], None).then_inc(spread_rows, 16)
            pool.wait_ge(spread_rows, 16 * 2 * UNITS)

            pool.wait_ge(e_out[0], 16 * (BLOCKS // 2))
            pool.wait_ge(e_out[1], 16 * (BLOCKS // 2))
            for c in range(UNITS):
                rows = P if c < 4 else STREAM
                if c >= 2:
                    pool.wait_ge(f_sum, 2 * c - 2)
                for k in range(2):
                    pool.indirect_dma_start(
                        fy[k][c % 2][0:rows, :], None, scr_y[:, :],
                        bass.IndirectOffsetOnAxis(slot_y[0:rows, k * UNITS + c:k * UNITS + c + 1], axis=0))\
                        .then_inc(f_y[c % 2], 16)

        @block.scalar
        def _(act):
            act.wait_ge(zeroed, 1)
            for c in range(UNITS):
                act.wait_ge(x_in[c % 2], 16 * (c // 2 + 1))
                if c == 4:
                    act.wait_ge(zeroed, 2)
                wait(act, x_square, c)
                act.activation(sqx[:, :], xin[c % 2][:, :], ACT.Square, accum_out=small_sb[:, c:c + 1])\
                   .then_inc(x_square, 1)
                act.wait_ge(x_square, c + 1)
                act.activation(small_sb[:, 8 + c:9 + c], small_sb[:, c:c + 1], ACT.Sqrt, scale=1.0 / D,
                               bias=epsq[:, 1:2]).then_inc(x_root, 1)
                act.wait_ge(x_turned, c + 1)
                act.wait_ge(const_in, 16 * 4)
                for k in range(KC):
                    ins = act.activation(xnh[:, k, c * P:(c + 1) * P], wide(c)[:, k * P:(k + 1) * P], ACT.Copy,
                                         scale=norms[:, k:k + 1])
                ins.then_inc(x_high, 1)
            act.activation(w16h[:, :, :], w16[:, :, :], ACT.Copy).then_inc(ba_w, 1)
            split_high(act, 0, 0)
            split_high(act, 0, 1)
            decays_scalar(act)
            act.wait_ge(zeroed, 3)
            for p in range(POS):
                proj_scalar(act, p, 0)
            with act.Fori(1, HEADS - 1) as i:
                for p in range(POS):
                    proj_scalar(act, p, i)
                    gdn_scalar(act, p, i - 1)
            for p in range(POS):
                proj_scalar(act, p, HEADS - 1, last=True)
                gdn_scalar(act, p, HEADS - 2)
            for p in range(POS):
                gdn_scalar(act, p, HEADS - 1)
            phase2_scalar(act)
            phase3_scalar(act)
            phase4_scalar(act)
            phase5_scalar(act)

        @block.vector
        def _(dve):
            for c in range(UNITS):
                dve.wait_ge(x_root, c + 1)
                dve.reciprocal(small_sb[:, 16 + c:17 + c], small_sb[:, 8 + c:9 + c]).then_inc(x_recip, 1)
                dve.wait_ge(x_recip, c + 1)
                dve.tensor_scalar(xin[c % 2][:, :], xin[c % 2][:, :], small_sb[:, 16 + c:17 + c], None, ALU.mult)\
                   .then_inc(x_scaled, 1)
                dve.wait_ge(x_high, c + 1)
                for k in range(KC):
                    ins = dve.scalar_tensor_tensor(xnl[:, k, c * P:(c + 1) * P], wide(c)[:, k * P:(k + 1) * P],
                                                   norms[:, k:k + 1], xnh[:, k, c * P:(c + 1) * P].bitcast(F32),
                                                   ALU.mult, ALU.subtract)
                ins.then_inc(x_low, 1)
            dve.wait_ge(ba_w, 1)
            dve.tensor_tensor(w16l[:, :, :], w16[:, :, :], w16h[:, :, :].bitcast(F32), ALU.subtract).then_inc(ba_w, 1)
            split_low(dve, 0, 0)
            split_low(dve, 0, 1)
            decays_vector(dve)
            dve.wait_ge(zeroed, 3)
            for p in range(POS):
                proj_vector(dve, p, 0)
            with dve.Fori(1, HEADS - 1) as i:
                for p in range(POS):
                    proj_vector(dve, p, i)
                    gdn_vector(dve, p, i - 1)
            for p in range(POS):
                proj_vector(dve, p, HEADS - 1, last=True)
                gdn_vector(dve, p, HEADS - 2)
            for p in range(POS):
                gdn_vector(dve, p, HEADS - 1)
            phase2_vector(dve)
            phase3_vector(dve)
            phase4_vector(dve)
            phase5_vector(dve)

        @block.tensor
        def _(pe):
            phase0_tensor(pe)
            for p in range(POS):
                proj_tensor(pe, p, 0)
            with pe.Fori(1, HEADS) as i:
                for p in range(POS):
                    proj_tensor(pe, p, i)
                    gdn_tensor(pe, p, i - 1)
            for p in range(POS):
                gdn_tensor(pe, p, HEADS - 1)
            phase2_tensor(pe)
            phase3_tensor(pe)
            phase4_tensor(pe)


def constants():
    i, j = np.arange(P)[:, None], np.arange(P)[None, :]
    parts = [i == j, i <= j, i >= j, np.ones((P, P)), i < j]
    for k in range(LEVELS + 1):
        b = 2 ** k
        cut = (i // (2 * b) == j // (2 * b)) & ((i // b) % 2 == 1) & ((j // b) % 2 == 0)
        parts.append(-cut.astype(np.float32))
    valid = np.ones((P, UNITS))
    valid[STREAM:, UNITS - 1] = 0
    return np.concatenate([np.asarray(p, np.float32) for p in parts], axis=1), valid.astype(np.float32)


def rows128(a):
    a = np.asarray(a)
    return np.moveaxis(a.reshape(a.shape[:-1] + (-1, P)), -1, 0)


def tiles_of(w):
    w = np.asarray(w)
    return w.reshape(KC, P, -1, P).transpose(2, 1, 0, 3)


def kernel(x_prompt, x_sample, cache_conv_a, cache_conv_qkv, state_gdn, norm1_g, w_in, conv_a_w, w_out_a,
           conv_qkv_w, a_log, dt_bias, onorm_g, w_out_b, w_o, norm2_g, w_router_group, b_router_group,
           w_router_expert, b_router_expert, w_gate, w_up, w_down, final_g):
    import concourse.bacc as bacc
    from concourse.bass_utils import run_bass_kernel_spmd

    table, valid = constants()

    def spread(row):
        return np.broadcast_to(np.asarray(row).reshape(1, -1), (P, np.asarray(row).size))

    iota = spread(np.arange(40, dtype=np.float32))
    consts = np.concatenate([table, valid, spread(a_log[0]), spread(dt_bias[0]),
                             spread(b_router_group[0]), spread(b_router_expert[0]), iota], axis=1)
    w_in = np.asarray(w_in)[0]
    qkv = 3 * D
    z = 6 * D
    ba = 7 * D
    gates = 7 * D + 2 * HEADS
    starts = {TQ: qkv, TK: qkv + D, TV: qkv + 2 * D, TZ: z, TGA: gates, TGB: gates + D, TH: 0, TC: 2 * D, TB: D}
    by_kind = np.stack([tiles_of(w_in[:, starts[t]:starts[t] + D]) for t in range(TILES)], axis=1)
    params = np.concatenate([
        rows128(conv_qkv_w[0].reshape(4, 3, D)).transpose(0, 3, 2, 1).reshape(P, HEADS, 12),
        rows128(conv_a_w[0]).transpose(0, 2, 1),
        rows128(np.asarray(cache_conv_qkv)[0, 0].reshape(3, 3, D)).transpose(0, 3, 2, 1).reshape(P, HEADS, 9),
        rows128(np.asarray(cache_conv_a)[0, 0]).transpose(0, 2, 1)], axis=2)
    norms = np.concatenate([rows128(norm1_g[0]), rows128(onorm_g[0])], axis=1)
    arrays = {
        "x": np.concatenate([np.asarray(x_prompt)[0], np.asarray(x_sample)[0]], axis=0),
        "consts": consts,
        "norms": norms,
        "params": params,
        "w16": w_in[:, ba:gates].reshape(KC, P, 16).transpose(1, 0, 2),
        "w_in": by_kind.reshape(HEADS * TILES, P, KC, P),
        "w_out": np.concatenate([tiles_of(w_out_a[0]), tiles_of(w_out_b[0]), tiles_of(w_o[0])], axis=0),
        "state": np.asarray(state_gdn)[0, 0],
        "g2row": spread(norm2_g[0]),
        "final_row": spread(final_g),
        "w_router": np.concatenate([np.asarray(w_router_group)[0], np.asarray(w_router_expert)[0]], axis=1)
        .reshape(KC, P, GROUPS + EXPERTS).transpose(1, 0, 2),
        "w_gate": np.asarray(w_gate)[0], "w_up": np.asarray(w_up)[0], "w_down": np.asarray(w_down)[0],
    }
    outs = {"y": (TOK, D), "tails": (P, HEADS, 22), "gdn_prompt": (HEADS, P, P), "gdn_sample": (HEADS, P, P)}
    nc = bacc.Bacc("TRN2", target_bir_lowering=False, num_devices=1)
    feeds, A, O = {}, {}, {}
    for name, a in arrays.items():
        feeds["in_" + name] = a = np.ascontiguousarray(a)
        A[name] = nc.dram_tensor("in_" + name, a.shape, mybir.dt.from_np(a.dtype), kind="ExternalInput").ap()
    for name, shape in outs.items():
        O[name] = nc.dram_tensor("out_" + name, shape, F32, kind="ExternalOutput").ap()
    encoder_layer(nc, A, O)
    r = run_bass_kernel_spmd(nc, [feeds], core_ids=[0]).results[0]
    y, tails = r["out_y"], r["out_tails"]

    def last_rows(columns, kinds, count):
        t = tails[:, :, columns].reshape(P, HEADS, kinds, count).transpose(3, 2, 1, 0)
        return np.ascontiguousarray(t.reshape(1, 1, count, kinds * HEADS * P))

    return (y[None, :PROMPT], y[None, PROMPT:], last_rows(slice(18, 20), 1, 2), last_rows(slice(0, 9), 3, 3),
            r["out_gdn_prompt"][None, None], last_rows(slice(20, 22), 1, 2), last_rows(slice(9, 18), 3, 3),
            r["out_gdn_sample"][None, None])
```

```python
from contextlib import ExitStack

import numpy as np

import concourse.bass as bass
from concourse import mybir

F32 = mybir.dt.float32
F32R = mybir.dt.float32r
I32 = mybir.dt.int32
ALU = mybir.AluOpType
ACT = mybir.ActivationFunctionType
X = mybir.AxisListType.X

P = 128
D = 1024
KC = D // P
PROMPT, STREAM = 512, 64
TOK = PROMPT + STREAM
HALF = TOK // 2
UNITS = 5
UW = UNITS * P
HEADS = 8
EPS = 1e-6
LEVELS = 6
GROUPS, PER_GROUP = 4, 8
EXPERTS = GROUPS * PER_GROUP
DE = 256
SLOTS = 2 * TOK
BR = 96
OVER = (SLOTS - 2) // BR
BLOCKS = EXPERTS + OVER
ROWS = SLOTS + BR
TB_FIRST, TB_EXPERT, TB_ROW, TB_COUNT = 0, EXPERTS, EXPERTS + OVER, EXPERTS + 2 * OVER

TQ, TK, TV, TZ, TGA, TGB, TH, TC, TB = range(9)
TILES = 9
PER = 3
POS = 2 * TILES * PER
ACT_HALVES = 2 * TC
DVE_HALVES = 2 * TILES - ACT_HALVES

PAR_QKV, PAR_A, PAR_CQKV, PAR_CA, PARS = 0, 12, 15, 24, 26
KBETA, KSUM, KEXP, KBEXP, KREST, KLAST, KINDS = range(7)
BETAS_AT, SUMS_AT = 8, 24
DECAY_AT = {12: 0, 27: 1}
DEC_STEPS, DEC_ACTS = 11, 7
R_PAIRS, R_GAP, R_PLACES, ROUTE_STEPS = 23, 25, 31, 63
C_ID, C_UPPER, C_LOWER, C_ONES, C_BEFORE, C_LEVEL = (P * k for k in range(6))
C_MISC = C_LEVEL + P * (LEVELS + 1)
M_VALID, M_ALOG, M_DT, M_RBIAS, M_IOTA, M_END = 0, 5, 13, 21, 57, 57 + 40
CONSTS = C_MISC + M_END


def wait(engine, sem, value):
    if not isinstance(value, int) or value > 0:
        engine.wait_ge(sem, value)


def at(index, length=1):
    return bass.ds(index, length)


PIECES = [[(0, HALF, 0, False)], [(0, PROMPT - HALF, HALF, False), (PROMPT - HALF, STREAM, 0, True)]]


def padded(first, stream, pad):
    return first + (PROMPT + 2 * pad if stream else pad)


def encoder_layer(nc, A, O):
    scr_gate = nc.dram_tensor("scr_gate", (HEADS, 2, P, TOK), F32, kind="Internal").ap()
    scr_x2 = nc.dram_tensor("scr_x2", (UNITS * P, D), F32, kind="Internal").ap()
    scr_rows = nc.dram_tensor("scr_rows", (ROWS, D), F32, kind="Internal").ap()
    scr_y = nc.dram_tensor("scr_y", (BLOCKS * BR, D), F32, kind="Internal").ap()

    top = ExitStack()
    with top:
        def sem(name):
            return top.enter_context(nc.semaphore(name))

        def sb(ctx, name, shape, dt=F32):
            return ctx.enter_context(nc.sbuf_tensor(name, shape, dt))

        proj = [top.enter_context(nc.psum_tensor(f"proj{k}", [P, 512], F32)) for k in range(3)]
        wideA = top.enter_context(nc.psum_tensor("wideA", [P, 1024], F32))
        wideB = top.enter_context(nc.psum_tensor("wideB", [P, 1024], F32))
        small = top.enter_context(nc.psum_tensor("small", [P, 512], F32))

        const = sb(top, "const", [P, CONSTS])
        ident = const[:, C_ID:C_ID + P]
        upper = const[:, C_UPPER:C_UPPER + P]
        ones = const[:, C_ONES:C_ONES + P]
        before = const[:, C_BEFORE:C_BEFORE + P]

        def level_mask(k):
            c = C_LEVEL + P * k
            return const[:, c:c + P].unsqueeze(1).to_broadcast([P, UNITS, P])

        lower_mask = const[:, C_LOWER:C_LOWER + P].unsqueeze(1).to_broadcast([P, UNITS, P])
        misc = const[:, C_MISC:CONSTS]
        small_sb = sb(top, "stats", [P, 64])
        epsq = small_sb[:, 60:62]
        coef = sb(top, "coef", [P, 2, UNITS])
        slot_row = sb(top, "slot_row", [P, 2 * UNITS], I32)
        slot_y = sb(top, "slot_y", [P, 2 * UNITS], I32)
        table = sb(top, "block_table", [1, TB_COUNT + 1], I32)

        ph1 = ExitStack()
        xnh = sb(ph1, "xnh", [P, KC, UW], F32R)
        xnl = sb(ph1, "xnl", [P, KC, UW], F32R)
        wraw = [sb(ph1, f"wraw{k}", [P, KC, P]) for k in range(3)]
        whi = [sb(ph1, f"whi{k}", [P, KC, P], F32R) for k in range(3)]
        wlo = [sb(ph1, f"wlo{k}", [P, KC, P], F32R) for k in range(3)]
        g0 = ExitStack()
        xin = [sb(g0, f"xin{c}", [P, D]) for c in range(UNITS)]
        sqx = sb(g0, "sqx", [P, D])
        w16 = sb(g0, "w16", [P, KC, 16])
        w16h = sb(g0, "w16h", [P, KC, 16], F32R)
        w16l = sb(g0, "w16l", [P, KC, 16], F32R)
        zero = sb(g0, "zero", [P, D])
        g0.close()
        yab = ExitStack()
        ya = sb(yab, "ya", [P, HEADS, TOK])
        yb = sb(yab, "yb", [P, HEADS, TOK])
        gd = ExitStack()
        raw = sb(gd, "raw", [P, 3, TOK + 6])
        ubuf = sb(gd, "ubuf", [P, TOK + 4])
        aout = sb(gd, "aout", [P, TOK + 2])
        cout = [sb(gd, f"cout{k}", [P, TOK + 3]) for k in range(2)]
        sil = sb(gd, "sil", [P, 3, UW])
        gate = [sb(gd, f"gate{k}", [P, TOK]) for k in range(2)]
        par = sb(gd, "par", [P, HEADS, PARS])
        pcur = sb(gd, "pcur", [P, PAR_CQKV])
        dec = sb(gd, "dec", [P, HEADS, KINDS, UNITS])
        gcur = sb(gd, "gcur", [P, KINDS, UNITS])
        onorm = sb(gd, "onorm", [P, 1])
        tails = sb(gd, "tails", [P, HEADS, 22])
        buf1 = sb(gd, "buf1", [P, 2 * UW])
        buf2 = sb(gd, "buf2", [P, 2 * UW])
        buf3 = sb(gd, "buf3", [P, 2 * UW])
        vbeta = sb(gd, "vbeta", [P, UW])
        kbexp = sb(gd, "kbexp", [P, UW])
        krest = sb(gd, "krest", [P, UW])
        kT = sb(gd, "kT", [P, UW])
        qT = sb(gd, "qT", [P, UW])
        T = sb(gd, "T", [P, UW])
        TT = sb(gd, "TT", [P, UW])
        vn = sb(gd, "vn", [P, UW])
        Sp = sb(gd, "Sp", [P, P])
        Ss = sb(gd, "Ss", [P, P])
        st = sb(gd, "st", [P, 40])
        dtmp = sb(gd, "dtmp", [P, 8, UNITS * HEADS])
        basb = sb(gd, "basb", [P, UNITS, 16])
        gd.close()
        g1 = ExitStack()
        g1row = sb(g1, "g1row", [P, D])
        g1.close()

        g2 = ExitStack()
        ybh = sb(g2, "ybh", [P, KC, TOK], F32R)
        ybl = sb(g2, "ybl", [P, KC, TOK], F32R)
        tg = [sb(g2, f"tg{k}", [P, TOK]) for k in range(2)]
        mix = [sb(g2, f"mix{k}", [P, TOK]) for k in range(2)]
        g2.close()
        yab.close()
        m_ctx = ExitStack()
        mh = sb(m_ctx, "mh", [P, KC, TOK], F32R)
        ml = sb(m_ctx, "ml", [P, KC, TOK], F32R)
        x2 = sb(m_ctx, "x2", [P, UNITS, D])
        oT = [sb(m_ctx, f"oT{k}", [P, UW]) for k in range(2)]
        m_ctx.close()
        ewt = ExitStack()
        sb(ewt, "below_weights", [P, 2 * KC * TOK + UNITS * D + 2 * UW])
        eraw = [None, sb(ewt, "eraw1", [P, 24 * DE])]
        eraw[0] = sb(ewt, "eraw0", [P, 24 * DE])
        hgate = [sb(ewt, f"hgate{k}", [P, DE]) for k in range(2)]
        hid = [sb(ewt, f"hid{k}", [P, DE]) for k in range(2)]
        hth = [sb(ewt, f"hth{k}", [P, 2, BR], F32R) for k in range(2)]
        htl = [sb(ewt, f"htl{k}", [P, 2, BR], F32R) for k in range(2)]
        ewt.close()
        ph1.close()
        p3 = ExitStack()
        tn = sb(p3, "tn", [P, UNITS, D])
        g2row = sb(p3, "g2row", [P, D])
        wr = sb(p3, "wr", [P, KC, GROUPS + EXPERTS])
        tT = [sb(p3, f"tT{k}", [P, D]) for k in range(2)]
        sqs = sb(p3, "sqs", [P, D])
        lg = sb(p3, "lg", [P, UNITS, GROUPS + EXPERTS])
        r4 = [sb(p3, f"r4_{k}", [P, UNITS, GROUPS]) for k in range(4)]
        r8 = [sb(p3, f"r8_{k}", [P, UNITS, PER_GROUP]) for k in range(5)]
        r5 = sb(p3, "r5", [P, 12, UNITS])
        pair = sb(p3, "pair", [P, 2, UNITS, EXPERTS])
        pick = sb(p3, "pick", [P, 2, UNITS, EXPERTS])
        r32 = [sb(p3, f"r32_{k}", [P, UNITS, EXPERTS]) for k in range(3)]
        ex = sb(p3, "ex", [P, 6, EXPERTS])
        bt = sb(p3, "bt", [P, 3, OVER, EXPERTS])
        brow = sb(p3, "brow", [P, 3, OVER])
        ehi, elo = [None, None], [None, None]
        ehi[0] = sb(p3, "ehi0", [P, 24 * DE], F32R)
        elo[0] = sb(p3, "elo0", [P, 24 * DE], F32R)
        xb = [sb(p3, f"xb{k}", [P, D]) for k in range(2)]
        xbh = [sb(p3, f"xbh{k}", [P, KC, BR], F32R) for k in range(2)]
        xbl = [sb(p3, f"xbl{k}", [P, KC, BR], F32R) for k in range(2)]
        yout = [sb(p3, f"yout{k}", [P, D]) for k in range(2)]
        p3.close()
        p4 = ExitStack()
        ehi[1] = sb(p4, "ehi1", [P, 24 * DE], F32R)
        elo[1] = sb(p4, "elo1", [P, 24 * DE], F32R)
        p4.close()
        p5 = ExitStack()
        fy = [[sb(p5, f"fy{j}_{c}", [P, D]) for c in range(UNITS)] for j in range(2)]
        fsq = sb(p5, "fsq", [P, D])
        fgrow = sb(p5, "fgrow", [P, D])
        sb(p5, "below_x", [P, 2 * KC * UW + 9 * D + 2 * KC * TOK + UNITS * D + 2 * UW - 12 * D])
        fx = [sb(p5, f"fx{c}", [P, D]) for c in range(UNITS)]
        p5.close()

        const_in, g1_in = sem("const_in"), sem("g1_in")
        par_in = sem("par_in")
        x_in = [sem(f"x_in{c}") for c in range(UNITS)]
        zeroed = sem("zeroed")
        x_square, x_root, x_recip, x_scaled = (sem(f"x_{s}") for s in ("square", "root", "recip", "scaled"))
        x_turned, x_high, x_low = (sem(f"x_{s}") for s in ("turned", "high", "low"))
        ba_w, ba_done, ba_out = sem("ba_w"), sem("ba_done"), sem("ba_out")
        dec_act, dec_dve, dec_pe = sem("dec_act"), sem("dec_dve"), sem("dec_pe")
        w_in = [sem(f"w_in{k}") for k in range(3)]
        w_high, w_low = sem("w_high"), sem("w_low")
        proj_done = sem("proj_done")
        act_half, dve_half = sem("act_half"), sem("dve_half")
        conv_step, conv_silu = sem("conv_step"), sem("conv_silu")
        gate_out = sem("gate_out")
        a_step = sem("a_step")
        pars_set, tail_kept, gdec_set = sem("pars_set"), sem("tail_kept"), sem("gdec_set")
        names = """qk_turned v_turned sums_spread hats_turned grams a_turned t_turned0 at_done tat_done
            t_turned uw_done ws_done kv_done o_turned
            qk_raw qk_square qk_root decay hats_T a_T tt0 tt_set w_set o_inter o_square o_root
            qk_sum qk_recip hats v_scaled dgap dclip decay_cut a_cut a_scaled t_cut t_set0 x_set t_set u_set
            vn_set s_set o_set o_sum o_recip o_scaled yb_set
            kbexp_set krest_set s_zero s_in s_out""".split()
        s = {n: sem(n) for n in names}
        tails_out = sem("tails_out")

        U = [slice(u * P, (u + 1) * P) for u in range(UNITS)]
        scan0 = 20 + 3 * LEVELS

        def spread(kind):
            return gcur[:, kind, :].unsqueeze(2).to_broadcast([P, UNITS, P])

        def units(ap):
            return ap.rearrange("p (u m) -> p u m", m=P)

        def gdn_tensor(pe, p, g):
            n = g + 1
            if p == 0:
                pe.wait_ge(conv_silu, 3 * g + 2)
                wait(pe, s["yb_set"], g)
                wait(pe, s["o_set"], g)
                for u in range(UNITS):
                    pe.transpose(wideA[:, U[u]], sil[:, 0, U[u]], ident)
                for u in range(UNITS):
                    mm = pe.transpose(wideB[:, U[u]], sil[:, 1, U[u]], ident)
                mm.then_inc(s["qk_turned"], 1)
            if p == 2:
                pe.wait_ge(conv_silu, 3 * g + 3)
                pe.wait_ge(s["qk_raw"], n)
                for u in range(UNITS):
                    mm = pe.transpose(wideA[:, U[u]], sil[:, 2, U[u]], ident)
                mm.then_inc(s["v_turned"], 1)
            if p == 4:
                pe.wait_ge(s["v_scaled"], n)
                pe.wait_ge(gdec_set, n)
                for u in range(UNITS):
                    mm = pe.transpose(wideA[:, U[u]], gcur[:, KSUM, u:u + 1].to_broadcast([P, P]), ident)
                mm.then_inc(s["sums_spread"], 1)
            if p == 8:
                pe.wait_ge(s["hats"], n)
                pe.wait_ge(s["dgap"], n)
                for u in range(UNITS):
                    pe.transpose(wideA[:, U[u]], buf3[:, u * P:(u + 1) * P], ident)
                for u in range(UNITS):
                    mm = pe.transpose(wideB[:, U[u]], buf3[:, UW + u * P:UW + (u + 1) * P], ident)
                mm.then_inc(s["hats_turned"], 1)
            if p == 11:
                pe.wait_ge(s["hats_T"], n)
                for u in range(UNITS):
                    pe.matmul(wideA[:, U[u]], qT[:, U[u]], kT[:, U[u]], start=True, stop=True)
                for u in range(UNITS):
                    mm = pe.matmul(wideB[:, U[u]], kT[:, U[u]], kT[:, U[u]], start=True, stop=True)
                mm.then_inc(s["grams"], 1)
            if p == 15:
                pe.wait_ge(s["a_scaled"], n)
                for u in range(UNITS):
                    pe.transpose(wideA[:, U[u]], buf1[:, u * P:(u + 1) * P], ident)
                for u in range(UNITS):
                    mm = pe.transpose(wideB[:, U[u]], buf1[:, UW + u * P:UW + (u + 1) * P], ident)
                mm.then_inc(s["a_turned"], 1)
            if p == 17:
                pe.wait_ge(s["t_set0"], n)
                pe.wait_ge(s["a_T"], n)
                for u in range(UNITS):
                    mm = pe.transpose(wideA[:, U[u]], T[:, U[u]], ident)
                mm.then_inc(s["t_turned0"], 1)
            if 19 <= p < 19 + 3 * LEVELS:
                k, step = divmod(p - 19, 3)
                done = g * LEVELS + k
                if step == 0:
                    if k > 0:
                        pe.wait_ge(s["tt_set"], done)
                    for u in range(UNITS):
                        mm = pe.matmul(wideB[:, U[u]], buf3[:, UW + u * P:UW + (u + 1) * P], T[:, U[u]],
                                       start=True, stop=True)
                    mm.then_inc(s["at_done"], 1)
                elif step == 1:
                    pe.wait_ge(s["x_set"], done + 1)
                    if k == 0:
                        pe.wait_ge(s["tt0"], n)
                    for u in range(UNITS):
                        mm = pe.matmul(wideA[:, U[u]], TT[:, U[u]], buf2[:, UW + u * P:UW + (u + 1) * P],
                                       start=True, stop=True)
                    mm.then_inc(s["tat_done"], 1)
                else:
                    pe.wait_ge(s["t_set"], done + 1)
                    for u in range(UNITS):
                        mm = pe.transpose(wideB[:, U[u]], T[:, U[u]], ident)
                    mm.then_inc(s["t_turned"], 1)
            if p == scan0 - 1:
                pe.wait_ge(s["tt_set"], LEVELS * n)
                pe.wait_ge(s["kbexp_set"], n)
                for u in range(UNITS):
                    pe.matmul(wideA[:, U[u]], TT[:, U[u]], vbeta[:, U[u]], start=True, stop=True)
                for u in range(UNITS):
                    mm = pe.matmul(wideB[:, U[u]], kbexp[:, U[u]], TT[:, U[u]], start=True, stop=True)
                mm.then_inc(s["uw_done"], 1)
            if scan0 + 1 <= p < scan0 + 9:
                c, step = divmod(p - scan0 - 1, 2)
                if step == 0:
                    if c == 0:
                        pe.wait_ge(s["w_set"], n)
                        pe.wait_ge(s["s_zero"], n)
                        pe.wait_ge(s["s_in"], 16 * n)
                        wait(pe, s["o_inter"], 4 * g)
                    else:
                        pe.wait_ge(s["s_set"], 4 * g + c)
                        pe.wait_ge(s["o_inter"], 4 * g + c)
                    mm = None
                    for u, state, o in [(c, Sp, 0)] + ([(4, Ss, 2 * P)] if c == 0 else []):
                        pe.matmul(small[:, o:o + P], buf1[:, UW + u * P:UW + (u + 1) * P], state[:, :],
                                  start=True, stop=True)
                        mm = pe.matmul(small[:, o + P:o + 2 * P], qT[:, U[u]], state[:, :], start=True, stop=True)
                    mm.then_inc(s["ws_done"], 1)
                else:
                    pe.wait_ge(s["vn_set"], 4 * g + c + 1)
                    pe.wait_ge(s["krest_set"], n)
                    for u, o in [(c, 0)] + ([(4, P)] if c == 0 else []):
                        pe.matmul(wideB[:, U[u]], buf3[:, u * P:(u + 1) * P], vn[:, U[u]], start=True, stop=True)
                        mm = pe.matmul(wideA[:, o:o + P], krest[:, U[u]], vn[:, U[u]], start=True, stop=True)
                    mm.then_inc(s["kv_done"], 1)
            if p == 52:
                pe.wait_ge(s["o_scaled"], n)
                for u in range(UNITS):
                    mm = pe.transpose(wideA[:, U[u]], vn[:, U[u]], ident)
                mm.then_inc(s["o_turned"], 1)

        def gdn_scalar(act, p, g):
            n = g + 1
            if p == 0:
                act.wait_ge(s["qk_turned"], n)
                wait(act, s["uw_done"], g)
                wait(act, s["kv_done"], 4 * g)
                act.activation(buf1[:, 0:UW], wideA[:, 0:UW], ACT.Copy)
                act.activation(buf1[:, UW:2 * UW], wideB[:, 0:UW], ACT.Copy).then_inc(s["qk_raw"], 1)
                wait(act, s["o_sum"], g)
                act.wait_ge(s["qk_raw"], n)
                act.activation(buf2[:, :], buf1[:, :], ACT.Square).then_inc(s["qk_square"], 1)
            if p == 3:
                act.wait_ge(s["qk_sum"], n)
                act.activation(st[:, 10:15], st[:, 0:5], ACT.Sqrt, scale=float(P), bias=epsq[:, 0:1])
                act.activation(st[:, 15:20], st[:, 5:10], ACT.Sqrt, bias=epsq[:, 1:2]).then_inc(s["qk_root"], 1)
            if p == 6:
                act.wait_ge(s["dclip"], n)
                act.activation(buf2[:, 0:UW], buf2[:, 0:UW], ACT.Exp, scale=-1.0).then_inc(s["decay"], 1)
            if p == 8:
                act.wait_ge(s["hats_turned"], n)
                act.activation(qT[:, :], wideA[:, 0:UW], ACT.Copy)
                act.activation(kT[:, :], wideB[:, 0:UW], ACT.Copy).then_inc(s["hats_T"], 1)
            if p == 15:
                act.wait_ge(s["a_turned"], n)
                act.wait_ge(s["krest_set"], n)
                act.activation(buf3[:, 0:UW], wideA[:, 0:UW], ACT.Copy)
                act.activation(buf3[:, UW:2 * UW], wideB[:, 0:UW], ACT.Copy).then_inc(s["a_T"], 1)
            if p == 17:
                act.wait_ge(s["t_turned0"], n)
                act.activation(TT[:, :], wideA[:, 0:UW], ACT.Copy).then_inc(s["tt0"], 1)
            if 19 <= p < 19 + 3 * LEVELS and (p - 19) % 3 == 2:
                k = (p - 19) // 3
                act.wait_ge(s["t_turned"], g * LEVELS + k + 1)
                act.activation(TT[:, :], wideB[:, 0:UW], ACT.Copy).then_inc(s["tt_set"], 1)
            if p == scan0 - 1:
                act.wait_ge(s["uw_done"], n)
                act.activation(buf1[:, UW:2 * UW], wideB[:, 0:UW], ACT.Copy).then_inc(s["w_set"], 1)
            if scan0 + 1 <= p < scan0 + 9 and (p - scan0 - 1) % 2 == 0:
                c = (p - scan0 - 1) // 2
                act.wait_ge(s["ws_done"], 4 * g + c + 1)
                act.wait_ge(s["vn_set"], 4 * g + c + 1)
                if c == 0:
                    act.activation(kT[:, U[4]], small[:, 3 * P:4 * P], ACT.Copy, scale=gcur[:, KEXP, 4:5])
                act.activation(kT[:, U[c]], small[:, P:2 * P], ACT.Copy, scale=gcur[:, KEXP, c:c + 1])\
                   .then_inc(s["o_inter"], 1)
            if p == 47:
                act.wait_ge(s["o_set"], n)
                act.activation(buf2[:, 0:UW], vn[:, :], ACT.Square).then_inc(s["o_square"], 1)
            if p == 48:
                act.wait_ge(s["s_set"], 4 * n)
                for name, state in (("gdn_prompt", Sp), ("gdn_sample", Ss)):
                    act.dma_start(O[name][at(g), :, :].rearrange("a k v -> (a k) v"), state[:, :])\
                       .then_inc(s["s_out"], 16)
            if p == 49:
                act.wait_ge(s["o_sum"], n)
                act.activation(st[:, 35:40], st[:, 30:35], ACT.Sqrt, scale=1.0 / P, bias=epsq[:, 1:2])\
                   .then_inc(s["o_root"], 1)

        def gdn_vector(dve, p, g):
            n = g + 1
            if p == 2:
                dve.wait_ge(s["qk_square"], n)
                dve.tensor_reduce(st[:, 0:10], buf2[:, :].rearrange("p (u m) -> p u m", m=P), X, ALU.add)\
                   .then_inc(s["qk_sum"], 1)
                dve.wait_ge(s["v_turned"], n)
                dve.wait_ge(gdec_set, n)
                dve.tensor_tensor(units(vbeta[:, :]), units(wideA[:, 0:UW]), spread(KBETA), ALU.mult)\
                   .then_inc(s["v_scaled"], 1)
            if p == 4:
                dve.wait_ge(s["qk_root"], n)
                dve.reciprocal(st[:, 20:30], st[:, 10:20]).then_inc(s["qk_recip"], 1)
                dve.wait_ge(s["qk_recip"], n)
                dve.tensor_tensor(units(buf3[:, :]), units(buf1[:, :]),
                                  st[:, 20:30].unsqueeze(2).to_broadcast([P, 2 * UNITS, P]), ALU.mult)\
                   .then_inc(s["hats"], 1)
            if p == 5:
                dve.wait_ge(s["sums_spread"], n)
                dve.tensor_tensor(units(buf2[:, 0:UW]), units(wideA[:, 0:UW]), spread(KSUM), ALU.subtract)\
                   .then_inc(s["dgap"], 1)
                dve.wait_ge(s["dgap"], n)
                dve.tensor_scalar(buf2[:, 0:UW], buf2[:, 0:UW], 0.0, None, ALU.max).then_inc(s["dclip"], 1)
            if p == 7:
                dve.wait_ge(s["decay"], n)
                dve.tensor_tensor(units(buf2[:, 0:UW]), units(buf2[:, 0:UW]), lower_mask, ALU.mult)\
                   .then_inc(s["decay_cut"], 1)
            if p == 11:
                dve.wait_ge(s["grams"], n)
                dve.wait_ge(s["decay_cut"], n)
                dve.tensor_tensor(buf1[:, UW:2 * UW], wideB[:, 0:UW], buf2[:, 0:UW], ALU.mult)\
                   .then_inc(s["a_cut"], 1)
                dve.tensor_tensor(buf1[:, 0:UW], wideA[:, 0:UW], buf2[:, 0:UW], ALU.mult)
                dve.wait_ge(s["a_cut"], n)
                dve.tensor_tensor(units(buf1[:, UW:2 * UW]), units(buf1[:, UW:2 * UW]), spread(KBETA), ALU.mult)\
                   .then_inc(s["a_scaled"], 1)
            if p == 13:
                dve.wait_ge(s["a_scaled"], n)
                dve.tensor_tensor(units(T[:, :]), units(buf1[:, UW:2 * UW]), level_mask(0), ALU.mult)\
                   .then_inc(s["t_cut"], 1)
                dve.wait_ge(s["t_cut"], n)
                dve.tensor_tensor(units(T[:, :]), units(T[:, :]),
                                  ident.unsqueeze(1).to_broadcast([P, UNITS, P]), ALU.add).then_inc(s["t_set0"], 1)
            if 19 <= p < 19 + 3 * LEVELS:
                k, step = divmod(p - 19, 3)
                done = g * LEVELS + k
                if step == 0:
                    dve.wait_ge(s["at_done"], done + 1)
                    dve.tensor_tensor(units(buf2[:, UW:2 * UW]), units(wideB[:, 0:UW]), level_mask(k + 1),
                                      ALU.mult).then_inc(s["x_set"], 1)
                elif step == 1:
                    dve.wait_ge(s["tat_done"], done + 1)
                    dve.tensor_tensor(T[:, :], T[:, :], wideA[:, 0:UW], ALU.add).then_inc(s["t_set"], 1)
            if p == scan0 - 1:
                dve.wait_ge(s["uw_done"], n)
                dve.tensor_copy(buf1[:, 0:UW], wideA[:, 0:UW]).then_inc(s["u_set"], 1)
            if scan0 + 1 <= p < scan0 + 9:
                c, step = divmod(p - scan0 - 1, 2)
                if step == 0:
                    dve.wait_ge(s["ws_done"], 4 * g + c + 1)
                    if c == 0:
                        dve.wait_ge(s["u_set"], n)
                        dve.tensor_tensor(vn[:, U[4]], buf1[:, 4 * P:5 * P], small[:, 2 * P:3 * P], ALU.subtract)
                    dve.tensor_tensor(vn[:, U[c]], buf1[:, c * P:(c + 1) * P], small[:, 0:P], ALU.subtract)\
                       .then_inc(s["vn_set"], 1)
                else:
                    dve.wait_ge(s["kv_done"], 4 * g + c + 1)
                    if c == 0:
                        dve.scalar_tensor_tensor(Ss[:, :], Ss[:, :], gcur[:, KLAST, 4:5], wideA[:, P:2 * P],
                                                 ALU.mult, ALU.add)
                    dve.scalar_tensor_tensor(Sp[:, :], Sp[:, :], gcur[:, KLAST, c:c + 1], wideA[:, 0:P],
                                             ALU.mult, ALU.add).then_inc(s["s_set"], 1)
                    if c == 3:
                        dve.wait_ge(s["o_inter"], 4 * n)
                        dve.tensor_tensor(vn[:, :], kT[:, :], wideB[:, 0:UW], ALU.add).then_inc(s["o_set"], 1)
            if p == 48:
                dve.wait_ge(s["o_square"], n)
                dve.tensor_reduce(st[:, 30:35], units(buf2[:, 0:UW]), X, ALU.add).then_inc(s["o_sum"], 1)
            if p == 50:
                dve.wait_ge(s["o_root"], n)
                dve.reciprocal(st[:, 20:25], st[:, 35:40]).then_inc(s["o_recip"], 1)
                dve.wait_ge(s["o_recip"], n)
                dve.tensor_tensor(units(vn[:, :]), units(vn[:, :]),
                                  st[:, 20:25].unsqueeze(2).to_broadcast([P, UNITS, P]), ALU.mult)\
                   .then_inc(s["o_scaled"], 1)
            if p == 53:
                dve.wait_ge(s["o_turned"], n)
                dve.wait_ge(act_half, ACT_HALVES * g + 2 * TZ + 2)
                head = yb[:, at(g), :].rearrange("p a m -> p (a m)")
                dve.scalar_tensor_tensor(head, wideA[:, 0:TOK], onorm[:, 0:1], head, ALU.mult, ALU.mult)\
                   .then_inc(s["yb_set"], 1)

        def gdn_pool(pool, g):
            n = g + 1
            wait(pool, s["yb_set"], g)
            pool.tensor_copy(gcur[:, :, :], dec[:, at(g), :, :].rearrange("p a k u -> p (a k) u"))\
                .then_inc(gdec_set, 1)
            pool.wait_ge(gdec_set, n)
            pool.wait_ge(s["hats"], n)
            pool.tensor_tensor(units(kbexp[:, :]), units(buf3[:, UW:2 * UW]), spread(KBEXP), ALU.mult)\
                .then_inc(s["kbexp_set"], 1)
            wait(pool, s["s_out"], 32 * g)
            pool.tensor_tensor(units(krest[:, :]), units(buf3[:, UW:2 * UW]), spread(KREST), ALU.mult)\
                .then_inc(s["krest_set"], 1)
            pool.memset(Sp[:, :], 0.0).then_inc(s["s_zero"], 1)
            pool.dma_start(Ss[:, :], A["state"][at(g), :, :].rearrange("a k v -> (a k) v")).then_inc(s["s_in"], 16)

        def half_read(h, i):
            if not isinstance(h, int):
                raise TypeError
            if h < 0:
                h, i = h + 2 * TILES, i - 1
            if isinstance(i, int) and i < 0:
                return act_half, 0
            if h < ACT_HALVES:
                return act_half, ACT_HALVES * i + h + 1
            return dve_half, DVE_HALVES * i + h - ACT_HALVES + 1

        def proj_tensor(pe, p, i):
            h, part = divmod(p, PER)
            t, hh = divmod(h, 2)
            if part == 0:
                if hh == 0:
                    pe.wait_ge(w_low, TILES * i + t + 1)
                if isinstance(i, int) and i == 0 and h < 2:
                    pe.wait_ge(x_low, (3, UNITS)[h])
                wait(pe, *half_read(h - 3, i))
            out = proj[h % 3][:, 0:HALF]
            for j in range(8 * part, 8 * part + 8):
                kc, term = divmod(j, 3)
                w = (whi, whi, wlo)[term][t % 3]
                x = (xnh, xnl, xnh)[term]
                mm = pe.matmul(out, w[:, kc, :], x[:, kc, hh * HALF:(hh + 1) * HALF], start=(j == 0), stop=(j == 23))
            if part == PER - 1:
                mm.then_inc(proj_done, 1)

        def split_high(act, i, t):
            act.wait_ge(w_in[t % 3], 16 * (3 * i + t // 3 + 1))
            wait(act, proj_done, 2 * TILES * i + 2 * (t - 2))
            act.activation(whi[t % 3][:, :, :], wraw[t % 3][:, :, :], ACT.Copy).then_inc(w_high, 1)

        def split_low(dve, i, t):
            dve.wait_ge(w_high, TILES * i + t + 1)
            dve.tensor_tensor(wlo[t % 3][:, :, :], wraw[t % 3][:, :, :], whi[t % 3][:, :, :].bitcast(F32),
                              ALU.subtract).then_inc(w_low, 1)

        CONV_AT = {7 + k: (0, k) for k in range(4)} | {13 + k: (1, k) for k in range(4)} | {19 + k: (2, k) for k in range(4)}
        A_AT = {48: 0, 49: 1, 50: 2}

        def proj_scalar(act, p, i, last=False):
            h, part = divmod(p, PER)
            t, hh = divmod(h, 2)
            if part == 0 and hh == 0 and not (last and t + 2 >= TILES):
                split_high(act, i, t + 2)
            if part == PER - 1 and t < TC:
                act.wait_ge(proj_done, 2 * TILES * i + h + 1)
                src = proj[h % 3]
                if t in (TQ, TK, TV):
                    wait(act, conv_step, 12 * (i - 1) + 4 * (t - TQ) + 4)
                    wait(act, tail_kept, 2 * (i - 1) + 1)
                    for lo, count, first, stream in PIECES[hh]:
                        c = padded(first, stream, 3)
                        ins = act.activation(raw[:, t - TQ, c:c + count], src[:, lo:lo + count], ACT.Copy)
                elif t == TZ:
                    ins = act.activation(yb[:, at(i), hh * HALF:(hh + 1) * HALF].rearrange("p a m -> p (a m)"),
                                         src[:, 0:HALF], ACT.Silu)
                elif t in (TGA, TGB):
                    wait(act, gate_out, 32 * i)
                    ins = act.activation(gate[t - TGA][:, hh * HALF:(hh + 1) * HALF], src[:, 0:HALF], ACT.Tanh,
                                         scale=0.5)
                else:
                    wait(act, tail_kept, 2 * i)
                    wait(act, a_step, 3 * i)
                    for lo, count, first, stream in PIECES[hh]:
                        c = padded(first, stream, 2)
                        ins = act.activation(ubuf[:, c:c + count], src[:, lo:lo + count], ACT.Copy)
                ins.then_inc(act_half, 1)
                if t in (TGA, TGB) and hh == 1:
                    act.wait_ge(act_half, ACT_HALVES * i + 2 * t + 2)
                    act.dma_start(scr_gate[at(i), t - TGA, :, :].rearrange("a p m -> (a p) m"),
                                  gate[t - TGA][:, :]).then_inc(gate_out, 16)
            if p in (11, 17, 23):
                k = (p - 11) // 6
                act.wait_ge(conv_step, 12 * i + 4 * k + 4)
                if k < 2:
                    wait(act, s["qk_turned"], i)
                else:
                    wait(act, s["v_turned"], i)
                act.activation(sil[:, k, 0:PROMPT], cout[k % 2][:, 0:PROMPT], ACT.Silu)
                act.activation(sil[:, k, PROMPT:TOK], cout[k % 2][:, PROMPT + 3:TOK + 3], ACT.Silu)\
                   .then_inc(conv_silu, 1)

        def proj_vector(dve, p, i, last=False):
            h, part = divmod(p, PER)
            t, hh = divmod(h, 2)
            if part == 0 and hh == 0 and not (last and t + 2 >= TILES):
                split_low(dve, i, t + 2)
            if p in CONV_AT:
                k, j = CONV_AT[p]
                n = 12 * i + 4 * k + j
                y = cout[k % 2][:, :]
                if j == 0:
                    dve.wait_ge(act_half, ACT_HALVES * i + 2 * k + 2)
                    dve.wait_ge(pars_set, i + 1)
                    wait(dve, conv_silu, 3 * i + k - 1 if k == 2 else 3 * (i - 1) + (3 if k == 0 else 2))
                    dve.tensor_scalar(y, raw[:, k, 0:TOK + 3], pcur[:, 4 * k:4 * k + 1], None, ALU.mult)\
                       .then_inc(conv_step, 1)
                else:
                    dve.wait_ge(conv_step, n)
                    dve.scalar_tensor_tensor(y, raw[:, k, j:j + TOK + 3], pcur[:, 4 * k + j:4 * k + j + 1], y,
                                             ALU.mult, ALU.add).then_inc(conv_step, 1)
            if p in A_AT:
                j = A_AT[p]
                if j == 0:
                    dve.wait_ge(dve_half, DVE_HALVES * i + 2)
                    dve.tensor_scalar(aout[:, :], ubuf[:, 0:TOK + 2], pcur[:, PAR_A:PAR_A + 1], None, ALU.mult)\
                       .then_inc(a_step, 1)
                else:
                    dve.wait_ge(a_step, 3 * i + j)
                    dve.scalar_tensor_tensor(aout[:, :], ubuf[:, j:j + TOK + 2], pcur[:, PAR_A + j:PAR_A + j + 1],
                                             aout[:, :], ALU.mult, ALU.add).then_inc(a_step, 1)
            if part == PER - 1 and t >= TC:
                dve.wait_ge(proj_done, 2 * TILES * i + h + 1)
                src = proj[h % 3]
                if t == TC:
                    dve.wait_ge(act_half, ACT_HALVES * i + 2 * TH + hh + 1)
                else:
                    dve.wait_ge(a_step, 3 * i + 3)
                for lo, count, first, stream in PIECES[hh]:
                    if t == TC:
                        c = padded(first, stream, 2)
                        ins = dve.tensor_tensor(ubuf[:, c:c + count], src[:, lo:lo + count], ubuf[:, c:c + count],
                                                ALU.mult)
                    else:
                        c = first + (PROMPT + 2 if stream else 0)
                        o = hh * HALF + lo
                        ins = dve.tensor_tensor(ya[:, at(i), o:o + count].rearrange("p a m -> p (a m)"),
                                                src[:, lo:lo + count], aout[:, c:c + count], ALU.mult)
                ins.then_inc(dve_half, 1)

        def proj_pool(pool, i):
            wait(pool, a_step, 3 * i)
            pool.tensor_copy(pcur[:, :], par[:, at(i), 0:PAR_CQKV].rearrange("p a k -> p (a k)"))
            pool.tensor_copy(raw[:, :, PROMPT + 3:PROMPT + 6],
                             par[:, at(i), PAR_CQKV:PAR_CA].rearrange("p a (k j) -> p (a k) j", j=3))
            pool.tensor_copy(ubuf[:, PROMPT + 2:PROMPT + 4],
                             par[:, at(i), PAR_CA:PARS].rearrange("p a k -> p (a k)")).then_inc(pars_set, 1)

        def tails_pool(pool, i, which):
            if which == 0:
                pool.wait_ge(act_half, ACT_HALVES * i + 2 * TV + 2)
                for k in range(2):
                    ins = pool.tensor_copy(
                        tails[:, at(i), 9 * k:9 * k + 9].rearrange("p a (c j) -> p (a c) j", j=3),
                        raw[:, :, PROMPT + k * (STREAM + 3):PROMPT + 3 + k * (STREAM + 3)])
                ins.then_inc(tail_kept, 1)
            else:
                pool.wait_ge(dve_half, DVE_HALVES * i + 2)
                for k in range(2):
                    c = PROMPT + k * (STREAM + 2)
                    ins = pool.tensor_copy(tails[:, at(i), 18 + 2 * k:20 + 2 * k].rearrange("p a j -> p (a j)"),
                                           ubuf[:, c:c + 2])
                ins.then_inc(tail_kept, 1)

        ya_high, yb_high, ya_low, yb_low = (sem(k) for k in ("ya_high", "yb_high", "ya_low", "yb_low"))
        p2_w, g_in = [sem("p2_w0"), sem("p2_w1")], [sem("gate_in0"), sem("gate_in1")]
        p2_high, p2_low, y_done, mixed, m_sum, m_high, m_low = (
            sem("p2_" + k) for k in ("high", "low", "done", "mixed", "msum", "mhigh", "mlow"))
        o_copied, o_back, x2_set, x2_in, oT_zero = (sem("o_" + k) for k in ("copied", "back", "x2", "x2in", "zero"))
        n_names = "square root recip scaled turned copied logits out".split()
        nx = {k: sem("n_" + k) for k in n_names}
        p3_in, route, route_act, route_pe, zero_set, zero_out = (sem(k) for k in
                                                                 ("p3_in", "route", "route_act", "route_pe", "zero_set", "zero_out"))
        spread_rows = sem("spread_rows")
        e_w = [sem("e_w0"), sem("e_w1")]
        e_x = [sem("e_x0"), sem("e_x1")]
        e_high, e_low, e_xt, e_xh, e_xl, e_gu, e_silu, e_hid, e_ht, e_hh, e_hl, e_dn, e_y = (
            sem("e_" + k) for k in "high low xt xh xl gu silu hid ht hh hl dn y".split())
        e_out = [sem("e_out0"), sem("e_out1")]
        o_x, o_w, o_out = sem("o_x"), sem("o_w"), sem("o_out")
        f_x = sem("f_x")
        f_y = [sem(f"f_y{k}") for k in range(3)]
        o_kept, f_sum = sem("o_kept"), sem("f_sum")
        f_out = sem("f_out")

        def frames(c):
            return slice(0, P if c < 4 else STREAM)

        def wide(c):
            return wideB if c % 2 else wideA

        def table_view(kind):
            return dec[:, :, kind, :]

        def by_head(row):
            return dtmp[:, row, :].rearrange("p (u h) -> p h u", h=HEADS)

        def phase0_tensor(pe):
            pe.wait_ge(const_in, 16)
            for c in range(UNITS):
                pe.wait_ge(x_scaled, c + 1)
                wait(pe, x_low, c - 1)
                for k in range(KC):
                    mm = pe.transpose(wide(c)[:, k * P:(k + 1) * P], xin[c][:, k * P:(k + 1) * P], ident)
                mm.then_inc(x_turned, 1)

        def betas_tensor(pe):
            pe.wait_ge(ba_w, 2)
            for c in range(UNITS):
                for j in range(3 * KC):
                    k, term = divmod(j, 3)
                    x = (xnh, xnl, xnh)[term][:, k, c * P:(c + 1) * P]
                    w = (w16h, w16h, w16l)[term][:, k, :]
                    mm = pe.matmul(small[:, 16 * c:16 * c + 16], x, w, start=(j == 0), stop=(j == 3 * KC - 1))
            mm.then_inc(ba_done, 1)

        def decays_tensor(pe):
            pe.wait_ge(dec_dve, 6)
            pe.matmul(small[:, 0:UNITS * HEADS], upper, dtmp[:, 7, :], start=True, stop=True)
            pe.matmul(small[:, 64:64 + UNITS * HEADS], ones, dtmp[:, 7, :], start=True, stop=True).then_inc(dec_pe, 1)

        def decays_scalar(act, part):
            row = dtmp[:, :, :]
            if part == 1:
                decays_scalar_end(act, row)
                return
            act.wait_ge(dec_dve, 1)
            act.activation(row[:, 0, :], basb[:, :, 0:HEADS], ACT.Tanh, scale=0.5).then_inc(dec_act, 1)
            act.wait_ge(dec_dve, 3)
            act.activation(row[:, 3, :], row[:, 2, :], ACT.Exp, scale=-1.0).then_inc(dec_act, 1)
            act.wait_ge(dec_act, 2)
            act.activation(row[:, 4, :], row[:, 3, :], ACT.Ln, bias=1.0).then_inc(dec_act, 1)
            act.activation(row[:, 6, 0:HEADS], misc[:, M_ALOG:M_ALOG + HEADS], ACT.Exp).then_inc(dec_act, 1)

        def decays_scalar_end(act, row):
            act.wait_ge(dec_dve, 10)
            act.activation(table_view(KEXP), table_view(KSUM), ACT.Exp).then_inc(dec_act, 1)
            act.activation(table_view(KREST), table_view(KREST), ACT.Exp).then_inc(dec_act, 1)
            act.activation(table_view(KLAST), by_head(1), ACT.Exp).then_inc(dec_act, 1)

        def decays_vector(dve, part):
            row = dtmp[:, :, :]
            if part == 1:
                decays_vector_end(dve, row)
                return

            def framed(r):
                return dtmp[:, r, :].rearrange("p (u h) -> p u h", h=HEADS)

            dve.wait_ge(ba_done, 1)
            dve.tensor_copy(basb[:, :, :], small[:, 0:UNITS * 16].rearrange("p (u h) -> p u h", h=16))\
               .then_inc(dec_dve, 1)
            dve.wait_ge(dec_dve, 1)
            dve.tensor_tensor(framed(1), basb[:, :, HEADS:16],
                              misc[:, M_DT:M_DT + HEADS].unsqueeze(1).to_broadcast([P, UNITS, HEADS]), ALU.add)\
               .then_inc(dec_dve, 1)
            dve.wait_ge(dec_dve, 2)
            dve.scalar_tensor_tensor(row[:, 2, :], row[:, 1, :], -1.0, row[:, 1, :], ALU.mult, ALU.max)\
               .then_inc(dec_dve, 1)
            dve.wait_ge(dec_act, 3)
            dve.scalar_tensor_tensor(row[:, 5, :], row[:, 1, :], 0.0, row[:, 4, :], ALU.max, ALU.add)\
               .then_inc(dec_dve, 1)
            dve.wait_ge(dec_act, 4)
            dve.wait_ge(dec_dve, 4)
            dve.scalar_tensor_tensor(framed(7), framed(5), -1.0,
                                     row[:, 6, 0:HEADS].unsqueeze(1).to_broadcast([P, UNITS, HEADS]),
                                     ALU.mult, ALU.mult).then_inc(dec_dve, 1)
            dve.wait_ge(dec_dve, 5)
            dve.tensor_tensor(framed(7), framed(7),
                              misc[:, M_VALID:M_VALID + UNITS].unsqueeze(2).to_broadcast([P, UNITS, HEADS]),
                              ALU.mult).then_inc(dec_dve, 1)
            dve.tensor_scalar(table_view(KBETA), by_head(0), 0.5, 0.5, ALU.mult, ALU.add).then_inc(dec_dve, 1)

        def decays_vector_end(dve, row):
            dve.wait_ge(dec_pe, 1)
            dve.tensor_copy(table_view(KSUM), small[:, 0:UNITS * HEADS].rearrange("p (u h) -> p h u", h=HEADS))\
               .then_inc(dec_dve, 1)
            dve.tensor_copy(row[:, 1, :], small[:, 64:64 + UNITS * HEADS]).then_inc(dec_dve, 1)
            dve.wait_ge(dec_dve, 9)
            dve.tensor_tensor(table_view(KREST), by_head(1), table_view(KSUM), ALU.subtract).then_inc(dec_dve, 1)
            dve.wait_ge(dec_act, 5)
            dve.tensor_tensor(table_view(KBEXP), table_view(KBETA), table_view(KEXP), ALU.mult).then_inc(dec_dve, 1)

        banks = [[proj[0], proj[1]], [proj[2], small]]

        def out_tensor(pe, q, k, xh, xl):
            pe.wait_ge(p2_low, q + 1)
            for hh in range(2):
                if isinstance(q, int) and q < 2:
                    pass
                elif xh is mh and not (isinstance(q, int) and q < 2 * KC + 2):
                    pe.wait_ge(o_copied, q - 2 * KC - 1)
                else:
                    pe.wait_ge(mixed, q - 1)
                for j in range(3 * KC):
                    kc, term = divmod(j, 3)
                    w = (whi, whi, wlo)[term][k]
                    x = (xh, xl, xh)[term]
                    mm = pe.matmul(banks[k][hh][:, 0:HALF], w[:, kc, :], x[:, kc, hh * HALF:(hh + 1) * HALF],
                                   start=(j == 0), stop=(j == 3 * KC - 1))
                mm.then_inc(y_done, 1)

        def back_tensor(pe, q, k):
            pe.wait_ge(o_copied, q - 2 * KC + 1)
            if not (isinstance(q, int) and q < 2 * KC + 2):
                pe.wait_ge(x2_set, q - 2 * KC - 1)
            for u in range(UNITS):
                mm = pe.transpose(wide(k)[:, U[u]], oT[k][:, U[u]], ident)
            mm.then_inc(o_back, 1)

        def phase2_tensor(pe):
            pe.wait_ge(ya_low, 1)
            for k in range(2):
                out_tensor(pe, k, k, xnh, xnl)
            with pe.Fori(1, KC // 2) as j:
                for k in range(2):
                    out_tensor(pe, 2 * j + k, k, xnh, xnl)
            pe.wait_ge(yb_low, 1)
            with pe.Fori(KC // 2, KC) as j:
                for k in range(2):
                    out_tensor(pe, 2 * j + k, k, ybh, ybl)
            pe.wait_ge(m_low, KC)
            first = 2 * KC
            out_tensor(pe, first, 0, mh, ml)
            out_tensor(pe, first + 1, 1, mh, ml)
            back_tensor(pe, first, 0)
            with pe.Fori(KC + 1, KC + KC // 2) as j:
                out_tensor(pe, 2 * j, 0, mh, ml)
                back_tensor(pe, 2 * j - 1, 1)
                out_tensor(pe, 2 * j + 1, 1, mh, ml)
                back_tensor(pe, 2 * j, 0)
            back_tensor(pe, 3 * KC - 1, 1)

        def out_split_high(act, q, k):
            if isinstance(q, int):
                act.wait_ge(p2_w[k], 16 * (q // 2 + 1))
            else:
                act.wait_ge(p2_w[k], 8 * (q - k) + 16)
            wait(act, y_done, 2 * (q - 1))
            act.activation(whi[k][:, :, :], wraw[k][:, :, :], ACT.Copy).then_inc(p2_high, 1)

        def out_split_low(dve, q, k):
            dve.wait_ge(p2_high, q + 1)
            dve.tensor_tensor(wlo[k][:, :, :], wraw[k][:, :, :], whi[k][:, :, :].bitcast(F32), ALU.subtract)\
               .then_inc(p2_low, 1)

        def mix_high(act, q, k):
            m = q - KC
            act.wait_ge(m_sum, m + 1)
            act.activation(mh[:, at(m), :].rearrange("p a m -> p (a m)"), mix[k][:, :], ACT.Copy, scale=0.5)\
               .then_inc(m_high, 1)

        def o_copy(act, q, k):
            n = q - 2 * KC
            act.wait_ge(y_done, 2 * q + 2)
            if not (isinstance(q, int) and n < 2):
                act.wait_ge(o_back, n - 1)
            for hh in range(2):
                ins = act.activation(oT[k][:, hh * HALF:(hh + 1) * HALF], banks[k][hh][:, 0:HALF], ACT.Copy)
            ins.then_inc(o_copied, 1)

        def phase2_scalar(act):
            act.wait_ge(proj_done, 2 * TILES * HEADS)
            act.wait_ge(dve_half, DVE_HALVES * HEADS)
            act.activation(xnh[:, :, 0:TOK], ya[:, :, :], ACT.Copy).then_inc(ya_high, 1)
            for k in range(2):
                out_split_high(act, k, k)
            act.wait_ge(s["yb_set"], HEADS)
            act.wait_ge(s["s_out"], 32 * HEADS)
            act.wait_ge(tails_out, 16)
            act.activation(ybh[:, :, :], yb[:, :, :], ACT.Copy).then_inc(yb_high, 1)
            with act.Fori(1, KC // 2) as j:
                for k in range(2):
                    out_split_high(act, 2 * j + k, k)
            for k in range(2):
                out_split_high(act, KC + k, k)
                if k == 1:
                    act.wait_ge(yb_low, 1)
                    act.wait_ge(ya_low, 1)
                    mix_high(act, KC, 0)
            with act.Fori(KC // 2 + 1, KC) as j:
                out_split_high(act, 2 * j, 0)
                mix_high(act, 2 * j - 1, 1)
                out_split_high(act, 2 * j + 1, 1)
                mix_high(act, 2 * j, 0)
            out_split_high(act, 2 * KC, 0)
            mix_high(act, 2 * KC - 1, 1)
            out_split_high(act, 2 * KC + 1, 1)
            act.wait_ge(oT_zero, 2)
            o_copy(act, 2 * KC, 0)
            with act.Fori(KC + 1, KC + KC // 2) as j:
                out_split_high(act, 2 * j, 0)
                o_copy(act, 2 * j - 1, 1)
                out_split_high(act, 2 * j + 1, 1)
                o_copy(act, 2 * j, 0)
            o_copy(act, 3 * KC - 1, 1)

        def mix_a(dve, q, k):
            if isinstance(q, int):
                dve.wait_ge(g_in[k], 16 * (q // 2 + 1))
            else:
                dve.wait_ge(g_in[k], 8 * (q - k) + 16)
            dve.wait_ge(y_done, 2 * q + 2)
            for hh in range(2):
                h = slice(hh * HALF, (hh + 1) * HALF)
                ins = dve.scalar_tensor_tensor(ya[:, at(q), h].rearrange("p a m -> p (a m)"), tg[k][:, h], 1.0,
                                               banks[k][hh][:, 0:HALF], ALU.add, ALU.mult)
            ins.then_inc(mixed, 1)

        def mix_b(dve, q, k):
            m = q - KC
            if isinstance(q, int):
                dve.wait_ge(g_in[k], 16 * (q // 2 + 1))
                wait(dve, m_high, m - 1)
            else:
                dve.wait_ge(g_in[k], 8 * (q - k) + 16)
                dve.wait_ge(m_high, m - 1)
            dve.wait_ge(y_done, 2 * q + 2)
            for hh in range(2):
                h = slice(hh * HALF, (hh + 1) * HALF)
                ins = dve.scalar_tensor_tensor(mix[k][:, h], tg[k][:, h], 1.0, banks[k][hh][:, 0:HALF],
                                               ALU.add, ALU.mult)
            ins.then_inc(mixed, 1)
            dve.wait_ge(mixed, q + 1)
            dve.tensor_tensor(mix[k][:, :], mix[k][:, :], ya[:, at(m), :].rearrange("p a m -> p (a m)"), ALU.add)\
               .then_inc(m_sum, 1)
            dve.wait_ge(m_high, m + 1)
            dve.scalar_tensor_tensor(ml[:, at(m), :].rearrange("p a m -> p (a m)"), mix[k][:, :], 0.5,
                                     mh[:, at(m), :].bitcast(F32).rearrange("p a m -> p (a m)"),
                                     ALU.mult, ALU.subtract).then_inc(m_low, 1)

        def x2_add(dve, q, k):
            n = q - 2 * KC
            dve.wait_ge(o_back, n + 1)
            dst = x2[:, :, at(n * P, P)]
            dve.tensor_tensor(dst, dst, wide(k)[:, 0:UW].rearrange("p (u m) -> p u m", m=P), ALU.add)\
               .then_inc(x2_set, 1)

        def phase2_vector(dve):
            dve.wait_ge(ya_high, 1)
            dve.tensor_tensor(xnl[:, :, 0:TOK], ya[:, :, :], xnh[:, :, 0:TOK].bitcast(F32), ALU.subtract)\
               .then_inc(ya_low, 1)
            for k in range(2):
                out_split_low(dve, k, k)
            dve.wait_ge(yb_high, 1)
            dve.tensor_tensor(ybl[:, :, :], yb[:, :, :], ybh[:, :, :].bitcast(F32), ALU.subtract)\
               .then_inc(yb_low, 1)
            dve.wait_ge(ya_low, 1)
            mix_a(dve, 0, 0)
            with dve.Fori(1, KC // 2) as j:
                out_split_low(dve, 2 * j, 0)
                mix_a(dve, 2 * j - 1, 1)
                out_split_low(dve, 2 * j + 1, 1)
                mix_a(dve, 2 * j, 0)
            out_split_low(dve, KC, 0)
            mix_a(dve, KC - 1, 1)
            out_split_low(dve, KC + 1, 1)
            mix_b(dve, KC, 0)
            with dve.Fori(KC // 2 + 1, KC) as j:
                out_split_low(dve, 2 * j, 0)
                mix_b(dve, 2 * j - 1, 1)
                out_split_low(dve, 2 * j + 1, 1)
                mix_b(dve, 2 * j, 0)
            out_split_low(dve, 2 * KC, 0)
            mix_b(dve, 2 * KC - 1, 1)
            out_split_low(dve, 2 * KC + 1, 1)
            dve.wait_ge(x2_in, 32)
            dve.wait_ge(oT_zero, 2)
            with dve.Fori(KC + 1, KC + KC // 2) as j:
                out_split_low(dve, 2 * j, 0)
                x2_add(dve, 2 * j - 2, 0)
                out_split_low(dve, 2 * j + 1, 1)
                x2_add(dve, 2 * j - 1, 1)
            x2_add(dve, 3 * KC - 2, 0)
            x2_add(dve, 3 * KC - 1, 1)

        def phase3_scalar(act):
            act.wait_ge(x2_set, KC)
            for c in range(UNITS):
                wait(act, nx["square"], c)
                act.activation(sqs[:, :], x2[:, c, :], ACT.Square, accum_out=small_sb[:, 24 + c:25 + c])\
                   .then_inc(nx["square"], 1)
            act.wait_ge(nx["square"], UNITS)
            act.activation(small_sb[:, 32:32 + UNITS], small_sb[:, 24:24 + UNITS], ACT.Sqrt, scale=1.0 / D,
                           bias=epsq[:, 1:2]).then_inc(nx["root"], 1)
            for c in range(UNITS):
                act.wait_ge(nx["turned"], c + 1)
                wait(act, nx["logits"], c - 1)
                act.activation(tT[c % 2][:, :], wide(c)[:, :], ACT.Copy).then_inc(nx["copied"], 1)
            for part in range(2):
                weights_high(act, 0, 0, part)
            act.wait_ge(route, R_GAP)
            act.activation(r4[3][:, :, :], r4[2][:, :, :], ACT.Exp).then_inc(route_act, 1)
            act.activation(r5[:, 9, :], r5[:, 8, :], ACT.Exp).then_inc(route_act, 1)

        def phase3_tensor(pe):
            pe.wait_ge(p3_in, 32)
            for c in range(UNITS):
                pe.wait_ge(nx["scaled"], c + 1)
                wait(pe, nx["copied"], c - 1)
                for k in range(KC):
                    mm = pe.transpose(wide(c)[:, k * P:(k + 1) * P], tn[:, c, k * P:(k + 1) * P], ident)
                mm.then_inc(nx["turned"], 1)
                pe.wait_ge(nx["copied"], c + 1)
                n = GROUPS + EXPERTS
                for k in range(KC):
                    mm = pe.matmul(small[:, n * c:n * c + n], tT[c % 2][:, k * P:(k + 1) * P], wr[:, k, :],
                                   start=(k == 0), stop=(k == KC - 1))
                mm.then_inc(nx["logits"], 1)
            pe.wait_ge(route, R_PAIRS)
            E = EXPERTS
            for c in range(UNITS):
                for j in range(c + 1):
                    pe.matmul(proj[0][:, E * c:E * c + E], ones if j < c else before, r32[0][:, j, :],
                              start=(j == 0), stop=(j == c))
            for j in range(UNITS):
                mm = pe.matmul(proj[0][:, E * UNITS:E * UNITS + E], ones, r32[0][:, j, :], start=(j == 0),
                               stop=(j == UNITS - 1))
            mm.then_inc(route_pe, 1)

        def phase3_vector(dve):
            dve.wait_ge(nx["root"], 1)
            dve.reciprocal(small_sb[:, 40:40 + UNITS], small_sb[:, 32:32 + UNITS]).then_inc(nx["recip"], 1)
            dve.wait_ge(nx["recip"], 1)
            dve.wait_ge(p3_in, 32)
            for c in range(UNITS):
                dve.scalar_tensor_tensor(tn[:, c, :], x2[:, c, :], small_sb[:, 40 + c:41 + c], g2row[:, :],
                                         ALU.mult, ALU.mult).then_inc(nx["scaled"], 1)
            weights_low(dve, 0, 0, 0)
            weights_low(dve, 0, 0, 1)
            dve.wait_ge(nx["logits"], UNITS)
            chain = [0]

            def link(ins):
                chain[0] += 1
                ins.then_inc(route, 1)
                dve.wait_ge(route, chain[0])

            def over(ap, axis, shape):
                return ap.unsqueeze(axis).to_broadcast(shape)

            def first_largest(values, count, top_row, index_row, tmp, chosen):
                shape = [P, UNITS, count]
                iota = over(misc[:, M_IOTA:M_IOTA + count], 1, shape)
                link(dve.tensor_reduce(r5[:, top_row, :], values, X, ALU.max))
                link(dve.tensor_tensor(tmp, values, over(r5[:, top_row, :], 2, shape), ALU.is_equal))
                link(dve.scalar_tensor_tensor(tmp, tmp, -64.0, iota, ALU.mult, ALU.add))
                link(dve.tensor_reduce(r5[:, index_row, :], tmp, X, ALU.min))
                link(dve.scalar_tensor_tensor(chosen, iota, -64.0, over(r5[:, index_row, :], 2, shape),
                                              ALU.add, ALU.is_equal))

            n = GROUPS + EXPERTS
            link(dve.tensor_tensor(lg[:, :, :], small[:, 0:UNITS * n].rearrange("p (u n) -> p u n", n=n),
                                   over(misc[:, M_RBIAS:M_RBIAS + n], 1, [P, UNITS, n]), ALU.add))
            first_largest(lg[:, :, 0:GROUPS], GROUPS, 0, 1, r4[1][:, :, :], r4[0][:, :, :])
            link(dve.tensor_tensor(r4[0][:, :, :], r4[0][:, :, :],
                                   over(misc[:, M_VALID:M_VALID + UNITS], 2, [P, UNITS, GROUPS]), ALU.mult))
            shape4 = [P, UNITS, GROUPS, PER_GROUP]

            def grouped(t):
                return t.rearrange("p u (g e) -> p u g e", g=GROUPS)

            link(dve.tensor_tensor(grouped(r32[0][:, :, :]), grouped(lg[:, :, GROUPS:n]), over(r4[0][:, :, :], 3, shape4),
                                   ALU.mult))
            link(dve.tensor_reduce(r8[0][:, :, :], r32[0][:, :, :].rearrange("p u (g e) -> p u e g", g=GROUPS), X,
                                   ALU.add))
            first_largest(r8[0][:, :, :], PER_GROUP, 4, 5, r8[4][:, :, :], r8[1][:, :, :])
            link(dve.scalar_tensor_tensor(r8[2][:, :, :], r8[1][:, :, :], -3.0e38, r8[0][:, :, :], ALU.mult, ALU.add))
            first_largest(r8[2][:, :, :], PER_GROUP, 6, 7, r8[4][:, :, :], r8[3][:, :, :])
            for k, chosen in ((0, r8[1]), (1, r8[3])):
                link(dve.tensor_tensor(grouped(pair[:, k, :, :]), over(r4[0][:, :, :], 3, shape4),
                                       over(chosen[:, :, :], 2, shape4), ALU.mult))
            link(dve.tensor_tensor(r32[0][:, :, :], pair[:, 0, :, :], pair[:, 1, :, :], ALU.add))
            assert chain[0] == R_PAIRS, chain
            link(dve.tensor_tensor(r4[2][:, :, :], lg[:, :, 0:GROUPS], over(r5[:, 0, :], 2, [P, UNITS, GROUPS]),
                                   ALU.subtract))
            link(dve.tensor_tensor(r5[:, 8, :], r5[:, 6, :], r5[:, 4, :], ALU.subtract))
            assert chain[0] == R_GAP, chain
            dve.wait_ge(route_pe, 1)
            E = EXPERTS
            both = [P, 2, UNITS, E]
            shape = [P, UNITS, E]
            earlier = proj[0][:, 0:UNITS * E].rearrange("p (u e) -> p u e", e=E)
            total = proj[0][:, UNITS * E:UNITS * E + E]
            link(dve.tensor_tensor_scan(ex[:, 2, :], ones[:, 0:E], total, 0.0, ALU.mult, ALU.add))
            link(dve.tensor_tensor(ex[:, 2, :], ex[:, 2, :], total, ALU.subtract))
            link(dve.tensor_tensor(r32[1][:, :, :], earlier, over(ex[:, 2, :], 1, shape), ALU.add))
            link(dve.tensor_tensor(pick[:, :, :, :], pair[:, :, :, :], over(r32[1][:, :, :], 1, both), ALU.mult))
            link(dve.tensor_reduce(r5[:, 10:12, :], pick[:, :, :, :], X, ALU.add))
            link(dve.tensor_copy(slot_row[:, :].rearrange("p (k u) -> p k u", k=2), r5[:, 10:12, :]))
            assert chain[0] == R_PLACES, chain
            link(dve.tensor_copy(table[0:1, TB_FIRST:TB_FIRST + E], ex[0:1, 2, :]))
            link(dve.tensor_scalar(ex[:, 1, :], total, float(BR), None, ALU.is_gt))
            for k in range(2, (TOK - 1) // BR + 1):
                link(dve.scalar_tensor_tensor(ex[:, 1, :], total, float(BR * k), ex[:, 1, :], ALU.is_gt, ALU.add))
            link(dve.tensor_tensor_scan(ex[:, 3, :], ones[:, 0:E], ex[:, 1, :], 0.0, ALU.mult, ALU.add))
            link(dve.tensor_copy(table[0:1, TB_COUNT:TB_COUNT + 1], ex[0:1, 3, E - 1:E]))
            link(dve.tensor_tensor(ex[:, 3, :], ex[:, 3, :], ex[:, 1, :], ALU.subtract))
            dve.wait_ge(route_act, 2)
            link(dve.tensor_reduce(r5[:, 2, :], r4[3][:, :, :], X, ALU.add))
            link(dve.scalar_tensor_tensor(r5[:, 3, :], r5[:, 9, :], 1.0, r5[:, 2, :], ALU.add, ALU.mult))
            link(dve.reciprocal(coef[:, 0, :], r5[:, 3, :]))
            link(dve.tensor_tensor(coef[:, 1, :], coef[:, 0, :], r5[:, 9, :], ALU.mult))
            iota_e = misc[:, M_IOTA:M_IOTA + E]
            link(dve.tensor_tensor(ex[:, 4, :], ex[:, 3, :], iota_e, ALU.subtract))
            link(dve.tensor_scalar(ex[:, 4, :], ex[:, 4, :], float(E - 1), float(BR), ALU.add, ALU.mult))
            link(dve.scalar_tensor_tensor(r32[1][:, :, :], earlier, float(BR), over(ex[:, 4, :], 1, shape),
                                          ALU.is_ge, ALU.mult))
            link(dve.tensor_tensor(r32[1][:, :, :], r32[1][:, :, :], earlier, ALU.add))
            link(dve.scalar_tensor_tensor(r32[1][:, :, :], over(iota_e, 1, shape), float(BR), r32[1][:, :, :],
                                          ALU.mult, ALU.add))
            link(dve.tensor_tensor(pick[:, :, :, :], pair[:, :, :, :], over(r32[1][:, :, :], 1, both), ALU.mult))
            link(dve.tensor_reduce(r5[:, 10:12, :], pick[:, :, :, :], X, ALU.add))
            link(dve.tensor_copy(slot_y[:, :].rearrange("p (k u) -> p k u", k=2), r5[:, 10:12, :]))
            one = [1, OVER, E]
            further = misc[0:1, M_IOTA:M_IOTA + OVER]
            link(dve.tensor_tensor(bt[0:1, 0, :, :], over(ex[0:1, 3, :], 1, one), over(further, 2, one), ALU.is_le))
            link(dve.tensor_reduce(brow[0:1, 0, :], bt[0:1, 0, :, :], X, ALU.add))
            link(dve.tensor_scalar(brow[0:1, 0, :], brow[0:1, 0, :], -1.0, None, ALU.add))
            link(dve.tensor_copy(table[0:1, TB_EXPERT:TB_EXPERT + OVER], brow[0:1, 0, :]))
            link(dve.tensor_tensor(bt[0:1, 1, :, :], over(misc[0:1, M_IOTA:M_IOTA + E], 1, one),
                                   over(brow[0:1, 0, :], 2, one), ALU.is_equal))
            link(dve.scalar_tensor_tensor(ex[0:1, 5, :], ex[0:1, 3, :], -float(BR), ex[0:1, 2, :], ALU.mult, ALU.add))
            link(dve.tensor_tensor(bt[0:1, 2, :, :], bt[0:1, 1, :, :], over(ex[0:1, 5, :], 1, one), ALU.mult))
            link(dve.tensor_reduce(brow[0:1, 1, :], bt[0:1, 2, :, :], X, ALU.add))
            link(dve.scalar_tensor_tensor(brow[0:1, 2, :], further, float(BR), brow[0:1, 1, :], ALU.mult, ALU.add))
            link(dve.tensor_scalar(brow[0:1, 2, :], brow[0:1, 2, :], float(BR), float(SLOTS), ALU.add, ALU.min))
            link(dve.tensor_copy(table[0:1, TB_ROW:TB_ROW + OVER], brow[0:1, 2, :]))
            assert chain[0] == ROUTE_STEPS, chain

        GU = 16 * DE

        def rows_turned(pe, b, k, arrived=None):
            pe.wait_ge(*(arrived or (e_x[k], 8 * (b - k) + 16)))
            wait(pe, e_xl, b)
            v = xb[k][0:BR, :].rearrange("s (p c) -> s c p", c=KC)
            for c in range(KC):
                mm = pe.transpose(wideA[:, c * P:c * P + BR], v[:, c, :], ident[0:BR, 0:BR])
            mm.then_inc(e_xt, 1)

        def gate_up(pe, b, k):
            pe.wait_ge(e_low, 2 * b + 1)
            pe.wait_ge(e_xl, b + 1)
            wait(pe, e_hid, b - 1)
            for j in range(3 * KC):
                c, term = divmod(j, 3)
                x = (xbh, xbl, xbh)[term][k][:, c, :]
                w = (ehi, ehi, elo)[term][k][:, 0:GU].rearrange("p (w c n) -> p w c n", w=2, c=KC)[:, :, c, :]
                mm = pe.matmul(proj[k][0:BR, :].rearrange("p (w n) -> p w n", w=2), x, w, start=(j == 0),
                               stop=(j == 3 * KC - 1))
            mm.then_inc(e_gu, 1)

        def hidden_turned(pe, b, k):
            pe.wait_ge(e_hid, b + 1)
            wait(pe, e_hl, b)
            v = hid[k][0:BR, :].rearrange("s (p c) -> s c p", c=2)
            for c in range(2):
                mm = pe.transpose(proj[2][:, c * BR:(c + 1) * BR], v[:, c, :], ident[0:BR, 0:BR])
            mm.then_inc(e_ht, 1)

        def down(pe, b, k):
            pe.wait_ge(e_hl, b + 1)
            pe.wait_ge(e_low, 2 * b + 2)
            wait(pe, e_y, b)
            for n in range(2):
                for j in range(6):
                    c, term = divmod(j, 3)
                    x = (hth, htl, hth)[term][k][:, c, :]
                    w = (ehi, ehi, elo)[term][k][:, GU + c * D + 512 * n:GU + c * D + 512 * (n + 1)]
                    mm = pe.matmul(wideB[0:BR, 512 * n:512 * (n + 1)], x, w, start=(j == 0), stop=(j == 5))
            mm.then_inc(e_dn, 1)

        def expert_tensor(pe, b, k, first=False, last=False):
            gate_up(pe, b, k)
            if not last:
                rows_turned(pe, b + 1, 1 - k)
            if not first:
                down(pe, b - 1, 1 - k)
            hidden_turned(pe, b, k)

        def further_blocks(engine, step):
            engine.wait_ge(route, ROUTE_STEPS)
            count = engine.value_load(table[0:1, TB_COUNT:TB_COUNT + 1], min_val=0, max_val=OVER)
            with engine.Fori(0, OVER) as j:
                with engine.If(count > j):
                    step(j)
            return count

        def phase4_tensor(pe):
            rows_turned(pe, 0, 0)
            expert_tensor(pe, 0, 0, first=True)
            expert_tensor(pe, 1, 1)
            with pe.Fori(1, EXPERTS // 2 - 1) as i:
                for k in range(2):
                    expert_tensor(pe, 2 * i + k, k)
            expert_tensor(pe, EXPERTS - 2, 0)
            expert_tensor(pe, EXPERTS - 1, 1, last=True)
            down(pe, EXPERTS - 1, 1)

            def further(j):
                b = j + EXPERTS
                rows_turned(pe, b, 0, arrived=(o_x, 16 * j + 16))
                gate_up(pe, b, 0)
                hidden_turned(pe, b, 0)
                down(pe, b, 0)

            further_blocks(pe, further)

        def weights_high(act, b, k, part, arrived=None):
            if part == 0:
                act.wait_ge(*(arrived or (e_w[k], 24 * (b - k) + 48)))
                wait(act, e_gu, b - 1)
                act.activation(ehi[k][:, 0:GU], eraw[k][:, 0:GU], ACT.Copy).then_inc(e_high, 1)
            else:
                wait(act, e_dn, b - 1)
                act.activation(ehi[k][:, GU:], eraw[k][:, GU:], ACT.Copy).then_inc(e_high, 1)

        def weights_low(dve, b, k, part):
            dve.wait_ge(e_high, 2 * b + 1 + part)
            cols = slice(0, GU) if part == 0 else slice(GU, 24 * DE)
            dve.tensor_tensor(elo[k][:, cols], eraw[k][:, cols], ehi[k][:, cols].bitcast(F32), ALU.subtract)\
               .then_inc(e_low, 1)

        turned_rows = wideA[:, :].rearrange("p (c m) -> p c m", c=KC)[:, :, 0:BR]
        turned_hidden = proj[2][:, 0:2 * BR].rearrange("p (c m) -> p c m", c=2)

        def rows_high(act, b, k):
            act.wait_ge(e_xt, b + 1)
            act.activation(xbh[k][:, :, :], turned_rows, ACT.Copy).then_inc(e_xh, 1)

        def rows_low(dve, b, k):
            dve.wait_ge(e_xh, b + 1)
            dve.tensor_tensor(xbl[k][:, :, :], turned_rows, xbh[k][:, :, :].bitcast(F32), ALU.subtract)\
               .then_inc(e_xl, 1)

        def silu_gate(act, b, k):
            act.wait_ge(e_gu, b + 1)
            wait(act, e_hid, b - 1)
            act.activation(hgate[k][0:BR, :], proj[k][0:BR, 0:DE], ACT.Silu).then_inc(e_silu, 1)

        def hidden_high(act, b, k):
            act.wait_ge(e_ht, b + 1)
            act.activation(hth[k][:, :, :], turned_hidden, ACT.Copy).then_inc(e_hh, 1)

        def y_copy(act, b, k, stored=None):
            act.wait_ge(e_dn, b + 1)
            if stored:
                wait(act, *stored)
            elif not (isinstance(b, int) and b < 2):
                act.wait_ge(e_out[k], 8 * (b - k))
            act.activation(yout[k][0:BR, :], wideB[0:BR, :], ACT.Copy).then_inc(e_y, 1)

        def expert_scalar(act, b, k, first=False, last=False):
            if not last:
                weights_high(act, b + 1, 1 - k, 0)
            silu_gate(act, b, k)
            if not last:
                rows_high(act, b + 1, 1 - k)
            if not first:
                y_copy(act, b - 1, 1 - k)
            if not last:
                weights_high(act, b + 1, 1 - k, 1)
            hidden_high(act, b, k)

        def phase4_scalar(act):
            rows_high(act, 0, 0)
            expert_scalar(act, 0, 0, first=True)
            expert_scalar(act, 1, 1)
            with act.Fori(1, EXPERTS // 2 - 1) as i:
                for k in range(2):
                    expert_scalar(act, 2 * i + k, k)
            expert_scalar(act, EXPERTS - 2, 0)
            expert_scalar(act, EXPERTS - 1, 1, last=True)
            y_copy(act, EXPERTS - 1, 1)
            act.wait_ge(e_out[0], 8 * EXPERTS)

            def further(j):
                b = j + EXPERTS
                weights_high(act, b, 0, 0, arrived=(o_w, 48 * j + 48))
                weights_high(act, b, 0, 1)
                rows_high(act, b, 0)
                silu_gate(act, b, 0)
                hidden_high(act, b, 0)
                y_copy(act, b, 0, stored=(o_out, 16 * j))

            further_blocks(act, further)

        def hidden_set(dve, b, k):
            dve.wait_ge(e_silu, b + 1)
            wait(dve, e_ht, b - 1)
            dve.tensor_tensor(hid[k][0:BR, :], proj[k][0:BR, DE:2 * DE], hgate[k][0:BR, :], ALU.mult)\
               .then_inc(e_hid, 1)

        def hidden_low(dve, b, k):
            dve.wait_ge(e_hh, b + 1)
            dve.tensor_tensor(htl[k][:, :, :], turned_hidden, hth[k][:, :, :].bitcast(F32), ALU.subtract)\
               .then_inc(e_hl, 1)

        def expert_vector(dve, b, k, last=False):
            if not last:
                weights_low(dve, b + 1, 1 - k, 0)
            hidden_set(dve, b, k)
            if not last:
                rows_low(dve, b + 1, 1 - k)
                weights_low(dve, b + 1, 1 - k, 1)
            hidden_low(dve, b, k)

        def phase4_vector(dve):
            rows_low(dve, 0, 0)
            expert_vector(dve, 0, 0)
            expert_vector(dve, 1, 1)
            with dve.Fori(1, EXPERTS // 2 - 1) as i:
                for k in range(2):
                    expert_vector(dve, 2 * i + k, k)
            expert_vector(dve, EXPERTS - 2, 0)
            expert_vector(dve, EXPERTS - 1, 1, last=True)

            def further(j):
                b = j + EXPERTS
                weights_low(dve, b, 0, 0)
                weights_low(dve, b, 0, 1)
                rows_low(dve, b, 0)
                hidden_set(dve, b, 0)
                hidden_low(dve, b, 0)

            count = further_blocks(dve, further)
            dve.wait_ge(o_out, 16 * count)
            dve.tensor_copy(small_sb[0:1, 59:60], epsq[0:1, 1:2]).then_inc(o_kept, 1)

        def phase5_scalar(act):
            for c in range(UNITS):
                r = frames(c)
                act.wait_ge(f_sum, 2 * c + 2)
                act.wait_ge(x_square, UNITS + c)
                act.activation(fsq[r, :], fx[c][r, :], ACT.Square, accum_out=small_sb[r, c:c + 1]).then_inc(x_square, 1)
                act.wait_ge(x_square, UNITS + c + 1)
                act.activation(small_sb[r, 8 + c:9 + c], small_sb[r, c:c + 1], ACT.Sqrt, scale=1.0 / D,
                               bias=epsq[r, 1:2]).then_inc(x_root, 1)
                if c > 0:
                    y_final(act, c - 1)
            y_final(act, UNITS - 1)

        def y_final(act, c):
            act.wait_ge(x_scaled, UNITS + c + 1)
            act.dma_start(O["y"][c * P:c * P + frames(c).stop, :], fx[c][frames(c), :]).then_inc(f_out, 16)

        def normed(dve, c):
            r = frames(c)
            dve.wait_ge(x_root, UNITS + c + 1)
            dve.reciprocal(small_sb[r, 16 + c:17 + c], small_sb[r, 8 + c:9 + c]).then_inc(x_recip, 1)
            dve.wait_ge(x_recip, UNITS + c + 1)
            dve.scalar_tensor_tensor(fx[c][r, :], fx[c][r, :], small_sb[r, 16 + c:17 + c], fgrow[r, :], ALU.mult,
                                     ALU.mult).then_inc(x_scaled, 1)

        def phase5_vector(dve):
            dve.wait_ge(f_x, 16 * (UNITS + 1))
            for c in range(UNITS):
                r = frames(c)
                for k in range(2):
                    dve.wait_ge(f_y[c // 2], 64 if c < 4 else 32)
                    dve.scalar_tensor_tensor(fx[c][r, :], fy[k][c][r, :], coef[r, k, c:c + 1], fx[c][r, :],
                                             ALU.mult, ALU.add).then_inc(f_sum, 1)
                    dve.wait_ge(f_sum, 2 * c + k + 1)
                if c > 0:
                    normed(dve, c - 1)
            normed(dve, UNITS - 1)

        block = top.enter_context(nc.Block())

        @block.sync
        def _(sp):
            for c in range(UNITS):
                rows = frames(c).stop
                sp.dma_start(xin[c][0:rows, :], A["x"][c * P:c * P + rows, :]).then_inc(x_in[c], 16)
                if c == 0:
                    sp.dma_start(g1row[:, :], A["g1row"]).then_inc(g1_in, 16)
                    sp.dma_start(const[:, :], A["consts"]).then_inc(const_in, 16)
                if c == 2:
                    sp.dma_start(wraw[0][:, :, :], A["w_in"][0]).then_inc(w_in[0], 16)
            for k in (1, 2):
                sp.dma_start(wraw[k][:, :, :], A["w_in"][k]).then_inc(w_in[k], 16)
            sp.dma_start(w16[:, :, :], A["w16"]).then_inc(par_in, 16)
            sp.dma_start(onorm[:, :], A["onorm"]).then_inc(par_in, 16)
            sp.dma_start(par[:, :, :], A["params"]).then_inc(par_in, 16)

            def tile_load(i, t):
                sp.wait_ge(w_low, TILES * i + t - 2)
                k = i * TILES + t
                sp.dma_start(wraw[t % 3][:, :, :], A["w_in"][at(k)].rearrange("a p k m -> (a p) k m"))\
                  .then_inc(w_in[t % 3], 16)

            for t in range(3, TILES):
                tile_load(0, t)
            sp.wait_ge(zero_set, 1)
            sp.dma_start(scr_rows[SLOTS:ROWS, :], zero[0:BR, :]).then_inc(zero_out, 16)
            sp.dma_start(scr_y[EXPERTS * BR:BLOCKS * BR, :].rearrange("(j p) d -> p j d", p=BR),
                         zero[0:BR, :].unsqueeze(1).to_broadcast([BR, OVER, D])).then_inc(zero_out, 16)
            with sp.Fori(1, HEADS) as i:
                for t in range(TILES):
                    tile_load(i, t)
            def expert_weights(e, k, arrived):
                v = eraw[k][:, 0:16 * DE].rearrange("p (w n) -> p w n", w=2)
                for j, w in enumerate(("w_gate", "w_up")):
                    sp.dma_start(v[:, j, :], A[w][at(e), :, :].rearrange("a (p c) n -> (a p) (c n)", p=P))\
                      .then_inc(arrived, 16)
                sp.dma_start(eraw[k][:, 16 * DE:], A["w_down"][at(e), :, :].rearrange("a (p c) n -> (a p) (c n)", p=P))\
                  .then_inc(arrived, 16)

            def weights_load(e, k):
                expert_weights(e, k, e_w[k])

            def out_load(q, k):
                wait(sp, p2_low, q - 1)
                sp.dma_start(wraw[k][:, :, :], A["w_out"][at(q)].rearrange("a p k m -> (a p) k m"))\
                  .then_inc(p2_w[k], 16)

            def gate_load(q, which, k):
                wait(sp, mixed, q - 1)
                m = q - KC * which
                sp.dma_start(tg[k][:, :], scr_gate[at(m), which, :, :].rearrange("a p m -> (a p) m"))\
                  .then_inc(g_in[k], 16)

            for k in range(2):
                sp.wait_ge(w_low, TILES * HEADS - 2 + k)
                out_load(k, k)
            sp.wait_ge(gate_out, 32 * HEADS)
            sp.wait_ge(s["yb_set"], HEADS)
            for k in range(2):
                gate_load(k, 0, k)
            with sp.Fori(1, KC // 2) as j:
                for k in range(2):
                    out_load(2 * j + k, k)
                    gate_load(2 * j + k, 0, k)
            with sp.Fori(KC // 2, KC) as j:
                for k in range(2):
                    out_load(2 * j + k, k)
                    gate_load(2 * j + k, 1, k)
            for k in range(2):
                out_load(2 * KC + k, k)
            sp.wait_ge(y_done, 32)
            sp.wait_ge(mixed, 16)
            sp.wait_ge(m_sum, KC)
            sp.wait_ge(m_low, KC)
            for k in range(2):
                weights_load(k, k)
            sp.dma_start(x2[:, 0:4, :], A["x"][0:PROMPT, :].rearrange("(c p) d -> p c d", p=P)).then_inc(x2_in, 16)
            sp.dma_start(x2[0:STREAM, 4, :], A["x"][PROMPT:TOK, :]).then_inc(x2_in, 16)
            with sp.Fori(KC + 1, KC + KC // 2) as j:
                for k in range(2):
                    out_load(2 * j + k, k)
            sp.wait_ge(y_done, 48)
            sp.dma_start(g2row[:, :], A["g2row"]).then_inc(p3_in, 16)
            sp.dma_start(wr[:, :, :], A["w_router"]).then_inc(p3_in, 16)
            sp.wait_ge(x2_set, 8)
            sp.dma_start(scr_x2.rearrange("(c p) d -> p c d", p=P), x2[:, :, :]).then_inc(nx["out"], 16)

            def rows_load(b, k):
                r = sp.value_load(table[0:1, at(b)], min_val=0, max_val=SLOTS)
                sp.dma_start(xb[k][0:BR, :], scr_rows[at(r, BR), :]).then_inc(e_x[k], 16)

            def y_store(b, k):
                sp.wait_ge(e_y, b + 1)
                sp.dma_start(scr_y[at(b * BR, BR), :], yout[k][0:BR, :]).then_inc(e_out[k], 16)

            sp.wait_ge(route, R_PLACES + 1)
            sp.wait_ge(spread_rows, 16 * 2 * UNITS)
            sp.wait_ge(nx["out"], 16)
            for k in range(2):
                rows_load(k, k)

            def next_load(b, k):
                sp.wait_ge(e_xt, b - 1)
                rows_load(b, k)
                sp.wait_ge(e_low, 2 * (b - 1))
                weights_load(b, k)

            for k in range(2):
                next_load(2 + k, k)
            with sp.Fori(2, EXPERTS // 2) as i:
                for k in range(2):
                    next_load(2 * i + k, k)
                    y_store(2 * i + k - 4, k)
            for b in range(EXPERTS - 4, EXPERTS):
                y_store(b, b % 2)
            sp.wait_ge(e_low, 2 * EXPERTS)

            def further(j):
                e = sp.value_load(table[0:1, at(j + TB_EXPERT)], min_val=0, max_val=EXPERTS - 1)
                r = sp.value_load(table[0:1, at(j + TB_ROW)], min_val=0, max_val=SLOTS)
                sp.wait_ge(e_y, j + EXPERTS)
                sp.dma_start(xb[0][0:BR, :], scr_rows[at(r, BR), :]).then_inc(o_x, 16)
                expert_weights(e, 0, o_w)
                sp.wait_ge(e_y, j + (EXPERTS + 1))
                sp.dma_start(scr_y[at((j + EXPERTS) * BR, BR), :], yout[0][0:BR, :]).then_inc(o_out, 16)

            further_blocks(sp, further)
            for c in range(UNITS):
                rows = frames(c).stop
                sp.dma_start(fx[c][0:rows, :], scr_x2[c * P:c * P + rows, :]).then_inc(f_x, 16)
            sp.wait_ge(e_dn, EXPERTS)
            sp.dma_start(fgrow[:, :], A["final_row"]).then_inc(f_x, 16)
            sp.wait_ge(f_out, 16 * UNITS)
            sp.wait_ge(s["s_out"], 32 * HEADS)
            sp.wait_ge(tails_out, 16)

        @block.gpsimd
        def _(pool):
            pool.memset(epsq[:, 0:1], EPS * P)
            pool.memset(epsq[:, 1:2], EPS).then_inc(zeroed, 1)
            pool.wait_ge(zeroed, 1)
            pool.memset(xin[4][STREAM:P, :], 0.0).then_inc(zeroed, 1)
            pool.wait_ge(zeroed, 2)
            pool.memset(zero[:, :], 0.0).then_inc(zero_set, 1)
            pool.wait_ge(zero_set, 1)
            pool.wait_ge(x_scaled, UNITS)
            pool.memset(raw[:, :, 0:3], 0.0)
            pool.memset(ubuf[:, 0:2], 0.0)
            pool.memset(sil[:, :, TOK:UW], 0.0).then_inc(zeroed, 1)
            pool.wait_ge(par_in, 16 * 3)
            proj_pool(pool, 0)
            tails_pool(pool, 0, 0)
            tails_pool(pool, 0, 1)
            pool.wait_ge(dec_dve, DEC_STEPS)
            pool.wait_ge(dec_act, DEC_ACTS)
            with pool.Fori(1, HEADS) as i:
                proj_pool(pool, i)
                gdn_pool(pool, i - 1)
                tails_pool(pool, i, 0)
                tails_pool(pool, i, 1)
            gdn_pool(pool, HEADS - 1)
            pool.wait_ge(tail_kept, 2 * HEADS)
            pool.dma_start(O["tails"], tails[:, :, :]).then_inc(tails_out, 16)
            pool.wait_ge(s["s_out"], 32 * HEADS)
            pool.wait_ge(tails_out, 16)
            pool.wait_ge(y_done, 32)
            pool.memset(oT[0][:, TOK:UW], 0.0)
            pool.memset(oT[1][:, TOK:UW], 0.0).then_inc(oT_zero, 1)
            pool.wait_ge(oT_zero, 1)
            pool.memset(x2[STREAM:P, 4, :], 0.0).then_inc(oT_zero, 1)
            pool.wait_ge(route, R_PLACES)
            pool.wait_ge(nx["scaled"], UNITS)
            for c in range(UNITS):
                rows = frames(c).stop
                for k in range(2):
                    pool.indirect_dma_start(
                        scr_rows[0:SLOTS, :],
                        bass.IndirectOffsetOnAxis(slot_row[0:rows, k * UNITS + c:k * UNITS + c + 1], axis=0),
                        tn[0:rows, c, :], None).then_inc(spread_rows, 16)
            pool.wait_ge(spread_rows, 16 * 2 * UNITS)

            pool.wait_ge(route, ROUTE_STEPS)
            pool.wait_ge(e_out[0], 8 * EXPERTS)
            pool.wait_ge(e_out[1], 8 * EXPERTS)
            pool.wait_ge(o_kept, 1)
            for c in range(UNITS):
                rows = frames(c).stop
                for k in range(2):
                    pool.indirect_dma_start(
                        fy[k][c][0:rows, :], None, scr_y[:, :],
                        bass.IndirectOffsetOnAxis(slot_y[0:rows, k * UNITS + c:k * UNITS + c + 1], axis=0))\
                        .then_inc(f_y[c // 2], 16)

        @block.scalar
        def _(act):
            act.wait_ge(zeroed, 1)
            for c in range(UNITS + 1):
                if c < UNITS:
                    act.wait_ge(x_in[c], 16)
                    if c == 4:
                        act.wait_ge(zeroed, 2)
                    wait(act, x_square, c)
                    act.activation(sqx[:, :], xin[c][:, :], ACT.Square, accum_out=small_sb[:, c:c + 1])\
                       .then_inc(x_square, 1)
                    act.wait_ge(x_square, c + 1)
                    act.activation(small_sb[:, 8 + c:9 + c], small_sb[:, c:c + 1], ACT.Sqrt, scale=1.0 / D,
                                   bias=epsq[:, 1:2]).then_inc(x_root, 1)
                if c > 0:
                    act.wait_ge(x_turned, c)
                    act.activation(xnh[:, :, (c - 1) * P:c * P], wide(c - 1)[:, :].rearrange("p (k m) -> p k m", k=KC),
                                   ACT.Copy).then_inc(x_high, 1)
                if c == 3:
                    split_high(act, 0, 0)
            split_high(act, 0, 1)
            act.wait_ge(par_in, 16 * 3)
            act.activation(w16h[:, :, :], w16[:, :, :], ACT.Copy).then_inc(ba_w, 1)
            act.wait_ge(zeroed, 3)
            act.wait_ge(ba_w, 2)
            for p in range(POS):
                proj_scalar(act, p, 0)
                if p in DECAY_AT:
                    decays_scalar(act, DECAY_AT[p])
            act.wait_ge(zero_out, 32)
            with act.Fori(1, HEADS - 1) as i:
                for p in range(POS):
                    proj_scalar(act, p, i)
                    gdn_scalar(act, p, i - 1)
            for p in range(POS):
                proj_scalar(act, p, HEADS - 1, last=True)
                gdn_scalar(act, p, HEADS - 2)
            for p in range(POS):
                gdn_scalar(act, p, HEADS - 1)
            phase2_scalar(act)
            phase3_scalar(act)
            phase4_scalar(act)
            phase5_scalar(act)

        @block.vector
        def _(dve):
            for c in range(UNITS + 1):
                if c < UNITS:
                    dve.wait_ge(x_root, c + 1)
                    dve.reciprocal(small_sb[:, 16 + c:17 + c], small_sb[:, 8 + c:9 + c]).then_inc(x_recip, 1)
                    dve.wait_ge(x_recip, c + 1)
                    if c == 0:
                        dve.wait_ge(g1_in, 16)
                    dve.scalar_tensor_tensor(xin[c][:, :], xin[c][:, :], small_sb[:, 16 + c:17 + c], g1row[:, :],
                                             ALU.mult, ALU.mult).then_inc(x_scaled, 1)
                if c > 0:
                    dve.wait_ge(x_high, c)
                    u = slice((c - 1) * P, c * P)
                    dve.tensor_tensor(xnl[:, :, u], wide(c - 1)[:, :].rearrange("p (k m) -> p k m", k=KC),
                                      xnh[:, :, u].bitcast(F32), ALU.subtract).then_inc(x_low, 1)
                if c == 3:
                    split_low(dve, 0, 0)
            split_low(dve, 0, 1)
            dve.wait_ge(ba_w, 1)
            dve.tensor_tensor(w16l[:, :, :], w16[:, :, :], w16h[:, :, :].bitcast(F32), ALU.subtract).then_inc(ba_w, 1)
            dve.wait_ge(zeroed, 3)
            for p in range(POS):
                proj_vector(dve, p, 0)
                if p in DECAY_AT:
                    decays_vector(dve, DECAY_AT[p])
            with dve.Fori(1, HEADS - 1) as i:
                for p in range(POS):
                    proj_vector(dve, p, i)
                    gdn_vector(dve, p, i - 1)
            for p in range(POS):
                proj_vector(dve, p, HEADS - 1, last=True)
                gdn_vector(dve, p, HEADS - 2)
            for p in range(POS):
                gdn_vector(dve, p, HEADS - 1)
            phase2_vector(dve)
            phase3_vector(dve)
            phase4_vector(dve)
            phase5_vector(dve)

        @block.tensor
        def _(pe):
            phase0_tensor(pe)
            for p in range(POS):
                proj_tensor(pe, p, 0)
                if p == BETAS_AT:
                    betas_tensor(pe)
                if p == SUMS_AT:
                    decays_tensor(pe)
            with pe.Fori(1, HEADS) as i:
                for p in range(POS):
                    proj_tensor(pe, p, i)
                    gdn_tensor(pe, p, i - 1)
            for p in range(POS):
                gdn_tensor(pe, p, HEADS - 1)
            phase2_tensor(pe)
            phase3_tensor(pe)
            phase4_tensor(pe)


def constants():
    i, j = np.arange(P)[:, None], np.arange(P)[None, :]
    parts = [i == j, i <= j, i >= j, np.ones((P, P)), i < j]
    for k in range(LEVELS + 1):
        b = 2 ** k
        cut = (i // (2 * b) == j // (2 * b)) & ((i // b) % 2 == 1) & ((j // b) % 2 == 0)
        parts.append(-cut.astype(np.float32))
    valid = np.ones((P, UNITS))
    valid[STREAM:, UNITS - 1] = 0
    return np.concatenate([np.asarray(p, np.float32) for p in parts], axis=1), valid.astype(np.float32)


def rows128(a):
    a = np.asarray(a)
    return np.moveaxis(a.reshape(a.shape[:-1] + (-1, P)), -1, 0)


def tiles_of(w):
    w = np.asarray(w)
    return w.reshape(KC, P, -1, P).transpose(2, 1, 0, 3)


def kernel(x_prompt, x_sample, cache_conv_a, cache_conv_qkv, state_gdn, norm1_g, w_in, conv_a_w, w_out_a,
           conv_qkv_w, a_log, dt_bias, onorm_g, w_out_b, w_o, norm2_g, w_router_group, b_router_group,
           w_router_expert, b_router_expert, w_gate, w_up, w_down, final_g):
    import concourse.bacc as bacc
    from concourse.bass_utils import run_bass_kernel_spmd

    table, valid = constants()

    def spread(row):
        return np.broadcast_to(np.asarray(row).reshape(1, -1), (P, np.asarray(row).size))

    iota = spread(np.arange(40, dtype=np.float32))
    consts = np.concatenate([table, valid, spread(a_log[0]), spread(dt_bias[0]),
                             spread(b_router_group[0]), spread(b_router_expert[0]), iota], axis=1)
    w_in = np.asarray(w_in)[0]
    qkv = 3 * D
    z = 6 * D
    ba = 7 * D
    gates = 7 * D + 2 * HEADS
    starts = {TQ: qkv, TK: qkv + D, TV: qkv + 2 * D, TZ: z, TGA: gates, TGB: gates + D, TH: 0, TC: 2 * D, TB: D}
    by_kind = np.stack([tiles_of(w_in[:, starts[t]:starts[t] + D]) for t in range(TILES)], axis=1)
    params = np.concatenate([
        rows128(conv_qkv_w[0].reshape(4, 3, D)).transpose(0, 3, 2, 1).reshape(P, HEADS, 12),
        rows128(conv_a_w[0]).transpose(0, 2, 1),
        rows128(np.asarray(cache_conv_qkv)[0, 0].reshape(3, 3, D)).transpose(0, 3, 2, 1).reshape(P, HEADS, 9),
        rows128(np.asarray(cache_conv_a)[0, 0]).transpose(0, 2, 1)], axis=2)
    arrays = {
        "x": np.concatenate([np.asarray(x_prompt)[0], np.asarray(x_sample)[0]], axis=0),
        "consts": consts,
        "onorm": rows128(onorm_g[0]),
        "g1row": spread(norm1_g[0]),
        "params": params,
        "w16": w_in[:, ba:gates].reshape(KC, P, 16).transpose(1, 0, 2),
        "w_in": by_kind.reshape(HEADS * TILES, P, KC, P),
        "w_out": np.concatenate([tiles_of(w_out_a[0]), tiles_of(w_out_b[0]), tiles_of(w_o[0])], axis=0),
        "state": np.asarray(state_gdn)[0, 0],
        "g2row": spread(norm2_g[0]),
        "final_row": spread(final_g),
        "w_router": np.concatenate([np.asarray(w_router_group)[0], np.asarray(w_router_expert)[0]], axis=1)
        .reshape(KC, P, GROUPS + EXPERTS).transpose(1, 0, 2),
        "w_gate": np.asarray(w_gate)[0], "w_up": np.asarray(w_up)[0], "w_down": np.asarray(w_down)[0],
    }
    outs = {"y": (TOK, D), "tails": (P, HEADS, 22), "gdn_prompt": (HEADS, P, P), "gdn_sample": (HEADS, P, P)}
    nc = bacc.Bacc("TRN2", target_bir_lowering=False, num_devices=1)
    feeds, A, O = {}, {}, {}
    for name, a in arrays.items():
        feeds["in_" + name] = a = np.ascontiguousarray(a)
        A[name] = nc.dram_tensor("in_" + name, a.shape, mybir.dt.from_np(a.dtype), kind="ExternalInput").ap()
    for name, shape in outs.items():
        O[name] = nc.dram_tensor("out_" + name, shape, F32, kind="ExternalOutput").ap()
    encoder_layer(nc, A, O)
    r = run_bass_kernel_spmd(nc, [feeds], core_ids=[0]).results[0]
    y, tails = r["out_y"], r["out_tails"]

    def last_rows(columns, kinds, count):
        t = tails[:, :, columns].reshape(P, HEADS, kinds, count).transpose(3, 2, 1, 0)
        return np.ascontiguousarray(t.reshape(1, 1, count, kinds * HEADS * P))

    return (y[None, :PROMPT], y[None, PROMPT:], last_rows(slice(18, 20), 1, 2), last_rows(slice(0, 9), 3, 3),
            r["out_gdn_prompt"][None, None], last_rows(slice(20, 22), 1, 2), last_rows(slice(9, 18), 3, 3),
            r["out_gdn_sample"][None, None])
```

```python
from contextlib import ExitStack

import numpy as np

import concourse.bass as bass
from concourse import mybir

F32 = mybir.dt.float32
F32R = mybir.dt.float32r
I32 = mybir.dt.int32
ALU = mybir.AluOpType
ACT = mybir.ActivationFunctionType
X = mybir.AxisListType.X

P = 128
D = 1024
KC = D // P
PROMPT, STREAM = 512, 64
TOK = PROMPT + STREAM
HALF = TOK // 2
UNITS = 5
UW = UNITS * P
HEADS = 8
EPS = 1e-6
LEVELS = 6
GROUPS, PER_GROUP = 4, 8
EXPERTS = GROUPS * PER_GROUP
DE = 256
SLOTS = 2 * TOK
BR = 80
OVER = (SLOTS - 2) // BR
BLOCKS = EXPERTS + OVER
ROWS = SLOTS + BR
TB_FIRST, TB_EXPERT, TB_ROW, TB_COUNT = 0, EXPERTS, EXPERTS + OVER, EXPERTS + 2 * OVER

TQ, TK, TV, TZ, TGA, TGB, TH, TC, TB = range(9)
TILES = 9
PER = 3
POS = 2 * TILES * PER
ACT_HALVES = 2 * TC
DVE_HALVES = 2 * TILES - ACT_HALVES

PAR_QKV, PAR_A, PAR_CQKV, PAR_CA, PARS = 0, 12, 15, 24, 26
KBETA, KSUM, KEXP, KBEXP, KREST, KLAST, KINDS = range(7)
BETAS_AT, TURNED_AT, SUMS_AT = 8, 14, 29
DECAY_AT = {9: None, 16: 0, 32: 1}
DEC_STEPS, DEC_ACTS = 11, 7
R_PAIRS, R_GAP, R_PLACES, ROUTE_STEPS = 23, 25, 32, 59 + (TOK - 1) // BR
C_ID, C_UPPER, C_LOWER, C_ONES, C_BEFORE, C_LEVEL = (P * k for k in range(6))
C_MISC = C_LEVEL + P * (LEVELS + 1)
M_VALID, M_ALOG, M_DT, M_RBIAS, M_IOTA, M_END = 0, 5, 13, 21, 57, 57 + 40
CONSTS = C_MISC + M_END


def wait(engine, sem, value):
    if not isinstance(value, int) or value > 0:
        engine.wait_ge(sem, value)


def at(index, length=1):
    return bass.ds(index, length)


PIECES = [[(0, HALF, 0, False)], [(0, PROMPT - HALF, HALF, False), (PROMPT - HALF, STREAM, 0, True)]]


def padded(first, stream, pad):
    return first + (PROMPT + 2 * pad if stream else pad)


def encoder_layer(nc, A, O):
    scr_gate = nc.dram_tensor("scr_gate", (HEADS, 2, P, TOK), F32, kind="Internal").ap()
    scr_x2 = nc.dram_tensor("scr_x2", (UNITS * P, D), F32, kind="Internal").ap()
    scr_rows = nc.dram_tensor("scr_rows", (ROWS, D), F32, kind="Internal").ap()
    scr_y = nc.dram_tensor("scr_y", (BLOCKS * BR, D), F32, kind="Internal").ap()

    top = ExitStack()
    with top:
        def sem(name):
            return top.enter_context(nc.semaphore(name))

        def sb(ctx, name, shape, dt=F32):
            return ctx.enter_context(nc.sbuf_tensor(name, shape, dt))

        proj = [top.enter_context(nc.psum_tensor(f"proj{k}", [P, 512], F32)) for k in range(3)]
        wideA = top.enter_context(nc.psum_tensor("wideA", [P, 1024], F32))
        wideB = top.enter_context(nc.psum_tensor("wideB", [P, 1024], F32))
        small = top.enter_context(nc.psum_tensor("small", [P, 512], F32))

        const = sb(top, "const", [P, CONSTS])
        ident = const[:, C_ID:C_ID + P]
        upper = const[:, C_UPPER:C_UPPER + P]
        ones = const[:, C_ONES:C_ONES + P]
        before = const[:, C_BEFORE:C_BEFORE + P]

        def level_mask(k):
            c = C_LEVEL + P * k
            return const[:, c:c + P].unsqueeze(1).to_broadcast([P, UNITS, P])

        lower_mask = const[:, C_LOWER:C_LOWER + P].unsqueeze(1).to_broadcast([P, UNITS, P])
        misc = const[:, C_MISC:CONSTS]
        small_sb = sb(top, "stats", [P, 64])
        epsq = small_sb[:, 60:62]
        coef = sb(top, "coef", [P, 2, UNITS])
        slot_row = sb(top, "slot_row", [P, 2 * UNITS], I32)
        slot_y = sb(top, "slot_y", [P, 2 * UNITS], I32)
        table = sb(top, "block_table", [1, TB_COUNT + 1], I32)

        ph1 = ExitStack()
        xnh = sb(ph1, "xnh", [P, KC, UW], F32R)
        xnl = sb(ph1, "xnl", [P, KC, UW], F32R)
        wraw = [sb(ph1, f"wraw{k}", [P, KC, P]) for k in range(3)]
        whi = [sb(ph1, f"whi{k}", [P, KC, P], F32R) for k in range(3)]
        wlo = [sb(ph1, f"wlo{k}", [P, KC, P], F32R) for k in range(3)]
        g0 = ExitStack()
        xin = [sb(g0, f"xin{c}", [P, D]) for c in range(UNITS)]
        sqx = sb(g0, "sqx", [P, D])
        w16 = sb(g0, "w16", [P, KC, 16])
        w16h = sb(g0, "w16h", [P, KC, 16], F32R)
        w16l = sb(g0, "w16l", [P, KC, 16], F32R)
        zero = sb(g0, "zero", [P, D])
        g0.close()
        yab = ExitStack()
        ya = sb(yab, "ya", [P, HEADS, TOK])
        yb = sb(yab, "yb", [P, HEADS, TOK])
        gd = ExitStack()
        raw = sb(gd, "raw", [P, 3, TOK + 6])
        ubuf = sb(gd, "ubuf", [P, TOK + 4])
        aout = sb(gd, "aout", [P, TOK + 2])
        cout = [sb(gd, f"cout{k}", [P, TOK + 3]) for k in range(2)]
        sil = sb(gd, "sil", [P, 3, UW])
        gate = [sb(gd, f"gate{k}", [P, TOK]) for k in range(2)]
        par = sb(gd, "par", [P, HEADS, PARS])
        pcur = sb(gd, "pcur", [P, PAR_CQKV])
        dec = sb(gd, "dec", [P, HEADS, KINDS, UNITS])
        gcur = sb(gd, "gcur", [P, KINDS, UNITS])
        onorm = sb(gd, "onorm", [P, 1])
        tails = sb(gd, "tails", [P, HEADS, 22])
        buf1 = sb(gd, "buf1", [P, 2 * UW])
        buf2 = sb(gd, "buf2", [P, 2 * UW])
        buf3 = sb(gd, "buf3", [P, 2 * UW])
        vbeta = sb(gd, "vbeta", [P, UW])
        kbexp = sb(gd, "kbexp", [P, UW])
        krest = sb(gd, "krest", [P, UW])
        kT = sb(gd, "kT", [P, UW])
        qT = sb(gd, "qT", [P, UW])
        T = sb(gd, "T", [P, UW])
        TT = sb(gd, "TT", [P, UW])
        vn = sb(gd, "vn", [P, UW])
        Sp = sb(gd, "Sp", [P, P])
        Ss = sb(gd, "Ss", [P, P])
        st = sb(gd, "st", [P, 40])
        dtmp = sb(gd, "dtmp", [P, 8, UNITS * HEADS])
        basb = sb(gd, "basb", [P, UNITS, 16])
        gd.close()
        g1 = ExitStack()
        g1row = sb(g1, "g1row", [P, D])
        g1.close()

        yab.close()
        ph1.close()
        areas = [0]

        def area(start):
            areas[0] += 1
            ctx = ExitStack()
            if start:
                sb(ctx, f"below_area{areas[0]}", [P, start])
            return ctx

        BRANCH = KC * TOK
        AT_YA = 2 * KC * UW + 9 * D
        AT_YB = AT_YA + BRANCH
        AT_GD = AT_YB + BRANCH
        AT_ML = AT_GD + UNITS * D
        AT_MIX = AT_ML + BRANCH
        EW = 24 * DE
        AT_P3 = EW
        a2 = area(AT_YA)
        mh = sb(a2, "mh", [P, KC, TOK], F32R)
        ybl = sb(a2, "ybl", [P, KC, TOK], F32R)
        ybh = sb(a2, "ybh", [P, KC, TOK], F32R)
        a2.close()
        a2 = area(AT_GD)
        x2 = sb(a2, "x2", [P, UNITS, D])
        ml = sb(a2, "ml", [P, KC, TOK], F32R)
        tg = [sb(a2, f"tg{k}", [P, TOK]) for k in range(2)]
        mix = [sb(a2, f"mix{k}", [P, TOK]) for k in range(2)]
        a2.close()
        a2 = area(AT_MIX)
        oT = [sb(a2, f"oT{k}", [P, UW]) for k in range(2)]
        a2.close()
        p3 = area(AT_P3)
        g2row = sb(p3, "g2row", [P, D])
        wr = sb(p3, "wr", [P, KC, GROUPS + EXPERTS])
        tn = sb(p3, "tn", [P, UNITS, D])
        tT = [sb(p3, f"tT{k}", [P, D]) for k in range(2)]
        sqs = sb(p3, "sqs", [P, D])
        lg = sb(p3, "lg", [P, UNITS, GROUPS + EXPERTS])
        r4 = [sb(p3, f"r4_{k}", [P, UNITS, GROUPS]) for k in range(4)]
        r8 = [sb(p3, f"r8_{k}", [P, UNITS, PER_GROUP]) for k in range(5)]
        r5 = sb(p3, "r5", [P, 12, UNITS])
        pair = sb(p3, "pair", [P, 2, UNITS, EXPERTS])
        pick = sb(p3, "pick", [P, 2, UNITS, EXPERTS])
        r32 = [sb(p3, f"r32_{k}", [P, UNITS, EXPERTS]) for k in range(3)]
        ex = sb(p3, "ex", [P, 6, EXPERTS])
        bt = sb(p3, "bt", [P, 3, OVER, EXPERTS])
        brow = sb(p3, "brow", [P, 3, OVER])
        eraw, ehi, elo = [None, None], [None, None], [None, None]
        ehi[0] = sb(p3, "ehi0", [P, EW], F32R)
        xb = [sb(p3, f"xb{k}", [P, D]) for k in range(2)]
        xbh = [sb(p3, f"xbh{k}", [P, KC, BR], F32R) for k in range(2)]
        xbl = [sb(p3, f"xbl{k}", [P, KC, BR], F32R) for k in range(2)]
        yout = [sb(p3, f"yout{k}", [P, D]) for k in range(2)]
        p3.close()
        p4 = area(0)
        eraw[0] = sb(p4, "eraw0", [P, EW])
        ehi[1] = sb(p4, "ehi1", [P, EW], F32R)
        elo[1] = sb(p4, "elo1", [P, EW], F32R)
        p4.close()
        p4 = area(AT_ML)
        elo[0] = sb(p4, "elo0", [P, EW], F32R)
        eraw[1] = sb(p4, "eraw1", [P, EW])
        hgate = [sb(p4, f"hgate{k}", [P, DE]) for k in range(2)]
        hid = [sb(p4, f"hid{k}", [P, DE]) for k in range(2)]
        hth = [sb(p4, f"hth{k}", [P, 2, BR], F32R) for k in range(2)]
        htl = [sb(p4, f"htl{k}", [P, 2, BR], F32R) for k in range(2)]
        p4.close()
        p5 = area(EW)
        fy = [[sb(p5, f"fy{j}_{c}", [P, D]) for c in range(UNITS)] for j in range(2)]
        fsq = sb(p5, "fsq", [P, D])
        p5.close()
        p5 = area(AT_ML + EW)
        fx = [sb(p5, f"fx{c}", [P, D]) for c in range(UNITS)]
        fgrow = sb(p5, "fgrow", [P, D])
        p5.close()

        ident_in, const_in, g1_in = sem("ident_in"), sem("const_in"), sem("g1_in")
        par_in = sem("par_in")
        x_in = [sem(f"x_in{c}") for c in range(UNITS)]
        zeroed = sem("zeroed")
        x_square, x_root, x_recip, x_scaled = (sem(f"x_{s}") for s in ("square", "root", "recip", "scaled"))
        x_turned, x_high, x_low = (sem(f"x_{s}") for s in ("turned", "high", "low"))
        ba_w, ba_done, ba_out = sem("ba_w"), sem("ba_done"), sem("ba_out")
        dec_act, dec_dve, dec_pe = sem("dec_act"), sem("dec_dve"), sem("dec_pe")
        w_in = [sem(f"w_in{k}") for k in range(3)]
        w_high, w_low = sem("w_high"), sem("w_low")
        proj_done = sem("proj_done")
        act_half, dve_half = sem("act_half"), sem("dve_half")
        conv_step, conv_silu = sem("conv_step"), sem("conv_silu")
        gate_out = sem("gate_out")
        a_step = sem("a_step")
        pars_set, tail_kept, gdec_set = sem("pars_set"), sem("tail_kept"), sem("gdec_set")
        names = """qk_turned v_turned sums_spread hats_turned grams a_turned t_turned0 at_done tat_done
            t_turned uw_done ws_done kv_done o_turned
            qk_raw qk_square qk_root decay hats_T a_T tt0 tt_set w_set o_inter o_square o_root
            qk_sum qk_recip hats v_scaled dgap dclip decay_cut a_cut a_scaled t_cut t_set0 x_set t_set u_set
            vn_set s_set o_set o_sum o_recip o_scaled yb_set
            kbexp_set krest_set s_zero s_in s_out""".split()
        s = {n: sem(n) for n in names}
        tails_out = sem("tails_out")

        U = [slice(u * P, (u + 1) * P) for u in range(UNITS)]
        scan0 = 20 + 3 * LEVELS

        def spread(kind):
            return gcur[:, kind, :].unsqueeze(2).to_broadcast([P, UNITS, P])

        def units(ap):
            return ap.rearrange("p (u m) -> p u m", m=P)

        def gdn_tensor(pe, p, g):
            n = g + 1
            if p == 0:
                pe.wait_ge(conv_silu, 3 * g + 2)
                wait(pe, s["yb_set"], g)
                wait(pe, s["o_set"], g)
                for u in range(UNITS):
                    pe.transpose(wideA[:, U[u]], sil[:, 0, U[u]], ident)
                for u in range(UNITS):
                    mm = pe.transpose(wideB[:, U[u]], sil[:, 1, U[u]], ident)
                mm.then_inc(s["qk_turned"], 1)
            if p == 2:
                pe.wait_ge(conv_silu, 3 * g + 3)
                pe.wait_ge(s["qk_raw"], n)
                for u in range(UNITS):
                    mm = pe.transpose(wideA[:, U[u]], sil[:, 2, U[u]], ident)
                mm.then_inc(s["v_turned"], 1)
            if p == 4:
                pe.wait_ge(s["v_scaled"], n)
                pe.wait_ge(gdec_set, n)
                for u in range(UNITS):
                    mm = pe.transpose(wideA[:, U[u]], gcur[:, KSUM, u:u + 1].to_broadcast([P, P]), ident)
                mm.then_inc(s["sums_spread"], 1)
            if p == 8:
                pe.wait_ge(s["hats"], n)
                pe.wait_ge(s["dgap"], n)
                for u in range(UNITS):
                    pe.transpose(wideA[:, U[u]], buf3[:, u * P:(u + 1) * P], ident)
                for u in range(UNITS):
                    mm = pe.transpose(wideB[:, U[u]], buf3[:, UW + u * P:UW + (u + 1) * P], ident)
                mm.then_inc(s["hats_turned"], 1)
            if p == 11:
                pe.wait_ge(s["hats_T"], n)
                for u in range(UNITS):
                    pe.matmul(wideA[:, U[u]], qT[:, U[u]], kT[:, U[u]], start=True, stop=True)
                for u in range(UNITS):
                    mm = pe.matmul(wideB[:, U[u]], kT[:, U[u]], kT[:, U[u]], start=True, stop=True)
                mm.then_inc(s["grams"], 1)
            if p == 15:
                pe.wait_ge(s["a_scaled"], n)
                for u in range(UNITS):
                    pe.transpose(wideA[:, U[u]], buf1[:, u * P:(u + 1) * P], ident)
                for u in range(UNITS):
                    mm = pe.transpose(wideB[:, U[u]], buf1[:, UW + u * P:UW + (u + 1) * P], ident)
                mm.then_inc(s["a_turned"], 1)
            if p == 17:
                pe.wait_ge(s["t_set0"], n)
                pe.wait_ge(s["a_T"], n)
                for u in range(UNITS):
                    mm = pe.transpose(wideA[:, U[u]], T[:, U[u]], ident)
                mm.then_inc(s["t_turned0"], 1)
            if 19 <= p < 19 + 3 * LEVELS:
                k, step = divmod(p - 19, 3)
                done = g * LEVELS + k
                if step == 0:
                    if k > 0:
                        pe.wait_ge(s["tt_set"], done)
                    for u in range(UNITS):
                        mm = pe.matmul(wideB[:, U[u]], buf3[:, UW + u * P:UW + (u + 1) * P], T[:, U[u]],
                                       start=True, stop=True)
                    mm.then_inc(s["at_done"], 1)
                elif step == 1:
                    pe.wait_ge(s["x_set"], done + 1)
                    if k == 0:
                        pe.wait_ge(s["tt0"], n)
                    for u in range(UNITS):
                        mm = pe.matmul(wideA[:, U[u]], TT[:, U[u]], buf2[:, UW + u * P:UW + (u + 1) * P],
                                       start=True, stop=True)
                    mm.then_inc(s["tat_done"], 1)
                else:
                    pe.wait_ge(s["t_set"], done + 1)
                    for u in range(UNITS):
                        mm = pe.transpose(wideB[:, U[u]], T[:, U[u]], ident)
                    mm.then_inc(s["t_turned"], 1)
            if p == scan0 - 1:
                pe.wait_ge(s["tt_set"], LEVELS * n)
                pe.wait_ge(s["kbexp_set"], n)
                for u in range(UNITS):
                    pe.matmul(wideA[:, U[u]], TT[:, U[u]], vbeta[:, U[u]], start=True, stop=True)
                for u in range(UNITS):
                    mm = pe.matmul(wideB[:, U[u]], kbexp[:, U[u]], TT[:, U[u]], start=True, stop=True)
                mm.then_inc(s["uw_done"], 1)
            if scan0 + 1 <= p < scan0 + 9:
                c, step = divmod(p - scan0 - 1, 2)
                if step == 0:
                    if c == 0:
                        pe.wait_ge(s["w_set"], n)
                        pe.wait_ge(s["s_zero"], n)
                        pe.wait_ge(s["s_in"], 16 * n)
                        wait(pe, s["o_inter"], 4 * g)
                    else:
                        pe.wait_ge(s["s_set"], 4 * g + c)
                        pe.wait_ge(s["o_inter"], 4 * g + c)
                    mm = None
                    for u, state, o in [(c, Sp, 0)] + ([(4, Ss, 2 * P)] if c == 0 else []):
                        pe.matmul(small[:, o:o + P], buf1[:, UW + u * P:UW + (u + 1) * P], state[:, :],
                                  start=True, stop=True)
                        mm = pe.matmul(small[:, o + P:o + 2 * P], qT[:, U[u]], state[:, :], start=True, stop=True)
                    mm.then_inc(s["ws_done"], 1)
                else:
                    pe.wait_ge(s["vn_set"], 4 * g + c + 1)
                    pe.wait_ge(s["krest_set"], n)
                    for u, o in [(c, 0)] + ([(4, P)] if c == 0 else []):
                        pe.matmul(wideB[:, U[u]], buf3[:, u * P:(u + 1) * P], vn[:, U[u]], start=True, stop=True)
                        mm = pe.matmul(wideA[:, o:o + P], krest[:, U[u]], vn[:, U[u]], start=True, stop=True)
                    mm.then_inc(s["kv_done"], 1)
            if p == 52:
                pe.wait_ge(s["o_scaled"], n)
                for u in range(UNITS):
                    mm = pe.transpose(wideA[:, U[u]], vn[:, U[u]], ident)
                mm.then_inc(s["o_turned"], 1)

        def gdn_scalar(act, p, g):
            n = g + 1
            if p == 0:
                act.wait_ge(s["qk_turned"], n)
                wait(act, s["uw_done"], g)
                wait(act, s["kv_done"], 4 * g)
                act.activation(buf1[:, 0:UW], wideA[:, 0:UW], ACT.Copy)
                act.activation(buf1[:, UW:2 * UW], wideB[:, 0:UW], ACT.Copy).then_inc(s["qk_raw"], 1)
                wait(act, s["o_sum"], g)
                act.wait_ge(s["qk_raw"], n)
                act.activation(buf2[:, :], buf1[:, :], ACT.Square).then_inc(s["qk_square"], 1)
            if p == 3:
                act.wait_ge(s["qk_sum"], n)
                act.activation(st[:, 10:15], st[:, 0:5], ACT.Sqrt, scale=float(P), bias=epsq[:, 0:1])
                act.activation(st[:, 15:20], st[:, 5:10], ACT.Sqrt, bias=epsq[:, 1:2]).then_inc(s["qk_root"], 1)
            if p == 6:
                act.wait_ge(s["dclip"], n)
                act.activation(buf2[:, 0:UW], buf2[:, 0:UW], ACT.Exp, scale=-1.0).then_inc(s["decay"], 1)
            if p == 8:
                act.wait_ge(s["hats_turned"], n)
                act.activation(qT[:, :], wideA[:, 0:UW], ACT.Copy)
                act.activation(kT[:, :], wideB[:, 0:UW], ACT.Copy).then_inc(s["hats_T"], 1)
            if p == 15:
                act.wait_ge(s["a_turned"], n)
                act.wait_ge(s["krest_set"], n)
                act.activation(buf3[:, 0:UW], wideA[:, 0:UW], ACT.Copy)
                act.activation(buf3[:, UW:2 * UW], wideB[:, 0:UW], ACT.Copy).then_inc(s["a_T"], 1)
            if p == 17:
                act.wait_ge(s["t_turned0"], n)
                act.activation(TT[:, :], wideA[:, 0:UW], ACT.Copy).then_inc(s["tt0"], 1)
            if 19 <= p < 19 + 3 * LEVELS and (p - 19) % 3 == 2:
                k = (p - 19) // 3
                act.wait_ge(s["t_turned"], g * LEVELS + k + 1)
                act.activation(TT[:, :], wideB[:, 0:UW], ACT.Copy).then_inc(s["tt_set"], 1)
            if p == scan0 - 1:
                act.wait_ge(s["uw_done"], n)
                act.activation(buf1[:, UW:2 * UW], wideB[:, 0:UW], ACT.Copy).then_inc(s["w_set"], 1)
            if scan0 + 1 <= p < scan0 + 9 and (p - scan0 - 1) % 2 == 0:
                c = (p - scan0 - 1) // 2
                act.wait_ge(s["ws_done"], 4 * g + c + 1)
                act.wait_ge(s["vn_set"], 4 * g + c + 1)
                if c == 0:
                    act.activation(kT[:, U[4]], small[:, 3 * P:4 * P], ACT.Copy, scale=gcur[:, KEXP, 4:5])
                act.activation(kT[:, U[c]], small[:, P:2 * P], ACT.Copy, scale=gcur[:, KEXP, c:c + 1])\
                   .then_inc(s["o_inter"], 1)
            if p == 47:
                act.wait_ge(s["o_set"], n)
                act.activation(buf2[:, 0:UW], vn[:, :], ACT.Square).then_inc(s["o_square"], 1)
            if p == 48:
                act.wait_ge(s["s_set"], 4 * n)
                for name, state in (("gdn_prompt", Sp), ("gdn_sample", Ss)):
                    act.dma_start(O[name][at(g), :, :].rearrange("a k v -> (a k) v"), state[:, :])\
                       .then_inc(s["s_out"], 16)
            if p == 49:
                act.wait_ge(s["o_sum"], n)
                act.activation(st[:, 35:40], st[:, 30:35], ACT.Sqrt, scale=1.0 / P, bias=epsq[:, 1:2])\
                   .then_inc(s["o_root"], 1)

        def gdn_vector(dve, p, g):
            n = g + 1
            if p == 2:
                dve.wait_ge(s["qk_square"], n)
                dve.tensor_reduce(st[:, 0:10], buf2[:, :].rearrange("p (u m) -> p u m", m=P), X, ALU.add)\
                   .then_inc(s["qk_sum"], 1)
                dve.wait_ge(s["v_turned"], n)
                dve.wait_ge(gdec_set, n)
                dve.tensor_tensor(units(vbeta[:, :]), units(wideA[:, 0:UW]), spread(KBETA), ALU.mult)\
                   .then_inc(s["v_scaled"], 1)
            if p == 4:
                dve.wait_ge(s["qk_root"], n)
                dve.reciprocal(st[:, 20:30], st[:, 10:20]).then_inc(s["qk_recip"], 1)
                dve.wait_ge(s["qk_recip"], n)
                dve.tensor_tensor(units(buf3[:, :]), units(buf1[:, :]),
                                  st[:, 20:30].unsqueeze(2).to_broadcast([P, 2 * UNITS, P]), ALU.mult)\
                   .then_inc(s["hats"], 1)
            if p == 5:
                dve.wait_ge(s["sums_spread"], n)
                dve.tensor_tensor(units(buf2[:, 0:UW]), units(wideA[:, 0:UW]), spread(KSUM), ALU.subtract)\
                   .then_inc(s["dgap"], 1)
                dve.wait_ge(s["dgap"], n)
                dve.tensor_scalar(buf2[:, 0:UW], buf2[:, 0:UW], 0.0, None, ALU.max).then_inc(s["dclip"], 1)
            if p == 7:
                dve.wait_ge(s["decay"], n)
                dve.tensor_tensor(units(buf2[:, 0:UW]), units(buf2[:, 0:UW]), lower_mask, ALU.mult)\
                   .then_inc(s["decay_cut"], 1)
            if p == 11:
                dve.wait_ge(s["grams"], n)
                dve.wait_ge(s["decay_cut"], n)
                dve.tensor_tensor(buf1[:, UW:2 * UW], wideB[:, 0:UW], buf2[:, 0:UW], ALU.mult)\
                   .then_inc(s["a_cut"], 1)
                dve.tensor_tensor(buf1[:, 0:UW], wideA[:, 0:UW], buf2[:, 0:UW], ALU.mult)
                dve.wait_ge(s["a_cut"], n)
                dve.tensor_tensor(units(buf1[:, UW:2 * UW]), units(buf1[:, UW:2 * UW]), spread(KBETA), ALU.mult)\
                   .then_inc(s["a_scaled"], 1)
            if p == 13:
                dve.wait_ge(s["a_scaled"], n)
                dve.tensor_tensor(units(T[:, :]), units(buf1[:, UW:2 * UW]), level_mask(0), ALU.mult)\
                   .then_inc(s["t_cut"], 1)
                dve.wait_ge(s["t_cut"], n)
                dve.tensor_tensor(units(T[:, :]), units(T[:, :]),
                                  ident.unsqueeze(1).to_broadcast([P, UNITS, P]), ALU.add).then_inc(s["t_set0"], 1)
            if 19 <= p < 19 + 3 * LEVELS:
                k, step = divmod(p - 19, 3)
                done = g * LEVELS + k
                if step == 0:
                    dve.wait_ge(s["at_done"], done + 1)
                    dve.tensor_tensor(units(buf2[:, UW:2 * UW]), units(wideB[:, 0:UW]), level_mask(k + 1),
                                      ALU.mult).then_inc(s["x_set"], 1)
                elif step == 1:
                    dve.wait_ge(s["tat_done"], done + 1)
                    dve.tensor_tensor(T[:, :], T[:, :], wideA[:, 0:UW], ALU.add).then_inc(s["t_set"], 1)
            if p == scan0 - 1:
                dve.wait_ge(s["uw_done"], n)
                dve.tensor_copy(buf1[:, 0:UW], wideA[:, 0:UW]).then_inc(s["u_set"], 1)
            if scan0 + 1 <= p < scan0 + 9:
                c, step = divmod(p - scan0 - 1, 2)
                if step == 0:
                    dve.wait_ge(s["ws_done"], 4 * g + c + 1)
                    if c == 0:
                        dve.wait_ge(s["u_set"], n)
                        dve.tensor_tensor(vn[:, U[4]], buf1[:, 4 * P:5 * P], small[:, 2 * P:3 * P], ALU.subtract)
                    dve.tensor_tensor(vn[:, U[c]], buf1[:, c * P:(c + 1) * P], small[:, 0:P], ALU.subtract)\
                       .then_inc(s["vn_set"], 1)
                else:
                    dve.wait_ge(s["kv_done"], 4 * g + c + 1)
                    if c == 0:
                        dve.scalar_tensor_tensor(Ss[:, :], Ss[:, :], gcur[:, KLAST, 4:5], wideA[:, P:2 * P],
                                                 ALU.mult, ALU.add)
                    dve.scalar_tensor_tensor(Sp[:, :], Sp[:, :], gcur[:, KLAST, c:c + 1], wideA[:, 0:P],
                                             ALU.mult, ALU.add).then_inc(s["s_set"], 1)
                    if c == 3:
                        dve.wait_ge(s["o_inter"], 4 * n)
                        dve.tensor_tensor(vn[:, :], kT[:, :], wideB[:, 0:UW], ALU.add).then_inc(s["o_set"], 1)
            if p == 48:
                dve.wait_ge(s["o_square"], n)
                dve.tensor_reduce(st[:, 30:35], units(buf2[:, 0:UW]), X, ALU.add).then_inc(s["o_sum"], 1)
            if p == 50:
                dve.wait_ge(s["o_root"], n)
                dve.reciprocal(st[:, 20:25], st[:, 35:40]).then_inc(s["o_recip"], 1)
                dve.wait_ge(s["o_recip"], n)
                dve.tensor_tensor(units(vn[:, :]), units(vn[:, :]),
                                  st[:, 20:25].unsqueeze(2).to_broadcast([P, UNITS, P]), ALU.mult)\
                   .then_inc(s["o_scaled"], 1)
            if p == 53:
                dve.wait_ge(s["o_turned"], n)
                dve.wait_ge(act_half, ACT_HALVES * g + 2 * TZ + 2)
                head = yb[:, at(g), :].rearrange("p a m -> p (a m)")
                dve.scalar_tensor_tensor(head, wideA[:, 0:TOK], onorm[:, 0:1], head, ALU.mult, ALU.mult)\
                   .then_inc(s["yb_set"], 1)

        def gdn_pool(pool, g):
            n = g + 1
            wait(pool, s["yb_set"], g)
            pool.tensor_copy(gcur[:, :, :], dec[:, at(g), :, :].rearrange("p a k u -> p (a k) u"))\
                .then_inc(gdec_set, 1)
            pool.wait_ge(gdec_set, n)
            pool.wait_ge(s["hats"], n)
            pool.tensor_tensor(units(kbexp[:, :]), units(buf3[:, UW:2 * UW]), spread(KBEXP), ALU.mult)\
                .then_inc(s["kbexp_set"], 1)
            wait(pool, s["s_out"], 32 * g)
            pool.tensor_tensor(units(krest[:, :]), units(buf3[:, UW:2 * UW]), spread(KREST), ALU.mult)\
                .then_inc(s["krest_set"], 1)
            pool.memset(Sp[:, :], 0.0).then_inc(s["s_zero"], 1)
            pool.dma_start(Ss[:, :], A["state"][at(g), :, :].rearrange("a k v -> (a k) v")).then_inc(s["s_in"], 16)

        def half_read(h, i):
            if not isinstance(h, int):
                raise TypeError
            if h < 0:
                h, i = h + 2 * TILES, i - 1
            if isinstance(i, int) and i < 0:
                return act_half, 0
            if h < ACT_HALVES:
                return act_half, ACT_HALVES * i + h + 1
            return dve_half, DVE_HALVES * i + h - ACT_HALVES + 1

        def proj_tensor(pe, p, i):
            h, part = divmod(p, PER)
            t, hh = divmod(h, 2)
            if part == 0:
                if hh == 0:
                    pe.wait_ge(w_low, TILES * i + t + 1)
                if isinstance(i, int) and i == 0 and h < 2:
                    pe.wait_ge(x_low, (3, UNITS)[h])
                wait(pe, *half_read(h - 3, i))
            out = proj[h % 3][:, 0:HALF]
            for j in range(8 * part, 8 * part + 8):
                kc, term = divmod(j, 3)
                w = (whi, whi, wlo)[term][t % 3]
                x = (xnh, xnl, xnh)[term]
                mm = pe.matmul(out, w[:, kc, :], x[:, kc, hh * HALF:(hh + 1) * HALF], start=(j == 0), stop=(j == 23))
            if part == PER - 1:
                mm.then_inc(proj_done, 1)

        def split_high(act, i, t):
            act.wait_ge(w_in[t % 3], 16 * (3 * i + t // 3 + 1))
            wait(act, proj_done, 2 * TILES * i + 2 * (t - 2))
            act.activation(whi[t % 3][:, :, :], wraw[t % 3][:, :, :], ACT.Copy).then_inc(w_high, 1)

        def split_low(dve, i, t):
            dve.wait_ge(w_high, TILES * i + t + 1)
            dve.tensor_tensor(wlo[t % 3][:, :, :], wraw[t % 3][:, :, :], whi[t % 3][:, :, :].bitcast(F32),
                              ALU.subtract).then_inc(w_low, 1)

        CONV_AT = {7 + k: (0, k) for k in range(4)} | {13 + k: (1, k) for k in range(4)} | {19 + k: (2, k) for k in range(4)}
        A_AT = {48: 0, 49: 1, 50: 2}
        FIRST_OUT_AT = {45: 0, 51: 1}

        def proj_scalar(act, p, i, last=False):
            h, part = divmod(p, PER)
            t, hh = divmod(h, 2)
            if part == 0 and hh == 0 and not (last and t + 2 >= TILES):
                split_high(act, i, t + 2)
            if last and p in FIRST_OUT_AT:
                out_split_high(act, FIRST_OUT_AT[p], FIRST_OUT_AT[p])
            if part == PER - 1 and t < TC:
                act.wait_ge(proj_done, 2 * TILES * i + h + 1)
                src = proj[h % 3]
                if t in (TQ, TK, TV):
                    wait(act, conv_step, 12 * (i - 1) + 4 * (t - TQ) + 4)
                    wait(act, tail_kept, 2 * (i - 1) + 1)
                    for lo, count, first, stream in PIECES[hh]:
                        c = padded(first, stream, 3)
                        ins = act.activation(raw[:, t - TQ, c:c + count], src[:, lo:lo + count], ACT.Copy)
                elif t == TZ:
                    ins = act.activation(yb[:, at(i), hh * HALF:(hh + 1) * HALF].rearrange("p a m -> p (a m)"),
                                         src[:, 0:HALF], ACT.Silu)
                elif t in (TGA, TGB):
                    wait(act, gate_out, 32 * i)
                    ins = act.activation(gate[t - TGA][:, hh * HALF:(hh + 1) * HALF], src[:, 0:HALF], ACT.Tanh,
                                         scale=0.5)
                else:
                    wait(act, tail_kept, 2 * i)
                    wait(act, a_step, 3 * i)
                    for lo, count, first, stream in PIECES[hh]:
                        c = padded(first, stream, 2)
                        ins = act.activation(ubuf[:, c:c + count], src[:, lo:lo + count], ACT.Copy)
                ins.then_inc(act_half, 1)
                if t in (TGA, TGB) and hh == 1:
                    act.wait_ge(act_half, ACT_HALVES * i + 2 * t + 2)
                    act.dma_start(scr_gate[at(i), t - TGA, :, :].rearrange("a p m -> (a p) m"),
                                  gate[t - TGA][:, :]).then_inc(gate_out, 16)
            if p in (11, 17, 23):
                k = (p - 11) // 6
                act.wait_ge(conv_step, 12 * i + 4 * k + 4)
                if k < 2:
                    wait(act, s["qk_turned"], i)
                else:
                    wait(act, s["v_turned"], i)
                act.activation(sil[:, k, 0:PROMPT], cout[k % 2][:, 0:PROMPT], ACT.Silu)
                act.activation(sil[:, k, PROMPT:TOK], cout[k % 2][:, PROMPT + 3:TOK + 3], ACT.Silu)\
                   .then_inc(conv_silu, 1)

        def proj_vector(dve, p, i, last=False):
            h, part = divmod(p, PER)
            t, hh = divmod(h, 2)
            if part == 0 and hh == 0 and not (last and t + 2 >= TILES):
                split_low(dve, i, t + 2)
            if last and p in FIRST_OUT_AT:
                out_split_low(dve, FIRST_OUT_AT[p], FIRST_OUT_AT[p])
            if p in CONV_AT:
                k, j = CONV_AT[p]
                n = 12 * i + 4 * k + j
                y = cout[k % 2][:, :]
                if j == 0:
                    dve.wait_ge(act_half, ACT_HALVES * i + 2 * k + 2)
                    dve.wait_ge(pars_set, i + 1)
                    wait(dve, conv_silu, 3 * i + k - 1 if k == 2 else 3 * (i - 1) + (3 if k == 0 else 2))
                    dve.tensor_scalar(y, raw[:, k, 0:TOK + 3], pcur[:, 4 * k:4 * k + 1], None, ALU.mult)\
                       .then_inc(conv_step, 1)
                else:
                    dve.wait_ge(conv_step, n)
                    dve.scalar_tensor_tensor(y, raw[:, k, j:j + TOK + 3], pcur[:, 4 * k + j:4 * k + j + 1], y,
                                             ALU.mult, ALU.add).then_inc(conv_step, 1)
            if p in A_AT:
                j = A_AT[p]
                if j == 0:
                    dve.wait_ge(dve_half, DVE_HALVES * i + 2)
                    dve.tensor_scalar(aout[:, :], ubuf[:, 0:TOK + 2], pcur[:, PAR_A:PAR_A + 1], None, ALU.mult)\
                       .then_inc(a_step, 1)
                else:
                    dve.wait_ge(a_step, 3 * i + j)
                    dve.scalar_tensor_tensor(aout[:, :], ubuf[:, j:j + TOK + 2], pcur[:, PAR_A + j:PAR_A + j + 1],
                                             aout[:, :], ALU.mult, ALU.add).then_inc(a_step, 1)
            if part == PER - 1 and t >= TC:
                dve.wait_ge(proj_done, 2 * TILES * i + h + 1)
                src = proj[h % 3]
                if t == TC:
                    dve.wait_ge(act_half, ACT_HALVES * i + 2 * TH + hh + 1)
                else:
                    dve.wait_ge(a_step, 3 * i + 3)
                for lo, count, first, stream in PIECES[hh]:
                    if t == TC:
                        c = padded(first, stream, 2)
                        ins = dve.tensor_tensor(ubuf[:, c:c + count], src[:, lo:lo + count], ubuf[:, c:c + count],
                                                ALU.mult)
                    else:
                        c = first + (PROMPT + 2 if stream else 0)
                        o = hh * HALF + lo
                        ins = dve.tensor_tensor(ya[:, at(i), o:o + count].rearrange("p a m -> p (a m)"),
                                                src[:, lo:lo + count], aout[:, c:c + count], ALU.mult)
                ins.then_inc(dve_half, 1)

        def proj_pool(pool, i):
            wait(pool, a_step, 3 * i)
            pool.tensor_copy(pcur[:, :], par[:, at(i), 0:PAR_CQKV].rearrange("p a k -> p (a k)"))
            pool.tensor_copy(raw[:, :, PROMPT + 3:PROMPT + 6],
                             par[:, at(i), PAR_CQKV:PAR_CA].rearrange("p a (k j) -> p (a k) j", j=3))
            pool.tensor_copy(ubuf[:, PROMPT + 2:PROMPT + 4],
                             par[:, at(i), PAR_CA:PARS].rearrange("p a k -> p (a k)")).then_inc(pars_set, 1)

        def tails_pool(pool, i, which):
            if which == 0:
                pool.wait_ge(act_half, ACT_HALVES * i + 2 * TV + 2)
                for k in range(2):
                    ins = pool.tensor_copy(
                        tails[:, at(i), 9 * k:9 * k + 9].rearrange("p a (c j) -> p (a c) j", j=3),
                        raw[:, :, PROMPT + k * (STREAM + 3):PROMPT + 3 + k * (STREAM + 3)])
                ins.then_inc(tail_kept, 1)
            else:
                pool.wait_ge(dve_half, DVE_HALVES * i + 2)
                for k in range(2):
                    c = PROMPT + k * (STREAM + 2)
                    ins = pool.tensor_copy(tails[:, at(i), 18 + 2 * k:20 + 2 * k].rearrange("p a j -> p (a j)"),
                                           ubuf[:, c:c + 2])
                ins.then_inc(tail_kept, 1)

        ya_high, yb_high, ya_low, yb_low = (sem(k) for k in ("ya_high", "yb_high", "ya_low", "yb_low"))
        p2_w, g_in = [sem("p2_w0"), sem("p2_w1")], [sem("gate_in0"), sem("gate_in1")]
        p2_high, p2_low, y_done, mixed, m_sum, m_high, m_low = (
            sem("p2_" + k) for k in ("high", "low", "done", "mixed", "msum", "mhigh", "mlow"))
        o_copied, o_back, x2_set, x2_in, oT_zero = (sem("o_" + k) for k in ("copied", "back", "x2", "x2in", "zero"))
        n_names = "turned copied logits out".split()
        nx = {k: sem("n_" + k) for k in n_names}
        p3_in, route, route_act, route_pe, zero_set, zero_out = (sem(k) for k in
                                                                 ("p3_in", "route", "route_act", "route_pe", "zero_set", "zero_out"))
        spread_rows = sem("spread_rows")
        e_w, e_wd = [sem("e_w0"), sem("e_w1")], [sem("e_wd0"), sem("e_wd1")]
        e_x = [sem("e_x0"), sem("e_x1")]
        e_high, e_low, e_xt, e_xh, e_xl, e_gu, e_silu, e_hid, e_ht, e_hh, e_hl, e_dn, e_y = (
            sem("e_" + k) for k in "high low xt xh xl gu silu hid ht hh hl dn y".split())
        e_out = [sem("e_out0"), sem("e_out1")]
        o_x, o_w, o_out = sem("o_x"), sem("o_w"), sem("o_out")
        f_x = sem("f_x")
        f_y = [sem(f"f_y{c}") for c in range(UNITS)]
        o_kept, f_sum = sem("o_kept"), sem("f_sum")
        f_out = sem("f_out")

        def frames(c):
            return slice(0, P if c < 4 else STREAM)

        def wide(c):
            return wideB if c % 2 else wideA

        def table_view(kind):
            return dec[:, :, kind, :]

        def by_head(row):
            return dtmp[:, row, :].rearrange("p (u h) -> p h u", h=HEADS)

        def x_turned_tensor(pe, c):
            pe.wait_ge(x_scaled, c + 1)
            wait(pe, x_low, c - 1)
            for k in range(KC):
                mm = pe.transpose(wide(c)[:, k * P:(k + 1) * P], xin[c][:, k * P:(k + 1) * P], ident)
            mm.then_inc(x_turned, 1)

        def betas_tensor(pe):
            pe.wait_ge(ba_w, 2)
            for hh in range(2):
                for j in range(3 * KC):
                    k, term = divmod(j, 3)
                    w = (w16h, w16h, w16l)[term][:, k, :]
                    x = (xnh, xnl, xnh)[term][:, k, hh * HALF:(hh + 1) * HALF]
                    mm = pe.matmul(wideA[0:16, 512 * hh:512 * hh + HALF], w, x, start=(j == 0), stop=(j == 3 * KC - 1))
            mm.then_inc(ba_done, 1)

        def betas_copied(dve):
            dve.wait_ge(ba_done, 1)
            for hh in range(2):
                ins = dve.tensor_copy(buf1[0:16, hh * HALF:(hh + 1) * HALF], wideA[0:16, 512 * hh:512 * hh + HALF])
            ins.then_inc(ba_out, 1)

        def betas_turned(pe):
            pe.wait_ge(ba_out, 1)
            pe.wait_ge(zeroed, 3)
            for c in range(UNITS):
                mm = pe.transpose(small[:, 16 * c:16 * c + 16], buf1[0:16, c * P:(c + 1) * P], ident[0:16, 0:16])
            mm.then_inc(ba_done, 1)

        def decays_tensor(pe):
            pe.wait_ge(const_in, 16)
            pe.wait_ge(dec_dve, 6)
            pe.matmul(small[:, 0:UNITS * HEADS], upper, dtmp[:, 7, :], start=True, stop=True)
            pe.matmul(small[:, 64:64 + UNITS * HEADS], ones, dtmp[:, 7, :], start=True, stop=True).then_inc(dec_pe, 1)

        def decays_scalar(act, part):
            row = dtmp[:, :, :]
            act.wait_ge(const_in, 16)
            if part == 1:
                decays_scalar_end(act, row)
                return
            act.wait_ge(dec_dve, 1)
            act.activation(row[:, 0, :], basb[:, :, 0:HEADS], ACT.Tanh, scale=0.5).then_inc(dec_act, 1)
            act.wait_ge(dec_dve, 3)
            act.activation(row[:, 3, :], row[:, 2, :], ACT.Exp, scale=-1.0).then_inc(dec_act, 1)
            act.wait_ge(dec_act, 2)
            act.activation(row[:, 4, :], row[:, 3, :], ACT.Ln, bias=1.0).then_inc(dec_act, 1)
            act.activation(row[:, 6, 0:HEADS], misc[:, M_ALOG:M_ALOG + HEADS], ACT.Exp).then_inc(dec_act, 1)

        def decays_scalar_end(act, row):
            act.wait_ge(dec_dve, 10)
            act.activation(table_view(KEXP), table_view(KSUM), ACT.Exp).then_inc(dec_act, 1)
            act.activation(table_view(KREST), table_view(KREST), ACT.Exp).then_inc(dec_act, 1)
            act.activation(table_view(KLAST), by_head(1), ACT.Exp).then_inc(dec_act, 1)

        def decays_vector(dve, part):
            row = dtmp[:, :, :]
            dve.wait_ge(const_in, 16)
            if part == 1:
                decays_vector_end(dve, row)
                return

            def framed(r):
                return dtmp[:, r, :].rearrange("p (u h) -> p u h", h=HEADS)

            dve.wait_ge(ba_done, 2)
            dve.tensor_copy(basb[:, :, :], small[:, 0:UNITS * 16].rearrange("p (u h) -> p u h", h=16))\
               .then_inc(dec_dve, 1)
            dve.wait_ge(dec_dve, 1)
            dve.tensor_tensor(framed(1), basb[:, :, HEADS:16],
                              misc[:, M_DT:M_DT + HEADS].unsqueeze(1).to_broadcast([P, UNITS, HEADS]), ALU.add)\
               .then_inc(dec_dve, 1)
            dve.wait_ge(dec_dve, 2)
            dve.scalar_tensor_tensor(row[:, 2, :], row[:, 1, :], -1.0, row[:, 1, :], ALU.mult, ALU.max)\
               .then_inc(dec_dve, 1)
            dve.wait_ge(dec_act, 3)
            dve.scalar_tensor_tensor(row[:, 5, :], row[:, 1, :], 0.0, row[:, 4, :], ALU.max, ALU.add)\
               .then_inc(dec_dve, 1)
            dve.wait_ge(dec_act, 4)
            dve.wait_ge(dec_dve, 4)
            dve.scalar_tensor_tensor(framed(7), framed(5), -1.0,
                                     row[:, 6, 0:HEADS].unsqueeze(1).to_broadcast([P, UNITS, HEADS]),
                                     ALU.mult, ALU.mult).then_inc(dec_dve, 1)
            dve.wait_ge(dec_dve, 5)
            dve.tensor_tensor(framed(7), framed(7),
                              misc[:, M_VALID:M_VALID + UNITS].unsqueeze(2).to_broadcast([P, UNITS, HEADS]),
                              ALU.mult).then_inc(dec_dve, 1)
            dve.tensor_scalar(table_view(KBETA), by_head(0), 0.5, 0.5, ALU.mult, ALU.add).then_inc(dec_dve, 1)

        def decays_vector_end(dve, row):
            dve.wait_ge(dec_pe, 1)
            dve.tensor_copy(table_view(KSUM), small[:, 0:UNITS * HEADS].rearrange("p (u h) -> p h u", h=HEADS))\
               .then_inc(dec_dve, 1)
            dve.tensor_copy(row[:, 1, :], small[:, 64:64 + UNITS * HEADS]).then_inc(dec_dve, 1)
            dve.wait_ge(dec_dve, 9)
            dve.tensor_tensor(table_view(KREST), by_head(1), table_view(KSUM), ALU.subtract).then_inc(dec_dve, 1)
            dve.wait_ge(dec_act, 5)
            dve.tensor_tensor(table_view(KBEXP), table_view(KBETA), table_view(KEXP), ALU.mult).then_inc(dec_dve, 1)

        banks = [[proj[0], proj[1]], [proj[2], small]]

        FILL = 2

        def fill_tensor(pe, p):
            q, part = divmod(p - FILL, 2 * PER)
            if not 0 <= q < KC:
                return
            hh, part = divmod(part, PER)
            h = 2 * q + hh
            if part == 0:
                if hh == 0:
                    pe.wait_ge(p2_low, q + 1)
                wait(pe, mixed, (h - 3) // 2 + 1)
            for j in range(8 * part, 8 * part + 8):
                kc, term = divmod(j, 3)
                if h == 0 and kc % 2 == 0 and term == 0:
                    pe.wait_ge(ya_low, kc // 2 + 1)
                w = (whi, whi, wlo)[term][q % 2]
                x = (xnh, xnl, xnh)[term]
                mm = pe.matmul(proj[h % 3][:, 0:HALF], w[:, kc, :], x[:, kc, hh * HALF:(hh + 1) * HALF],
                               start=(j == 0), stop=(j == 23))
            if part == PER - 1:
                mm.then_inc(y_done, 1)

        def fill_scalar(act, p):
            if p == 0:
                act.wait_ge(proj_done, 2 * TILES * HEADS)
                act.wait_ge(dve_half, DVE_HALVES * HEADS)
                for j in range(0, KC, 2):
                    act.activation(xnh[:, j:j + 2, 0:TOK], ya[:, j:j + 2, :], ACT.Copy).then_inc(ya_high, 1)
            q, part = divmod(p - FILL, 2 * PER)
            if part == 0 and 1 <= q < KC:
                out_split_high(act, q + 1, (q + 1) % 2)
            if p in YB_AT:
                j = YB_AT[p]
                act.wait_ge(s["yb_set"], HEADS - 1)
                act.wait_ge(tail_kept, 2 * HEADS)
                act.activation(ybh[:, j, :], yb[:, j, :], ACT.Copy).then_inc(yb_high, 1)

        def fill_vector(dve, p):
            if p == 0:
                for j in range(0, KC, 2):
                    dve.wait_ge(ya_high, j // 2 + 1)
                    dve.tensor_tensor(xnl[:, j:j + 2, 0:TOK], ya[:, j:j + 2, :], xnh[:, j:j + 2, 0:TOK].bitcast(F32),
                                      ALU.subtract).then_inc(ya_low, 1)
                dve.wait_ge(ya_low, KC // 2)
            q, part = divmod(p - FILL, 2 * PER)
            if part == 0 and 1 <= q <= KC:
                mix_a(dve, q - 1)
                if q < KC:
                    out_split_low(dve, q + 1, (q + 1) % 2)
            if p in YB_AT:
                yb_low_part(dve, YB_AT[p])

        YB_AT = {20 + 2 * j: j for j in range(HEADS - 1)}

        def yb_low_part(dve, j):
            dve.wait_ge(yb_high, j + 1)
            dve.tensor_tensor(ybl[:, j, :], yb[:, j, :], ybh[:, j, :].bitcast(F32), ALU.subtract).then_inc(yb_low, 1)

        def out_tensor(pe, q, k, xh, xl):
            pe.wait_ge(p2_low, q + 1)
            for hh in range(2):
                if isinstance(q, int) and q < KC + 2:
                    pe.wait_ge(mixed, KC)
                elif xh is mh and not (isinstance(q, int) and q < 2 * KC + 2):
                    pe.wait_ge(o_copied, q - 2 * KC - 1)
                else:
                    pe.wait_ge(mixed, q - 1)
                for j in range(3 * KC):
                    kc, term = divmod(j, 3)
                    if isinstance(q, int) and q == 2 * KC and (hh, j) == (0, 3 * KC - 3):
                        pe.wait_ge(m_low, KC)
                    w = (whi, whi, wlo)[term][k]
                    x = (xh, xl, xh)[term]
                    mm = pe.matmul(banks[k][hh][:, 0:HALF], w[:, kc, :], x[:, kc, hh * HALF:(hh + 1) * HALF],
                                   start=(j == 0), stop=(j == 3 * KC - 1))
                mm.then_inc(y_done, 1)

        def back_tensor(pe, q, k):
            pe.wait_ge(o_copied, q - 2 * KC + 1)
            if not (isinstance(q, int) and q < 2 * KC + 2):
                pe.wait_ge(x2_set, q - 2 * KC - 1)
            for u in range(UNITS):
                mm = pe.transpose(wide(k)[:, U[u]], oT[k][:, U[u]], ident)
            mm.then_inc(o_back, 1)

        def phase2_tensor(pe):
            pe.wait_ge(yb_low, HEADS)
            for k in range(2):
                out_tensor(pe, KC + k, k, ybh, ybl)
            with pe.Fori(KC // 2 + 1, KC) as j:
                for k in range(2):
                    out_tensor(pe, 2 * j + k, k, ybh, ybl)
            pe.wait_ge(m_low, KC - 1)
            first = 2 * KC
            out_tensor(pe, first, 0, mh, ml)
            out_tensor(pe, first + 1, 1, mh, ml)
            back_tensor(pe, first, 0)
            with pe.Fori(KC + 1, KC + KC // 2) as j:
                out_tensor(pe, 2 * j, 0, mh, ml)
                back_tensor(pe, 2 * j - 1, 1)
                out_tensor(pe, 2 * j + 1, 1, mh, ml)
                back_tensor(pe, 2 * j, 0)
            back_tensor(pe, 3 * KC - 1, 1)

        def out_split_high(act, q, k):
            if isinstance(q, int):
                act.wait_ge(p2_w[k], 16 * (q // 2 + 1))
            else:
                act.wait_ge(p2_w[k], 8 * (q - k) + 16)
            if isinstance(q, int) and q < 2:
                act.wait_ge(proj_done, 2 * TILES * (HEADS - 1) + 2 * (TILES - 2 + q))
            wait(act, y_done, 2 * (q - 1))
            act.activation(whi[k][:, :, :], wraw[k][:, :, :], ACT.Copy).then_inc(p2_high, 1)

        def out_split_low(dve, q, k):
            dve.wait_ge(p2_high, q + 1)
            dve.tensor_tensor(wlo[k][:, :, :], wraw[k][:, :, :], whi[k][:, :, :].bitcast(F32), ALU.subtract)\
               .then_inc(p2_low, 1)

        def mix_high(act, q, k):
            m = q - KC
            act.wait_ge(m_sum, m + 1)
            act.activation(mh[:, at(m), :].rearrange("p a m -> p (a m)"), mix[k][:, :], ACT.Copy, scale=0.5)\
               .then_inc(m_high, 1)

        def o_copy(act, q, k):
            n = q - 2 * KC
            act.wait_ge(y_done, 2 * q + 2)
            if not (isinstance(q, int) and n < 2):
                act.wait_ge(o_back, n - 1)
            for hh in range(2):
                ins = act.activation(oT[k][:, hh * HALF:(hh + 1) * HALF], banks[k][hh][:, 0:HALF], ACT.Copy)
            ins.then_inc(o_copied, 1)

        def phase2_scalar(act):
            act.wait_ge(s["yb_set"], HEADS)
            act.activation(ybh[:, HEADS - 1, :], yb[:, HEADS - 1, :], ACT.Copy).then_inc(yb_high, 1)
            act.wait_ge(s["s_out"], 32 * HEADS)
            act.wait_ge(tails_out, 16)
            out_split_high(act, KC + 1, 1)
            act.wait_ge(yb_low, HEADS)
            mix_high(act, KC, 0)
            with act.Fori(KC // 2 + 1, KC) as j:
                out_split_high(act, 2 * j, 0)
                mix_high(act, 2 * j - 1, 1)
                out_split_high(act, 2 * j + 1, 1)
                mix_high(act, 2 * j, 0)
            out_split_high(act, 2 * KC, 0)
            mix_high(act, 2 * KC - 1, 1)
            out_split_high(act, 2 * KC + 1, 1)
            act.wait_ge(oT_zero, 2)
            o_copy(act, 2 * KC, 0)
            with act.Fori(KC + 1, KC + KC // 2) as j:
                out_split_high(act, 2 * j, 0)
                o_copy(act, 2 * j - 1, 1)
                out_split_high(act, 2 * j + 1, 1)
                o_copy(act, 2 * j, 0)
            o_copy(act, 3 * KC - 1, 1)

        def mix_a(dve, q):
            dve.wait_ge(g_in[q % 2], 16 * (q // 2 + 1))
            dve.wait_ge(y_done, 2 * q + 2)
            for hh in range(2):
                h = slice(hh * HALF, (hh + 1) * HALF)
                ins = dve.scalar_tensor_tensor(ya[:, q, h], gate[q % 2][:, h], 1.0, proj[(2 * q + hh) % 3][:, 0:HALF],
                                               ALU.add, ALU.mult)
            ins.then_inc(mixed, 1)

        def mix_b(dve, q, k):
            m = q - KC
            if isinstance(q, int):
                dve.wait_ge(g_in[k], 16 * (q // 2 + 1))
                wait(dve, m_high, m - 1)
            else:
                dve.wait_ge(g_in[k], 8 * (q - k) + 16)
                dve.wait_ge(m_high, m - 1)
            dve.wait_ge(y_done, 2 * q + 2)
            for hh in range(2):
                h = slice(hh * HALF, (hh + 1) * HALF)
                ins = dve.scalar_tensor_tensor(mix[k][:, h], tg[k][:, h], 1.0, banks[k][hh][:, 0:HALF],
                                               ALU.add, ALU.mult)
            ins.then_inc(mixed, 1)
            dve.wait_ge(mixed, q + 1)
            dve.tensor_tensor(mix[k][:, :], mix[k][:, :], ya[:, at(m), :].rearrange("p a m -> p (a m)"), ALU.add)\
               .then_inc(m_sum, 1)
            dve.wait_ge(m_high, m + 1)
            dve.scalar_tensor_tensor(ml[:, at(m), :].rearrange("p a m -> p (a m)"), mix[k][:, :], 0.5,
                                     mh[:, at(m), :].bitcast(F32).rearrange("p a m -> p (a m)"),
                                     ALU.mult, ALU.subtract).then_inc(m_low, 1)

        def x2_add(dve, q, k):
            n = q - 2 * KC
            dve.wait_ge(o_back, n + 1)
            dst = x2[:, :, at(n * P, P)]
            dve.tensor_tensor(dst, dst, wide(k)[:, 0:UW].rearrange("p (u m) -> p u m", m=P), ALU.add)\
               .then_inc(x2_set, 1)

        def phase2_vector(dve):
            yb_low_part(dve, HEADS - 1)
            out_split_low(dve, KC + 1, 1)
            mix_b(dve, KC, 0)
            with dve.Fori(KC // 2 + 1, KC) as j:
                out_split_low(dve, 2 * j, 0)
                mix_b(dve, 2 * j - 1, 1)
                out_split_low(dve, 2 * j + 1, 1)
                mix_b(dve, 2 * j, 0)
            out_split_low(dve, 2 * KC, 0)
            mix_b(dve, 2 * KC - 1, 1)
            out_split_low(dve, 2 * KC + 1, 1)
            dve.wait_ge(x2_in, 32)
            dve.wait_ge(oT_zero, 2)
            with dve.Fori(KC + 1, KC + KC // 2) as j:
                out_split_low(dve, 2 * j, 0)
                x2_add(dve, 2 * j - 2, 0)
                out_split_low(dve, 2 * j + 1, 1)
                x2_add(dve, 2 * j - 1, 1)
            x2_add(dve, 3 * KC - 2, 0)
            x2_add(dve, 3 * KC - 1, 1)

        def phase3_scalar(act):
            act.wait_ge(x2_set, KC)
            for c in range(UNITS + 2):
                n = UNITS + c
                if c < UNITS:
                    act.wait_ge(x_square, n)
                    act.activation(sqs[:, :], x2[:, c, :], ACT.Square, accum_out=small_sb[:, c:c + 1])\
                       .then_inc(x_square, 1)
                    act.wait_ge(x_square, n + 1)
                    act.activation(small_sb[:, 8 + c:9 + c], small_sb[:, c:c + 1], ACT.Sqrt, scale=1.0 / D,
                                   bias=epsq[:, 1:2]).then_inc(x_root, 1)
                if c > 1:
                    act.wait_ge(nx["turned"], c - 1)
                    wait(act, nx["logits"], c - 3)
                    act.activation(tT[c % 2][:, :], wide(c)[:, :], ACT.Copy).then_inc(nx["copied"], 1)
            for part in range(2):
                weights_high(act, 0, 0, part)
            act.wait_ge(route, R_GAP)
            act.activation(r4[3][:, :, :], r4[2][:, :, :], ACT.Exp).then_inc(route_act, 1)
            act.activation(r5[:, 9, :], r5[:, 8, :], ACT.Exp).then_inc(route_act, 1)

        def phase3_tensor(pe):
            pe.wait_ge(p3_in, 32)
            n = GROUPS + EXPERTS
            for c in range(UNITS + 1):
                if c < UNITS:
                    pe.wait_ge(x_scaled, UNITS + c + 1)
                    wait(pe, nx["copied"], c - 1)
                    for k in range(KC):
                        mm = pe.transpose(wide(c)[:, k * P:(k + 1) * P], tn[:, c, k * P:(k + 1) * P], ident)
                    mm.then_inc(nx["turned"], 1)
                if c > 0:
                    pe.wait_ge(nx["copied"], c)
                    for k in range(KC):
                        mm = pe.matmul(small[:, n * (c - 1):n * c], tT[(c - 1) % 2][:, k * P:(k + 1) * P], wr[:, k, :],
                                       start=(k == 0), stop=(k == KC - 1))
                    mm.then_inc(nx["logits"], 1)
            pe.wait_ge(route, R_PAIRS)
            E = EXPERTS
            pairs = r32[0][:, :, :].rearrange("p u e -> p (u e)")
            pe.matmul(proj[0][:, 0:UNITS * E], before, pairs, start=True, stop=False)
            for j in range(1, UNITS):
                pe.matmul(proj[0][:, E * j:E * UNITS], ones, pairs[:, 0:E * (UNITS - j)], start=False,
                          stop=(j == UNITS - 1))
            mm = pe.matmul(proj[1][:, 0:UNITS * E], ones, pairs, start=True, stop=True)
            mm.then_inc(route_pe, 1)

        def phase3_vector(dve):
            dve.wait_ge(p3_in, 32)
            for c in range(UNITS):
                n = UNITS + c + 1
                dve.wait_ge(x_root, n)
                dve.reciprocal(small_sb[:, 16 + c:17 + c], small_sb[:, 8 + c:9 + c]).then_inc(x_recip, 1)
                dve.wait_ge(x_recip, n)
                dve.scalar_tensor_tensor(tn[:, c, :], x2[:, c, :], small_sb[:, 16 + c:17 + c], g2row[:, :],
                                         ALU.mult, ALU.mult).then_inc(x_scaled, 1)
            dve.wait_ge(nx["logits"], UNITS)
            chain = [0]

            def link(ins):
                chain[0] += 1
                ins.then_inc(route, 1)
                dve.wait_ge(route, chain[0])

            def over(ap, axis, shape):
                return ap.unsqueeze(axis).to_broadcast(shape)

            def first_largest(values, count, top_row, index_row, tmp, chosen):
                shape = [P, UNITS, count]
                iota = over(misc[:, M_IOTA:M_IOTA + count], 1, shape)
                link(dve.tensor_reduce(r5[:, top_row, :], values, X, ALU.max))
                link(dve.tensor_tensor(tmp, values, over(r5[:, top_row, :], 2, shape), ALU.is_equal))
                link(dve.scalar_tensor_tensor(tmp, tmp, -64.0, iota, ALU.mult, ALU.add))
                link(dve.tensor_reduce(r5[:, index_row, :], tmp, X, ALU.min))
                link(dve.scalar_tensor_tensor(chosen, iota, -64.0, over(r5[:, index_row, :], 2, shape),
                                              ALU.add, ALU.is_equal))

            n = GROUPS + EXPERTS
            link(dve.tensor_tensor(lg[:, :, :], small[:, 0:UNITS * n].rearrange("p (u n) -> p u n", n=n),
                                   over(misc[:, M_RBIAS:M_RBIAS + n], 1, [P, UNITS, n]), ALU.add))
            first_largest(lg[:, :, 0:GROUPS], GROUPS, 0, 1, r4[1][:, :, :], r4[0][:, :, :])
            link(dve.tensor_tensor(r4[0][:, :, :], r4[0][:, :, :],
                                   over(misc[:, M_VALID:M_VALID + UNITS], 2, [P, UNITS, GROUPS]), ALU.mult))
            shape4 = [P, UNITS, GROUPS, PER_GROUP]

            def grouped(t):
                return t.rearrange("p u (g e) -> p u g e", g=GROUPS)

            link(dve.tensor_tensor(grouped(r32[0][:, :, :]), grouped(lg[:, :, GROUPS:n]), over(r4[0][:, :, :], 3, shape4),
                                   ALU.mult))
            link(dve.tensor_reduce(r8[0][:, :, :], r32[0][:, :, :].rearrange("p u (g e) -> p u e g", g=GROUPS), X,
                                   ALU.add))
            first_largest(r8[0][:, :, :], PER_GROUP, 4, 5, r8[4][:, :, :], r8[1][:, :, :])
            link(dve.scalar_tensor_tensor(r8[2][:, :, :], r8[1][:, :, :], -3.0e38, r8[0][:, :, :], ALU.mult, ALU.add))
            first_largest(r8[2][:, :, :], PER_GROUP, 6, 7, r8[4][:, :, :], r8[3][:, :, :])
            for k, chosen in ((0, r8[1]), (1, r8[3])):
                link(dve.tensor_tensor(grouped(pair[:, k, :, :]), over(r4[0][:, :, :], 3, shape4),
                                       over(chosen[:, :, :], 2, shape4), ALU.mult))
            link(dve.tensor_tensor(r32[0][:, :, :], pair[:, 0, :, :], pair[:, 1, :, :], ALU.add))
            assert chain[0] == R_PAIRS, chain
            link(dve.tensor_tensor(r4[2][:, :, :], lg[:, :, 0:GROUPS], over(r5[:, 0, :], 2, [P, UNITS, GROUPS]),
                                   ALU.subtract))
            link(dve.tensor_tensor(r5[:, 8, :], r5[:, 6, :], r5[:, 4, :], ALU.subtract))
            assert chain[0] == R_GAP, chain
            dve.wait_ge(route_pe, 1)
            E = EXPERTS
            both = [P, 2, UNITS, E]
            shape = [P, UNITS, E]
            earlier = proj[0][:, 0:UNITS * E].rearrange("p (u e) -> p u e", e=E)
            total = ex[:, 0, :]
            link(dve.tensor_reduce(total, proj[1][:, 0:UNITS * E].rearrange("p (u e) -> p e u", e=E), X, ALU.add))
            link(dve.tensor_tensor_scan(ex[:, 2, :], ones[:, 0:E], total, 0.0, ALU.mult, ALU.add))
            link(dve.tensor_tensor(ex[:, 2, :], ex[:, 2, :], total, ALU.subtract))
            link(dve.tensor_tensor(r32[1][:, :, :], earlier, over(ex[:, 2, :], 1, shape), ALU.add))
            link(dve.tensor_tensor(pick[:, :, :, :], pair[:, :, :, :], over(r32[1][:, :, :], 1, both), ALU.mult))
            link(dve.tensor_reduce(r5[:, 10:12, :], pick[:, :, :, :], X, ALU.add))
            link(dve.tensor_copy(slot_row[:, :].rearrange("p (k u) -> p k u", k=2), r5[:, 10:12, :]))
            assert chain[0] == R_PLACES, chain
            link(dve.tensor_copy(table[0:1, TB_FIRST:TB_FIRST + E], ex[0:1, 2, :]))
            weights_low(dve, 0, 0, 0)
            weights_low(dve, 0, 0, 1)
            link(dve.tensor_scalar(ex[:, 1, :], total, float(BR), None, ALU.is_gt))
            for k in range(2, (TOK - 1) // BR + 1):
                link(dve.scalar_tensor_tensor(ex[:, 1, :], total, float(BR * k), ex[:, 1, :], ALU.is_gt, ALU.add))
            link(dve.tensor_tensor_scan(ex[:, 3, :], ones[:, 0:E], ex[:, 1, :], 0.0, ALU.mult, ALU.add))
            link(dve.tensor_copy(table[0:1, TB_COUNT:TB_COUNT + 1], ex[0:1, 3, E - 1:E]))
            link(dve.tensor_tensor(ex[:, 3, :], ex[:, 3, :], ex[:, 1, :], ALU.subtract))
            dve.wait_ge(route_act, 2)
            link(dve.tensor_reduce(r5[:, 2, :], r4[3][:, :, :], X, ALU.add))
            link(dve.scalar_tensor_tensor(r5[:, 3, :], r5[:, 9, :], 1.0, r5[:, 2, :], ALU.add, ALU.mult))
            link(dve.reciprocal(coef[:, 0, :], r5[:, 3, :]))
            link(dve.tensor_tensor(coef[:, 1, :], coef[:, 0, :], r5[:, 9, :], ALU.mult))
            iota_e = misc[:, M_IOTA:M_IOTA + E]
            link(dve.tensor_tensor(ex[:, 4, :], ex[:, 3, :], iota_e, ALU.subtract))
            link(dve.tensor_scalar(ex[:, 4, :], ex[:, 4, :], float(E - 1), float(BR), ALU.add, ALU.mult))
            link(dve.scalar_tensor_tensor(r32[1][:, :, :], earlier, float(BR), over(ex[:, 4, :], 1, shape),
                                          ALU.is_ge, ALU.mult))
            link(dve.tensor_tensor(r32[1][:, :, :], r32[1][:, :, :], earlier, ALU.add))
            link(dve.scalar_tensor_tensor(r32[1][:, :, :], over(iota_e, 1, shape), float(BR), r32[1][:, :, :],
                                          ALU.mult, ALU.add))
            link(dve.tensor_tensor(pick[:, :, :, :], pair[:, :, :, :], over(r32[1][:, :, :], 1, both), ALU.mult))
            link(dve.tensor_reduce(r5[:, 10:12, :], pick[:, :, :, :], X, ALU.add))
            link(dve.tensor_copy(slot_y[:, :].rearrange("p (k u) -> p k u", k=2), r5[:, 10:12, :]))
            one = [1, OVER, E]
            further = misc[0:1, M_IOTA:M_IOTA + OVER]
            link(dve.tensor_tensor(bt[0:1, 0, :, :], over(ex[0:1, 3, :], 1, one), over(further, 2, one), ALU.is_le))
            link(dve.tensor_reduce(brow[0:1, 0, :], bt[0:1, 0, :, :], X, ALU.add))
            link(dve.tensor_scalar(brow[0:1, 0, :], brow[0:1, 0, :], -1.0, None, ALU.add))
            link(dve.tensor_copy(table[0:1, TB_EXPERT:TB_EXPERT + OVER], brow[0:1, 0, :]))
            link(dve.tensor_tensor(bt[0:1, 1, :, :], over(misc[0:1, M_IOTA:M_IOTA + E], 1, one),
                                   over(brow[0:1, 0, :], 2, one), ALU.is_equal))
            link(dve.scalar_tensor_tensor(ex[0:1, 5, :], ex[0:1, 3, :], -float(BR), ex[0:1, 2, :], ALU.mult, ALU.add))
            link(dve.tensor_tensor(bt[0:1, 2, :, :], bt[0:1, 1, :, :], over(ex[0:1, 5, :], 1, one), ALU.mult))
            link(dve.tensor_reduce(brow[0:1, 1, :], bt[0:1, 2, :, :], X, ALU.add))
            link(dve.scalar_tensor_tensor(brow[0:1, 2, :], further, float(BR), brow[0:1, 1, :], ALU.mult, ALU.add))
            link(dve.tensor_scalar(brow[0:1, 2, :], brow[0:1, 2, :], float(BR), float(SLOTS), ALU.add, ALU.min))
            link(dve.tensor_copy(table[0:1, TB_ROW:TB_ROW + OVER], brow[0:1, 2, :]))
            assert chain[0] == ROUTE_STEPS, chain

        DOWN_AT = 12
        GU = 16 * DE

        def rows_turned(pe, b, k, arrived=None):
            pe.wait_ge(*(arrived or (e_x[k], 8 * (b - k) + 16)))
            wait(pe, e_xl, b)
            v = xb[k][0:BR, :].rearrange("s (p c) -> s c p", c=KC)
            for c in range(KC):
                mm = pe.transpose(wideA[:, c * P:c * P + BR], v[:, c, :], ident[0:BR, 0:BR])
            mm.then_inc(e_xt, 1)

        def gate_up(pe, b, k, between=None):
            pe.wait_ge(e_low, 2 * b + 1)
            pe.wait_ge(e_xl, b + 1)
            wait(pe, e_hid, b - 1)
            for j in range(3 * KC):
                c, term = divmod(j, 3)
                if between and j == DOWN_AT:
                    between()
                x = (xbh, xbl, xbh)[term][k][:, c, :]
                w = (ehi, ehi, elo)[term][k][:, 0:GU].rearrange("p (w c n) -> p w c n", w=2, c=KC)[:, :, c, :]
                mm = pe.matmul(proj[k][0:BR, :].rearrange("p (w n) -> p w n", w=2), x, w, start=(j == 0),
                               stop=(j == 3 * KC - 1))
            mm.then_inc(e_gu, 1)

        def hidden_turned(pe, b, k):
            pe.wait_ge(e_hid, b + 1)
            wait(pe, e_hl, b)
            v = hid[k][0:BR, :].rearrange("s (p c) -> s c p", c=2)
            for c in range(2):
                mm = pe.transpose(proj[2][:, c * BR:(c + 1) * BR], v[:, c, :], ident[0:BR, 0:BR])
            mm.then_inc(e_ht, 1)

        def down(pe, b, k):
            pe.wait_ge(e_hl, b + 1)
            pe.wait_ge(e_low, 2 * b + 2)
            wait(pe, e_y, b)
            for n in range(2):
                for j in range(6):
                    c, term = divmod(j, 3)
                    x = (hth, htl, hth)[term][k][:, c, :]
                    w = (ehi, ehi, elo)[term][k][:, GU + c * D + 512 * n:GU + c * D + 512 * (n + 1)]
                    mm = pe.matmul(wideB[0:BR, 512 * n:512 * (n + 1)], x, w, start=(j == 0), stop=(j == 5))
            mm.then_inc(e_dn, 1)

        def expert_tensor(pe, b, k, first=False, last=False):
            gate_up(pe, b, k, None if first else lambda: down(pe, b - 1, 1 - k))
            if not last:
                rows_turned(pe, b + 1, 1 - k)
            hidden_turned(pe, b, k)

        def further_blocks(engine, step):
            engine.wait_ge(route, ROUTE_STEPS)
            count = engine.value_load(table[0:1, TB_COUNT:TB_COUNT + 1], min_val=0, max_val=OVER)
            with engine.Fori(0, OVER) as j:
                with engine.If(count > j):
                    step(j)
            return count

        def phase4_tensor(pe):
            rows_turned(pe, 0, 0)
            expert_tensor(pe, 0, 0, first=True)
            expert_tensor(pe, 1, 1)
            with pe.Fori(1, EXPERTS // 2 - 1) as i:
                for k in range(2):
                    expert_tensor(pe, 2 * i + k, k)
            expert_tensor(pe, EXPERTS - 2, 0)
            expert_tensor(pe, EXPERTS - 1, 1, last=True)
            down(pe, EXPERTS - 1, 1)

            def further(j):
                b = j + EXPERTS
                rows_turned(pe, b, 0, arrived=(o_x, 16 * j + 16))
                gate_up(pe, b, 0)
                hidden_turned(pe, b, 0)
                down(pe, b, 0)

            further_blocks(pe, further)

        def weights_high(act, b, k, part, arrived=None):
            if part == 0:
                act.wait_ge(*(arrived or (e_w[k], 16 * (b - k) + 32)))
                wait(act, e_gu, b - 1)
                act.activation(ehi[k][:, 0:GU], eraw[k][:, 0:GU], ACT.Copy).then_inc(e_high, 1)
            else:
                if not arrived:
                    act.wait_ge(e_wd[k], 8 * (b - k) + 16)
                wait(act, e_dn, b - 1)
                act.activation(ehi[k][:, GU:], eraw[k][:, GU:], ACT.Copy).then_inc(e_high, 1)

        def weights_low(dve, b, k, part):
            dve.wait_ge(e_high, 2 * b + 1 + part)
            cols = slice(0, GU) if part == 0 else slice(GU, 24 * DE)
            dve.tensor_tensor(elo[k][:, cols], eraw[k][:, cols], ehi[k][:, cols].bitcast(F32), ALU.subtract)\
               .then_inc(e_low, 1)

        turned_rows = wideA[:, :].rearrange("p (c m) -> p c m", c=KC)[:, :, 0:BR]
        turned_hidden = proj[2][:, 0:2 * BR].rearrange("p (c m) -> p c m", c=2)

        def rows_high(act, b, k):
            act.wait_ge(e_xt, b + 1)
            act.activation(xbh[k][:, :, :], turned_rows, ACT.Copy).then_inc(e_xh, 1)

        def rows_low(dve, b, k):
            dve.wait_ge(e_xh, b + 1)
            dve.tensor_tensor(xbl[k][:, :, :], turned_rows, xbh[k][:, :, :].bitcast(F32), ALU.subtract)\
               .then_inc(e_xl, 1)

        def silu_gate(act, b, k):
            act.wait_ge(e_gu, b + 1)
            wait(act, e_hid, b - 1)
            act.activation(hgate[k][0:BR, :], proj[k][0:BR, 0:DE], ACT.Silu).then_inc(e_silu, 1)

        def hidden_high(act, b, k):
            act.wait_ge(e_ht, b + 1)
            act.activation(hth[k][:, :, :], turned_hidden, ACT.Copy).then_inc(e_hh, 1)

        def y_copy(act, b, k, stored=None):
            act.wait_ge(e_dn, b + 1)
            if stored:
                wait(act, *stored)
            elif not (isinstance(b, int) and b < 2):
                act.wait_ge(e_out[k], 8 * (b - k))
            act.activation(yout[k][0:BR, :], wideB[0:BR, :], ACT.Copy).then_inc(e_y, 1)

        def expert_scalar(act, b, k, first=False, last=False):
            if not last:
                weights_high(act, b + 1, 1 - k, 0)
            if not first:
                y_copy(act, b - 1, 1 - k)
            if not last:
                weights_high(act, b + 1, 1 - k, 1)
            silu_gate(act, b, k)
            if not last:
                rows_high(act, b + 1, 1 - k)
            hidden_high(act, b, k)

        def phase4_scalar(act):
            rows_high(act, 0, 0)
            expert_scalar(act, 0, 0, first=True)
            expert_scalar(act, 1, 1)
            with act.Fori(1, EXPERTS // 2 - 1) as i:
                for k in range(2):
                    expert_scalar(act, 2 * i + k, k)
            expert_scalar(act, EXPERTS - 2, 0)
            expert_scalar(act, EXPERTS - 1, 1, last=True)
            y_copy(act, EXPERTS - 1, 1)
            act.wait_ge(e_out[0], 8 * EXPERTS)

            def further(j):
                b = j + EXPERTS
                weights_high(act, b, 0, 0, arrived=(o_w, 48 * j + 48))
                weights_high(act, b, 0, 1, arrived=(o_w, 48 * j + 48))
                rows_high(act, b, 0)
                silu_gate(act, b, 0)
                hidden_high(act, b, 0)
                y_copy(act, b, 0, stored=(o_out, 16 * j))

            further_blocks(act, further)

        def hidden_set(dve, b, k):
            dve.wait_ge(e_silu, b + 1)
            wait(dve, e_ht, b - 1)
            dve.tensor_tensor(hid[k][0:BR, :], proj[k][0:BR, DE:2 * DE], hgate[k][0:BR, :], ALU.mult)\
               .then_inc(e_hid, 1)

        def hidden_low(dve, b, k):
            dve.wait_ge(e_hh, b + 1)
            dve.tensor_tensor(htl[k][:, :, :], turned_hidden, hth[k][:, :, :].bitcast(F32), ALU.subtract)\
               .then_inc(e_hl, 1)

        def expert_vector(dve, b, k, last=False):
            if not last:
                weights_low(dve, b + 1, 1 - k, 0)
            hidden_set(dve, b, k)
            if not last:
                rows_low(dve, b + 1, 1 - k)
                weights_low(dve, b + 1, 1 - k, 1)
            hidden_low(dve, b, k)

        def phase4_vector(dve):
            rows_low(dve, 0, 0)
            expert_vector(dve, 0, 0)
            expert_vector(dve, 1, 1)
            with dve.Fori(1, EXPERTS // 2 - 1) as i:
                for k in range(2):
                    expert_vector(dve, 2 * i + k, k)
            expert_vector(dve, EXPERTS - 2, 0)
            expert_vector(dve, EXPERTS - 1, 1, last=True)

            def further(j):
                b = j + EXPERTS
                weights_low(dve, b, 0, 0)
                weights_low(dve, b, 0, 1)
                rows_low(dve, b, 0)
                hidden_set(dve, b, 0)
                hidden_low(dve, b, 0)

            count = further_blocks(dve, further)
            dve.wait_ge(o_out, 16 * count)
            dve.tensor_copy(small_sb[0:1, 59:60], epsq[0:1, 1:2]).then_inc(o_kept, 1)

        def phase5_scalar(act):
            for c in range(UNITS):
                r = frames(c)
                act.wait_ge(f_sum, 2 * c + 2)
                act.wait_ge(x_square, 2 * UNITS + c)
                act.activation(fsq[r, :], fx[c][r, :], ACT.Square, accum_out=small_sb[r, c:c + 1]).then_inc(x_square, 1)
                act.wait_ge(x_square, 2 * UNITS + c + 1)
                act.activation(small_sb[r, 8 + c:9 + c], small_sb[r, c:c + 1], ACT.Sqrt, scale=1.0 / D,
                               bias=epsq[r, 1:2]).then_inc(x_root, 1)
                if c > 0:
                    y_final(act, c - 1)
            y_final(act, UNITS - 1)

        def y_final(act, c):
            act.wait_ge(x_scaled, 2 * UNITS + c + 1)
            act.dma_start(O["y"][c * P:c * P + frames(c).stop, :], fx[c][frames(c), :]).then_inc(f_out, 16)

        def normed(dve, c):
            r = frames(c)
            dve.wait_ge(x_root, 2 * UNITS + c + 1)
            dve.reciprocal(small_sb[r, 16 + c:17 + c], small_sb[r, 8 + c:9 + c]).then_inc(x_recip, 1)
            dve.wait_ge(x_recip, 2 * UNITS + c + 1)
            dve.scalar_tensor_tensor(fx[c][r, :], fx[c][r, :], small_sb[r, 16 + c:17 + c], fgrow[r, :], ALU.mult,
                                     ALU.mult).then_inc(x_scaled, 1)

        def phase5_vector(dve):
            dve.wait_ge(f_x, 16 * (UNITS + 1))
            for c in range(UNITS):
                r = frames(c)
                for k in range(2):
                    dve.wait_ge(f_y[c], 32)
                    dve.scalar_tensor_tensor(fx[c][r, :], fy[k][c][r, :], coef[r, k, c:c + 1], fx[c][r, :],
                                             ALU.mult, ALU.add).then_inc(f_sum, 1)
                    dve.wait_ge(f_sum, 2 * c + k + 1)
                if c > 0:
                    normed(dve, c - 1)
            normed(dve, UNITS - 1)

        GDN_FIRST_ACT, GDN_FIRST_DVE = (), range(POS)

        def both_scalar(act, p, i, g, last=False):
            if p in GDN_FIRST_ACT:
                gdn_scalar(act, p, g)
            proj_scalar(act, p, i, last)
            if p not in GDN_FIRST_ACT:
                gdn_scalar(act, p, g)

        def both_vector(dve, p, i, g, last=False):
            if p in GDN_FIRST_DVE:
                gdn_vector(dve, p, g)
            proj_vector(dve, p, i, last)
            if p not in GDN_FIRST_DVE:
                gdn_vector(dve, p, g)

        block = top.enter_context(nc.Block())

        @block.sync
        def _(sp):
            for c in range(UNITS):
                rows = frames(c).stop
                sp.dma_start(xin[c][0:rows, :], A["x"][c * P:c * P + rows, :]).then_inc(x_in[c], 16)
                if c == 0:
                    sp.dma_start(ident, A["consts"][:, C_ID:C_ID + P]).then_inc(ident_in, 16)
                    sp.dma_start(g1row[:, :], A["g1row"]).then_inc(g1_in, 16)
                if c == 2:
                    sp.dma_start(wraw[0][:, :, :], A["w_in"][0]).then_inc(w_in[0], 16)
            for k in (1, 2):
                sp.dma_start(wraw[k][:, :, :], A["w_in"][k]).then_inc(w_in[k], 16)
            sp.dma_start(w16[:, :, :], A["w16"]).then_inc(par_in, 16)
            sp.dma_start(const[:, P:CONSTS], A["consts"][:, P:CONSTS]).then_inc(const_in, 16)
            sp.dma_start(onorm[:, :], A["onorm"]).then_inc(par_in, 16)
            sp.dma_start(par[:, :, :], A["params"]).then_inc(par_in, 16)

            def tile_load(i, t):
                sp.wait_ge(w_low, TILES * i + t - 2)
                k = i * TILES + t
                sp.dma_start(wraw[t % 3][:, :, :], A["w_in"][at(k)].rearrange("a p k m -> (a p) k m"))\
                  .then_inc(w_in[t % 3], 16)

            for t in range(3, TILES):
                tile_load(0, t)
            sp.wait_ge(zero_set, 1)
            sp.dma_start(scr_rows[SLOTS:ROWS, :], zero[0:BR, :]).then_inc(zero_out, 16)
            sp.dma_start(scr_y[EXPERTS * BR:BLOCKS * BR, :].rearrange("(j p) d -> p j d", p=BR),
                         zero[0:BR, :].unsqueeze(1).to_broadcast([BR, OVER, D])).then_inc(zero_out, 16)
            with sp.Fori(1, HEADS) as i:
                for t in range(TILES):
                    tile_load(i, t)
            def gate_up_load(e, k, arrived):
                v = eraw[k][:, 0:16 * DE].rearrange("p (w n) -> p w n", w=2)
                for j, w in enumerate(("w_gate", "w_up")):
                    sp.dma_start(v[:, j, :], A[w][at(e), :, :].rearrange("a (p c) n -> (a p) (c n)", p=P))\
                      .then_inc(arrived, 16)

            def down_load(e, k, arrived):
                sp.dma_start(eraw[k][:, 16 * DE:], A["w_down"][at(e), :, :].rearrange("a (p c) n -> (a p) (c n)", p=P))\
                  .then_inc(arrived, 16)

            def out_load(q, k):
                wait(sp, p2_low, q - 1)
                sp.dma_start(wraw[k][:, :, :], A["w_out"][at(q)].rearrange("a p k m -> (a p) k m"))\
                  .then_inc(p2_w[k], 16)

            def gate_load(q, which, k, place):
                wait(sp, mixed, q - 1)
                m = q - KC * which
                sp.dma_start(place[k][:, :], scr_gate[at(m), which, :, :].rearrange("a p m -> (a p) m"))\
                  .then_inc(g_in[k], 16)

            for k in range(2):
                sp.wait_ge(w_low, TILES * HEADS - 2 + k)
                out_load(k, k)
            sp.wait_ge(gate_out, 32 * HEADS)
            for k in range(2):
                gate_load(k, 0, k, gate)
            with sp.Fori(1, KC // 2) as j:
                for k in range(2):
                    out_load(2 * j + k, k)
                    gate_load(2 * j + k, 0, k, gate)
            for k in range(2):
                out_load(KC + k, k)
            sp.wait_ge(s["yb_set"], HEADS)
            for k in range(2):
                gate_load(KC + k, 1, k, tg)
            with sp.Fori(KC // 2 + 1, KC) as j:
                for k in range(2):
                    out_load(2 * j + k, k)
                    gate_load(2 * j + k, 1, k, tg)
            for k in range(2):
                out_load(2 * KC + k, k)
            sp.wait_ge(y_done, 32)
            sp.wait_ge(mixed, 16)
            sp.dma_start(x2[:, 0:4, :], A["x"][0:PROMPT, :].rearrange("(c p) d -> p c d", p=P)).then_inc(x2_in, 16)
            sp.dma_start(x2[0:STREAM, 4, :], A["x"][PROMPT:TOK, :]).then_inc(x2_in, 16)
            sp.wait_ge(m_low, KC)
            with sp.Fori(KC + 1, KC + KC // 2) as j:
                for k in range(2):
                    out_load(2 * j + k, k)
            sp.dma_start(g2row[:, :], A["g2row"]).then_inc(p3_in, 16)
            sp.dma_start(wr[:, :, :], A["w_router"]).then_inc(p3_in, 16)
            for k in range(2):
                gate_up_load(k, k, e_w[k])
                down_load(k, k, e_wd[k])
            sp.wait_ge(x2_set, 8)
            sp.dma_start(scr_x2.rearrange("(c p) d -> p c d", p=P), x2[:, :, :]).then_inc(nx["out"], 16)

            def rows_load(b, k):
                r = sp.value_load(table[0:1, at(b)], min_val=0, max_val=SLOTS)
                sp.dma_start(xb[k][0:BR, :], scr_rows[at(r, BR), :]).then_inc(e_x[k], 16)

            def y_store(b, k):
                sp.wait_ge(e_y, b + 1)
                sp.dma_start(scr_y[at(b * BR, BR), :], yout[k][0:BR, :]).then_inc(e_out[k], 16)

            sp.wait_ge(route, R_PLACES + 1)
            sp.wait_ge(spread_rows, 16 * 2 * UNITS)
            sp.wait_ge(nx["out"], 16)
            for k in range(2):
                rows_load(k, k)

            def next_load(b, k):
                sp.wait_ge(e_low, 2 * (b - 2) + 1)
                gate_up_load(b, k, e_w[k])
                sp.wait_ge(e_xt, b - 1)
                rows_load(b, k)
                sp.wait_ge(e_low, 2 * (b - 1))
                down_load(b, k, e_wd[k])

            for k in range(2):
                next_load(2 + k, k)
            with sp.Fori(2, EXPERTS // 2) as i:
                for k in range(2):
                    next_load(2 * i + k, k)
                    y_store(2 * i + k - 4, k)
            for b in range(EXPERTS - 4, EXPERTS - 1):
                y_store(b, b % 2)
            sp.wait_ge(e_low, 2 * EXPERTS)
            for c in range(UNITS):
                rows = frames(c).stop
                sp.dma_start(fx[c][0:rows, :], scr_x2[c * P:c * P + rows, :]).then_inc(f_x, 16)
            sp.dma_start(fgrow[:, :], A["final_row"]).then_inc(f_x, 16)
            y_store(EXPERTS - 1, 1)

            def further(j):
                e = sp.value_load(table[0:1, at(j + TB_EXPERT)], min_val=0, max_val=EXPERTS - 1)
                r = sp.value_load(table[0:1, at(j + TB_ROW)], min_val=0, max_val=SLOTS)
                sp.wait_ge(e_y, j + EXPERTS)
                sp.dma_start(xb[0][0:BR, :], scr_rows[at(r, BR), :]).then_inc(o_x, 16)
                gate_up_load(e, 0, o_w)
                down_load(e, 0, o_w)
                sp.wait_ge(e_y, j + (EXPERTS + 1))
                sp.dma_start(scr_y[at((j + EXPERTS) * BR, BR), :], yout[0][0:BR, :]).then_inc(o_out, 16)

            further_blocks(sp, further)
            sp.wait_ge(f_out, 16 * UNITS)
            sp.wait_ge(s["s_out"], 32 * HEADS)
            sp.wait_ge(tails_out, 16)

        @block.gpsimd
        def _(pool):
            pool.memset(epsq[:, 0:1], EPS * P)
            pool.memset(epsq[:, 1:2], EPS).then_inc(zeroed, 1)
            pool.wait_ge(zeroed, 1)
            pool.memset(xin[4][STREAM:P, :], 0.0).then_inc(zeroed, 1)
            pool.wait_ge(zeroed, 2)
            pool.memset(zero[:, :], 0.0).then_inc(zero_set, 1)
            pool.wait_ge(zero_set, 1)
            pool.wait_ge(x_scaled, UNITS)
            pool.memset(raw[:, :, 0:3], 0.0)
            pool.memset(ubuf[:, 0:2], 0.0)
            pool.memset(buf1[0:16, TOK:UW], 0.0)
            pool.memset(sil[:, :, TOK:UW], 0.0).then_inc(zeroed, 1)
            pool.wait_ge(par_in, 16 * 3)
            proj_pool(pool, 0)
            tails_pool(pool, 0, 0)
            tails_pool(pool, 0, 1)
            pool.wait_ge(dec_dve, DEC_STEPS)
            pool.wait_ge(dec_act, DEC_ACTS)
            with pool.Fori(1, HEADS) as i:
                proj_pool(pool, i)
                gdn_pool(pool, i - 1)
                tails_pool(pool, i, 0)
                tails_pool(pool, i, 1)
            gdn_pool(pool, HEADS - 1)
            pool.wait_ge(tail_kept, 2 * HEADS)
            pool.dma_start(O["tails"], tails[:, :, :]).then_inc(tails_out, 16)
            pool.wait_ge(s["s_out"], 32 * HEADS)
            pool.wait_ge(tails_out, 16)
            pool.wait_ge(m_low, KC)
            pool.memset(oT[0][:, TOK:UW], 0.0)
            pool.memset(oT[1][:, TOK:UW], 0.0).then_inc(oT_zero, 1)
            pool.wait_ge(oT_zero, 1)
            pool.memset(x2[STREAM:P, 4, :], 0.0).then_inc(oT_zero, 1)
            pool.wait_ge(route, R_PLACES)
            pool.wait_ge(x_scaled, 2 * UNITS)
            for c in range(UNITS):
                rows = frames(c).stop
                for k in range(2):
                    pool.indirect_dma_start(
                        scr_rows[0:SLOTS, :],
                        bass.IndirectOffsetOnAxis(slot_row[0:rows, k * UNITS + c:k * UNITS + c + 1], axis=0),
                        tn[0:rows, c, :], None).then_inc(spread_rows, 16)
            pool.wait_ge(spread_rows, 16 * 2 * UNITS)

            pool.wait_ge(route, ROUTE_STEPS)
            pool.wait_ge(e_out[0], 8 * EXPERTS)
            pool.wait_ge(e_out[1], 8 * EXPERTS)
            pool.wait_ge(o_kept, 1)
            for c in range(UNITS):
                rows = frames(c).stop
                for k in range(2):
                    pool.indirect_dma_start(
                        fy[k][c][0:rows, :], None, scr_y[:, :],
                        bass.IndirectOffsetOnAxis(slot_y[0:rows, k * UNITS + c:k * UNITS + c + 1], axis=0))\
                        .then_inc(f_y[c], 16)

        @block.scalar
        def _(act):
            act.wait_ge(zeroed, 1)
            for c in range(UNITS + 1):
                if c < UNITS:
                    act.wait_ge(x_in[c], 16)
                    if c == 4:
                        act.wait_ge(zeroed, 2)
                    wait(act, x_square, c)
                    act.activation(sqx[:, :], xin[c][:, :], ACT.Square, accum_out=small_sb[:, c:c + 1])\
                       .then_inc(x_square, 1)
                    act.wait_ge(x_square, c + 1)
                    act.activation(small_sb[:, 8 + c:9 + c], small_sb[:, c:c + 1], ACT.Sqrt, scale=1.0 / D,
                                   bias=epsq[:, 1:2]).then_inc(x_root, 1)
                if c > 0:
                    act.wait_ge(x_turned, c)
                    act.activation(xnh[:, :, (c - 1) * P:c * P], wide(c - 1)[:, :].rearrange("p (k m) -> p k m", k=KC),
                                   ACT.Copy).then_inc(x_high, 1)
                if c == 3:
                    split_high(act, 0, 0)
            split_high(act, 0, 1)
            act.wait_ge(par_in, 16 * 3)
            act.activation(w16h[:, :, :], w16[:, :, :], ACT.Copy).then_inc(ba_w, 1)
            act.wait_ge(zeroed, 3)
            act.wait_ge(ba_w, 2)
            for p in range(POS):
                proj_scalar(act, p, 0)
                if DECAY_AT.get(p) is not None:
                    decays_scalar(act, DECAY_AT[p])
            act.wait_ge(zero_out, 32)
            with act.Fori(1, HEADS - 1) as i:
                for p in range(POS):
                    both_scalar(act, p, i, i - 1)
            for p in range(POS):
                both_scalar(act, p, HEADS - 1, HEADS - 2, last=True)
            for p in range(POS):
                gdn_scalar(act, p, HEADS - 1)
                fill_scalar(act, p)
            phase2_scalar(act)
            phase3_scalar(act)
            phase4_scalar(act)
            phase5_scalar(act)

        @block.vector
        def _(dve):
            for c in range(UNITS + 1):
                if c < UNITS:
                    dve.wait_ge(x_root, c + 1)
                    dve.reciprocal(small_sb[:, 16 + c:17 + c], small_sb[:, 8 + c:9 + c]).then_inc(x_recip, 1)
                    dve.wait_ge(x_recip, c + 1)
                    if c == 0:
                        dve.wait_ge(g1_in, 16)
                    dve.scalar_tensor_tensor(xin[c][:, :], xin[c][:, :], small_sb[:, 16 + c:17 + c], g1row[:, :],
                                             ALU.mult, ALU.mult).then_inc(x_scaled, 1)
                if c > 0:
                    dve.wait_ge(x_high, c)
                    u = slice((c - 1) * P, c * P)
                    dve.tensor_tensor(xnl[:, :, u], wide(c - 1)[:, :].rearrange("p (k m) -> p k m", k=KC),
                                      xnh[:, :, u].bitcast(F32), ALU.subtract).then_inc(x_low, 1)
                if c == 3:
                    split_low(dve, 0, 0)
            split_low(dve, 0, 1)
            dve.wait_ge(ba_w, 1)
            dve.tensor_tensor(w16l[:, :, :], w16[:, :, :], w16h[:, :, :].bitcast(F32), ALU.subtract).then_inc(ba_w, 1)
            dve.wait_ge(zeroed, 3)
            for p in range(POS):
                proj_vector(dve, p, 0)
                if p in DECAY_AT:
                    if DECAY_AT[p] is None:
                        betas_copied(dve)
                    else:
                        decays_vector(dve, DECAY_AT[p])
            with dve.Fori(1, HEADS - 1) as i:
                for p in range(POS):
                    both_vector(dve, p, i, i - 1)
            for p in range(POS):
                both_vector(dve, p, HEADS - 1, HEADS - 2, last=True)
            for p in range(POS):
                gdn_vector(dve, p, HEADS - 1)
                fill_vector(dve, p)
            phase2_vector(dve)
            phase3_vector(dve)
            phase4_vector(dve)
            phase5_vector(dve)

        @block.tensor
        def _(pe):
            pe.wait_ge(ident_in, 16)
            for c in range(3):
                x_turned_tensor(pe, c)
            for p in range(POS):
                proj_tensor(pe, p, 0)
                if p < UNITS - 3:
                    x_turned_tensor(pe, 3 + p)
                if p == BETAS_AT:
                    betas_tensor(pe)
                if p == TURNED_AT:
                    betas_turned(pe)
                if p == SUMS_AT:
                    decays_tensor(pe)
            with pe.Fori(1, HEADS) as i:
                for p in range(POS):
                    proj_tensor(pe, p, i)
                    gdn_tensor(pe, p, i - 1)
            for p in range(POS):
                gdn_tensor(pe, p, HEADS - 1)
                fill_tensor(pe, p)
            phase2_tensor(pe)
            phase3_tensor(pe)
            phase4_tensor(pe)


def constants():
    i, j = np.arange(P)[:, None], np.arange(P)[None, :]
    parts = [i == j, i <= j, i >= j, np.ones((P, P)), i < j]
    for k in range(LEVELS + 1):
        b = 2 ** k
        cut = (i // (2 * b) == j // (2 * b)) & ((i // b) % 2 == 1) & ((j // b) % 2 == 0)
        parts.append(-cut.astype(np.float32))
    valid = np.ones((P, UNITS))
    valid[STREAM:, UNITS - 1] = 0
    return np.concatenate([np.asarray(p, np.float32) for p in parts], axis=1), valid.astype(np.float32)


def rows128(a):
    a = np.asarray(a)
    return np.moveaxis(a.reshape(a.shape[:-1] + (-1, P)), -1, 0)


def tiles_of(w):
    w = np.asarray(w)
    return w.reshape(KC, P, -1, P).transpose(2, 1, 0, 3)


def kernel(x_prompt, x_sample, cache_conv_a, cache_conv_qkv, state_gdn, norm1_g, w_in, conv_a_w, w_out_a,
           conv_qkv_w, a_log, dt_bias, onorm_g, w_out_b, w_o, norm2_g, w_router_group, b_router_group,
           w_router_expert, b_router_expert, w_gate, w_up, w_down, final_g):
    import concourse.bacc as bacc
    from concourse.bass_utils import run_bass_kernel_spmd

    table, valid = constants()

    def spread(row):
        return np.broadcast_to(np.asarray(row).reshape(1, -1), (P, np.asarray(row).size))

    iota = spread(np.arange(40, dtype=np.float32))
    consts = np.concatenate([table, valid, spread(a_log[0]), spread(dt_bias[0]),
                             spread(b_router_group[0]), spread(b_router_expert[0]), iota], axis=1)
    w_in = np.asarray(w_in)[0]
    qkv = 3 * D
    z = 6 * D
    ba = 7 * D
    gates = 7 * D + 2 * HEADS
    starts = {TQ: qkv, TK: qkv + D, TV: qkv + 2 * D, TZ: z, TGA: gates, TGB: gates + D, TH: 0, TC: 2 * D, TB: D}
    by_kind = np.stack([tiles_of(w_in[:, starts[t]:starts[t] + D]) for t in range(TILES)], axis=1)
    params = np.concatenate([
        rows128(conv_qkv_w[0].reshape(4, 3, D)).transpose(0, 3, 2, 1).reshape(P, HEADS, 12),
        rows128(conv_a_w[0]).transpose(0, 2, 1),
        rows128(np.asarray(cache_conv_qkv)[0, 0].reshape(3, 3, D)).transpose(0, 3, 2, 1).reshape(P, HEADS, 9),
        rows128(np.asarray(cache_conv_a)[0, 0]).transpose(0, 2, 1)], axis=2)
    arrays = {
        "x": np.concatenate([np.asarray(x_prompt)[0], np.asarray(x_sample)[0]], axis=0),
        "consts": consts,
        "onorm": rows128(onorm_g[0]),
        "g1row": spread(norm1_g[0]),
        "params": params,
        "w16": w_in[:, ba:gates].reshape(KC, P, 16).transpose(1, 0, 2),
        "w_in": by_kind.reshape(HEADS * TILES, P, KC, P),
        "w_out": np.concatenate([tiles_of(w_out_a[0]), tiles_of(w_out_b[0]), tiles_of(w_o[0])], axis=0),
        "state": np.asarray(state_gdn)[0, 0],
        "g2row": spread(norm2_g[0]),
        "final_row": spread(final_g),
        "w_router": np.concatenate([np.asarray(w_router_group)[0], np.asarray(w_router_expert)[0]], axis=1)
        .reshape(KC, P, GROUPS + EXPERTS).transpose(1, 0, 2),
        "w_gate": np.asarray(w_gate)[0], "w_up": np.asarray(w_up)[0], "w_down": np.asarray(w_down)[0],
    }
    outs = {"y": (TOK, D), "tails": (P, HEADS, 22), "gdn_prompt": (HEADS, P, P), "gdn_sample": (HEADS, P, P)}
    nc = bacc.Bacc("TRN2", target_bir_lowering=False, num_devices=1)
    feeds, A, O = {}, {}, {}
    for name, a in arrays.items():
        feeds["in_" + name] = a = np.ascontiguousarray(a)
        A[name] = nc.dram_tensor("in_" + name, a.shape, mybir.dt.from_np(a.dtype), kind="ExternalInput").ap()
    for name, shape in outs.items():
        O[name] = nc.dram_tensor("out_" + name, shape, F32, kind="ExternalOutput").ap()
    encoder_layer(nc, A, O)
    r = run_bass_kernel_spmd(nc, [feeds], core_ids=[0]).results[0]
    y, tails = r["out_y"], r["out_tails"]

    def last_rows(columns, kinds, count):
        t = tails[:, :, columns].reshape(P, HEADS, kinds, count).transpose(3, 2, 1, 0)
        return np.ascontiguousarray(t.reshape(1, 1, count, kinds * HEADS * P))

    return (y[None, :PROMPT], y[None, PROMPT:], last_rows(slice(18, 20), 1, 2), last_rows(slice(0, 9), 3, 3),
            r["out_gdn_prompt"][None, None], last_rows(slice(20, 22), 1, 2), last_rows(slice(9, 18), 3, 3),
            r["out_gdn_sample"][None, None])
```
